# Optimizing a Trainium2 kernel written in Bass

```python
import jax, jax.numpy as jnp
from jax import lax
import numpy as np

D_MODEL = 2048
BATCH = 1
SEQ = 512
DEPTH = 2
DEC_BATCH = 8
DEC_SEQ = 1
PAST_LEN = 512
PAGE_SIZE = 128

POOL_WINDOWS = (2, 4, 8, 16)
POOL_W = D_MODEL // 2
POOL_GROUP_W = POOL_W // len(POOL_WINDOWS)
POOL_STATE = max(POOL_WINDOWS) - 1
M_HEADS = 4
M_W = D_MODEL // 2
M_HEAD_DIM = M_W // M_HEADS
M_CHUNK = 64
N_HEADS = 16
HEAD_DIM = D_MODEL // N_HEADS
N_KV = 4
Q_PER_KV = N_HEADS // N_KV
NSA_W = N_HEADS * HEAD_DIM
KV_W = 2 * N_KV * HEAD_DIM
CMP_BLOCK = 32
SEL_BLOCK = 64
SEL_TOPK = 16
WINDOW = 512
ATT_Q_BLOCK = 128
SEL_Q_BLOCK = 64
ROPE_THETA = 10000.0
ATT_SCALE = HEAD_DIM ** -0.5
IN0 = 2 * POOL_W + 5 * M_W + 2 * M_HEADS
IN1 = 2 * NSA_W + 3 * KV_W + 3 * N_HEADS
EPS = 1e-6

kernel_name = 'hybrid_pool_mlstm_nsa_step'

def rmsnorm(x, g):
    xf = x.astype(jnp.float32)
    r = lax.rsqrt(jnp.mean(xf * xf, axis=-1, keepdims=True) + EPS)
    return (xf * r).astype(x.dtype) * g

def split_cols(a, widths):
    outs, start = [], 0
    for w in widths:
        outs.append(a[..., start:start + w])
        start += w
    return outs

def rope(x, pos):
    half = x.shape[-1] // 2
    inv = ROPE_THETA ** (-jnp.arange(half, dtype=jnp.float32) / half)
    ang = pos.astype(jnp.float32)[:, None] * inv[None, :]
    cos = jnp.cos(ang)[None, :, None, :]
    sin = jnp.sin(ang)[None, :, None, :]
    xf = x.astype(jnp.float32)
    x1, x2 = xf[..., :half], xf[..., half:]
    return jnp.concatenate([x1 * cos - x2 * sin, x2 * cos + x1 * sin], axis=-1).astype(x.dtype)

def masked_softmax(s, mask):
    s = jnp.where(mask, s.astype(jnp.float32), -jnp.inf)
    m = jnp.max(s, axis=-1, keepdims=True)
    m = jnp.where(jnp.isfinite(m), m, 0.0)
    p = jnp.exp(s - m)
    return p / jnp.maximum(jnp.sum(p, axis=-1, keepdims=True), 1e-30)

def pool_mix(buf, n_new, w_pool, pool_scale):
    B, R, _ = buf.shape
    bf = buf.astype(jnp.float32)
    csz = jnp.concatenate([jnp.zeros((B, 1, POOL_W), jnp.float32), jnp.cumsum(bf, axis=1)], axis=1)
    outs = []
    for g, w in enumerate(POOL_WINDOWS):
        sl = slice(g * POOL_GROUP_W, (g + 1) * POOL_GROUP_W)
        c = csz[:, :, sl]
        hi = c[:, 1:]
        lo = jnp.concatenate([jnp.zeros((B, w - 1, POOL_GROUP_W), jnp.float32), c], axis=1)[:, :R]
        cnt = jnp.minimum(jnp.arange(1, R + 1), w).astype(jnp.float32)[None, :, None]
        pooled = ((hi - lo) / cnt - bf[:, :, sl])[:, R - n_new:]
        outs.append(jnp.einsum('btc,cd->btd', pooled, w_pool[g].astype(jnp.float32)))
    y = jnp.concatenate(outs, axis=-1) * pool_scale.astype(jnp.float32)
    return y.astype(buf.dtype)

def mlstm_chunk(state, inp):
    c, n, m = state
    q, k, v, ig, lf = inp
    L = q.shape[1]
    b = jnp.cumsum(lf, axis=1)
    inter = b + m[:, None, :]
    dmat = b[:, :, None, :] - b[:, None, :, :] + ig[:, None, :, :]
    causal = jnp.tril(jnp.ones((L, L), dtype=bool))[None, :, :, None]
    dmat = jnp.where(causal, dmat, -jnp.inf)
    m_t = jnp.maximum(inter, jnp.max(dmat, axis=2))
    dw = jnp.exp(dmat - m_t[:, :, None, :])
    iw = jnp.exp(inter - m_t)
    qk = jnp.einsum('bthd,bshd->btsh', q, k) * dw
    num = iw[..., None] * jnp.einsum('bthd,bhde->bthe', q, c) + jnp.einsum('btsh,bshe->bthe', qk, v)
    den = iw * jnp.einsum('bthd,bhd->bth', q, n) + jnp.sum(qk, axis=2)
    h = num / jnp.maximum(jnp.abs(den), jnp.exp(-m_t))[..., None]
    m_new = m_t[:, -1]
    ws = dw[:, -1]
    dec = iw[:, -1]
    c_new = dec[..., None, None] * c + jnp.einsum('bsh,bshd,bshe->bhde', ws, k, v)
    n_new = dec[..., None] * n + jnp.einsum('bsh,bshd->bhd', ws, k)
    return (c_new, n_new, m_new), h

def pool_mlstm_layer(x, pool_prev, c0, n0, m0, prompt, norm_g, w_in, b_gate, w_pool, pool_scale, mh_norm_g, w_out):
    f32 = jnp.float32
    B, T, _ = x.shape
    h = rmsnorm(x, norm_g)
    proj = jnp.einsum('btd,de->bte', h, w_in)
    u, z_p, q, k, v, o, z_m, gts = split_cols(proj, (POOL_W, POOL_W, M_W, M_W, M_W, M_W, M_W, 2 * M_HEADS))
    buf = jnp.concatenate([pool_prev.astype(u.dtype), u], axis=1)
    y_pool = pool_mix(buf, T, w_pool, pool_scale) * jax.nn.silu(z_p)
    new_pool = buf[:, -POOL_STATE:]
    shp = (B, T, M_HEADS, M_HEAD_DIM)
    qh = q.reshape(shp).astype(f32)
    kh = k.reshape(shp).astype(f32) * (M_HEAD_DIM ** -0.5)
    vh = v.reshape(shp).astype(f32)
    gts = (gts + b_gate).astype(f32)
    ig = gts[..., :M_HEADS]
    lf = jax.nn.log_sigmoid(gts[..., M_HEADS:])
    if prompt:
        nc = T // M_CHUNK

        def to_chunks(a):
            return jnp.moveaxis(a.reshape((B, nc, M_CHUNK) + a.shape[2:]), 1, 0)

        init = (jnp.zeros((B, M_HEADS, M_HEAD_DIM, M_HEAD_DIM), f32),
                jnp.zeros((B, M_HEADS, M_HEAD_DIM), f32),
                jnp.zeros((B, M_HEADS), f32))
        (c1, n1, m1), hc = lax.scan(mlstm_chunk, init,
                                    (to_chunks(qh), to_chunks(kh), to_chunks(vh), to_chunks(ig), to_chunks(lf)))
        hcell = jnp.moveaxis(hc, 0, 1).reshape(shp)
    else:
        (c1, n1, m1), hcell = mlstm_chunk((c0.astype(f32), n0.astype(f32), m0.astype(f32)), (qh, kh, vh, ig, lf))
    hcell = hcell * jax.nn.sigmoid(o.astype(f32)).reshape(shp)
    hcell = hcell * lax.rsqrt(jnp.mean(hcell * hcell, axis=-1, keepdims=True) + EPS)
    y_m = (hcell.reshape(B, T, M_W) * mh_norm_g.astype(f32)).astype(x.dtype) * jax.nn.silu(z_m)
    y = jnp.einsum('bte,ed->btd', jnp.concatenate([y_pool, y_m], axis=-1), w_out)
    return x + y.astype(x.dtype), new_pool, c1, n1, m1

def cmp_attend(q, q_pos, blocks):
    B, Tq = q.shape[:2]
    nc = blocks.shape[1]
    qg = q.reshape(B, Tq, N_KV, Q_PER_KV, HEAD_DIM)
    s = jnp.einsum('bqgrd,bngd->bgrqn', qg, blocks[:, :, 0].astype(q.dtype)) * ATT_SCALE
    end = (jnp.arange(nc) + 1) * CMP_BLOCK - 1
    p = masked_softmax(s, end[None, :] <= q_pos[:, None])
    o = jnp.einsum('bgrqn,bngd->bqgrd', p.astype(q.dtype), blocks[:, :, 1].astype(q.dtype))
    return o.reshape(B, Tq, N_HEADS, HEAD_DIM), p

def sel_attend(q, q_pos, idx, rows):
    B, Tq = q.shape[:2]
    K = idx.shape[-1]
    qg = q.reshape(B, Tq, N_KV, Q_PER_KV, HEAD_DIM)
    pos = idx[..., None] * SEL_BLOCK + jnp.arange(SEL_BLOCK)
    mask = (pos <= q_pos[None, None, :, None, None]).reshape(B, N_KV, Tq, 1, K * SEL_BLOCK)
    s = jnp.einsum('bqgrd,bgqkld->bgqrkl', qg, rows[..., 0, :]) * ATT_SCALE
    p = masked_softmax(s.reshape(B, N_KV, Tq, Q_PER_KV, K * SEL_BLOCK), mask)
    p = p.reshape(B, N_KV, Tq, Q_PER_KV, K, SEL_BLOCK).astype(q.dtype)
    o = jnp.einsum('bgqrkl,bgqkld->bqgrd', p, rows[..., 1, :])
    return o.reshape(B, Tq, N_HEADS, HEAD_DIM)

def win_attend(q, q_pos, kv, k_pos):
    B, Tq = q.shape[:2]
    qg = q.reshape(B, Tq, N_KV, Q_PER_KV, HEAD_DIM)
    s = jnp.einsum('bqgrd,bsgd->bgrqs', qg, kv[:, :, 0]) * ATT_SCALE
    dpos = q_pos[:, None] - k_pos[None, :]
    mask = (dpos >= 0) & (dpos <= WINDOW) & (k_pos[None, :] >= 0)
    p = masked_softmax(s, mask).astype(q.dtype)
    o = jnp.einsum('bgrqs,bsgd->bqgrd', p, kv[:, :, 1])
    return o.reshape(B, Tq, N_HEADS, HEAD_DIM)

def nsa_layer(x, prompt, win_buf, cache_kv_cmp, cache_kv_sel, cache_kv_win, page_table, norm_g, w_in, b_gate, w_out):
    f32 = jnp.float32
    B, T, _ = x.shape
    h = rmsnorm(x, norm_g)
    proj = jnp.einsum('btd,de->bte', h, w_in)
    q, kv_c, kv_s, kv_w, gts, z = split_cols(proj, (NSA_W, KV_W, KV_W, KV_W, 3 * N_HEADS, NSA_W))
    q = q.reshape(B, T, N_HEADS, HEAD_DIM)
    kv_shape = (B, T, 2, N_KV, HEAD_DIM)
    kv_c = kv_c.reshape(kv_shape)
    kv_s = kv_s.reshape(kv_shape)
    kv_w = kv_w.reshape(kv_shape)
    past_len = 0 if prompt else page_table.shape[1] * PAGE_SIZE
    q_pos = past_len + jnp.arange(T)
    q_rot = rope(q, q_pos)
    kv_s = jnp.stack([rope(kv_s[:, :, 0], q_pos), kv_s[:, :, 1]], axis=2)
    kv_w = jnp.stack([rope(kv_w[:, :, 0], q_pos), kv_w[:, :, 1]], axis=2)
    s_total = past_len + T

    nb_new = T // CMP_BLOCK
    new_blocks = kv_c[:, :nb_new * CMP_BLOCK].astype(f32).reshape(B, nb_new, CMP_BLOCK, 2, N_KV, HEAD_DIM).mean(2)
    if prompt:
        blocks = new_blocks
    else:
        past_c = cache_kv_cmp[page_table].astype(f32)
        past_blocks = past_c.reshape(B, past_len // CMP_BLOCK, CMP_BLOCK, 2, N_KV, HEAD_DIM).mean(2)
        blocks = jnp.concatenate([past_blocks, new_blocks], axis=1)
    o_c, p_c = cmp_attend(q, q_pos, blocks.astype(q.dtype))

    n_sel = -(-s_total // SEL_BLOCK)
    nc = blocks.shape[1]
    imp = jnp.pad(p_c.sum(axis=2), ((0, 0), (0, 0), (0, 0), (0, 2 * n_sel - nc)))
    imp = imp.reshape(B, N_KV, T, n_sel, 2).sum(-1)
    blk = jnp.arange(n_sel)
    imp = jnp.where(blk[None, :] == (q_pos // SEL_BLOCK)[:, None], jnp.inf, imp)
    imp = jnp.where(blk[None, :] * SEL_BLOCK > q_pos[:, None], -jnp.inf, imp)
    k_top = min(SEL_TOPK, n_sel)
    _, idx = lax.top_k(imp, k_top)

    if prompt:
        kvs_blocks = jnp.moveaxis(kv_s.reshape(B, n_sel, SEL_BLOCK, 2, N_KV, HEAD_DIM), 4, 1)
        bi = jnp.arange(B)[:, None, None, None]
        gi = jnp.arange(N_KV)[None, :, None, None]
        nsb = T // SEL_Q_BLOCK
        q_blk = jnp.moveaxis(q_rot.reshape(B, nsb, SEL_Q_BLOCK, N_HEADS, HEAD_DIM), 1, 0)
        p_blk = q_pos.reshape(nsb, SEL_Q_BLOCK)
        i_blk = jnp.moveaxis(idx.reshape(B, N_KV, nsb, SEL_Q_BLOCK, k_top), 2, 0)
        o_s = lax.map(lambda a: sel_attend(a[0], a[1], a[2], kvs_blocks[bi, gi, a[2]]), (q_blk, p_blk, i_blk))
        o_s = jnp.moveaxis(o_s, 0, 1).reshape(B, T, N_HEADS, HEAD_DIM)

        nqb = T // ATT_Q_BLOCK
        kv_pad = jnp.concatenate([jnp.zeros((B, WINDOW, 2, N_KV, HEAD_DIM), kv_w.dtype), kv_w], axis=1)
        qw_blk = jnp.moveaxis(q_rot.reshape(B, nqb, ATT_Q_BLOCK, N_HEADS, HEAD_DIM), 1, 0)

        def win_block(a):
            qb, i = a
            start = i * ATT_Q_BLOCK
            kvb = lax.dynamic_slice_in_dim(kv_pad, start, WINDOW + ATT_Q_BLOCK, axis=1)
            k_pos = start - WINDOW + jnp.arange(WINDOW + ATT_Q_BLOCK)
            return win_attend(qb, start + jnp.arange(ATT_Q_BLOCK), kvb, k_pos)

        o_w = lax.map(win_block, (qw_blk, jnp.arange(nqb)))
        o_w = jnp.moveaxis(o_w, 0, 1).reshape(B, T, N_HEADS, HEAD_DIM)
        new_win = kv_pad[:, -win_buf:]
    else:
        pos = idx[..., None] * SEL_BLOCK + jnp.arange(SEL_BLOCK)
        bix = jnp.arange(B)[:, None, None, None, None]
        gix = jnp.arange(N_KV)[None, :, None, None, None]
        pp = jnp.minimum(pos, past_len - 1)
        phys = page_table[bix, pp // PAGE_SIZE]
        past_rows = cache_kv_sel[phys, pp % PAGE_SIZE, :, gix, :]
        new_rows = kv_s[bix, jnp.clip(pos - past_len, 0, T - 1), :, gix, :]
        rows = jnp.where((pos < past_len)[..., None, None], past_rows.astype(kv_s.dtype), new_rows)
        o_s = sel_attend(q_rot, q_pos, idx, rows)

        kvw_all = jnp.concatenate([cache_kv_win.astype(kv_w.dtype), kv_w], axis=1)
        k_pos = past_len - win_buf + jnp.arange(win_buf + T)
        o_w = win_attend(q_rot, q_pos, kvw_all, k_pos)
        new_win = kvw_all[:, -win_buf:]

    gate = jax.nn.sigmoid((gts + b_gate).astype(f32)).reshape(B, T, N_HEADS, 3)
    o = gate[..., 0:1] * o_c + gate[..., 1:2] * o_s + gate[..., 2:3] * o_w
    y = jnp.einsum('bte,ed->btd', o.reshape(B, T, NSA_W).astype(x.dtype) * jax.nn.silu(z), w_out)
    return x + y.astype(x.dtype), kv_c, kv_s, new_win

def setup_inputs(seed: int = 0) -> dict:
    key = jax.random.key(seed)
    ks = jax.random.split(key, 24)
    f32 = jnp.float32
    n_pages = PAST_LEN // PAGE_SIZE
    n_used = DEC_BATCH * n_pages
    n_pool = n_used + (n_used + 3) // 4
    page_table = jax.random.permutation(ks[0], n_pool)[:n_used].reshape(DEC_BATCH, n_pages).astype(jnp.int32)
    win_buf = min(WINDOW, PAST_LEN)

    def nrm(k, shape, scale):
        return jax.random.normal(k, shape, f32) * scale

    b_gate0 = jnp.concatenate([nrm(ks[13], (M_HEADS,), 0.1), 3.0 + nrm(ks[14], (M_HEADS,), 0.5)])
    return {
        'x_prompt': nrm(ks[1], (BATCH, SEQ, D_MODEL), 1.0),
        'x_sample': nrm(ks[2], (DEC_BATCH, DEC_SEQ, D_MODEL), 1.0),
        'state_pool': nrm(ks[3], (DEC_BATCH, POOL_STATE, POOL_W), 1.0),
        'state_mlstm_c': nrm(ks[4], (DEC_BATCH, M_HEADS, M_HEAD_DIM, M_HEAD_DIM), 0.05),
        'state_mlstm_n': nrm(ks[5], (DEC_BATCH, M_HEADS, M_HEAD_DIM), 0.5),
        'state_mlstm_m': nrm(ks[6], (DEC_BATCH, M_HEADS), 1.0),
        'cache_kv_cmp': nrm(ks[7], (n_pool, PAGE_SIZE, 2, N_KV, HEAD_DIM), 1.0),
        'cache_kv_sel': nrm(ks[8], (n_pool, PAGE_SIZE, 2, N_KV, HEAD_DIM), 1.0),
        'cache_kv_win': nrm(ks[9], (DEC_BATCH, win_buf, 2, N_KV, HEAD_DIM), 1.0),
        'page_table': page_table,
        'norm0_g': 1.0 + nrm(ks[10], (D_MODEL,), 0.1),
        'w_in0': nrm(ks[11], (D_MODEL, IN0), D_MODEL ** -0.5),
        'b_gate0': b_gate0,
        'w_pool': nrm(ks[12], (len(POOL_WINDOWS), POOL_GROUP_W, POOL_GROUP_W), POOL_GROUP_W ** -0.5),
        'pool_scale': 1.0 + nrm(ks[15], (POOL_W,), 0.1),
        'mh_norm_g': 1.0 + nrm(ks[16], (M_W,), 0.1),
        'w_out0': nrm(ks[17], (POOL_W + M_W, D_MODEL), (POOL_W + M_W) ** -0.5),
        'norm1_g': 1.0 + nrm(ks[18], (D_MODEL,), 0.1),
        'w_in1': nrm(ks[19], (D_MODEL, IN1), D_MODEL ** -0.5),
        'b_gate1': nrm(ks[20], (3 * N_HEADS,), 0.1),
        'w_out1': nrm(ks[21], (NSA_W, D_MODEL), NSA_W ** -0.5),
        'final_g': 1.0 + nrm(ks[22], (D_MODEL,), 0.1),
    }

def reference(x_prompt, x_sample, state_pool, state_mlstm_c, state_mlstm_n, state_mlstm_m,
              cache_kv_cmp, cache_kv_sel, cache_kv_win, page_table,
              norm0_g, w_in0, b_gate0, w_pool, pool_scale, mh_norm_g, w_out0,
              norm1_g, w_in1, b_gate1, w_out1, final_g):
    xp, xs = x_prompt, x_sample
    win_buf = cache_kv_win.shape[1]
    empty_pool = jnp.zeros((xp.shape[0], 0, POOL_W), xp.dtype)
    for layer in range(DEPTH):
        if layer % 2 == 0:
            xp, pool_p, c_p, n_p, m_p = pool_mlstm_layer(
                xp, empty_pool, None, None, None, True,
                norm0_g, w_in0, b_gate0, w_pool, pool_scale, mh_norm_g, w_out0)
            xs, pool_s, c_s, n_s, m_s = pool_mlstm_layer(
                xs, state_pool, state_mlstm_c, state_mlstm_n, state_mlstm_m, False,
                norm0_g, w_in0, b_gate0, w_pool, pool_scale, mh_norm_g, w_out0)
        else:
            xp, kvc_p, kvs_p, kvw_p = nsa_layer(
                xp, True, win_buf, None, None, None, None, norm1_g, w_in1, b_gate1, w_out1)
            xs, kvc_s, kvs_s, kvw_s = nsa_layer(
                xs, False, win_buf, cache_kv_cmp, cache_kv_sel, cache_kv_win, page_table,
                norm1_g, w_in1, b_gate1, w_out1)
    y_prompt = rmsnorm(xp, final_g)
    y_sample = rmsnorm(xs, final_g)
    return (y_prompt, y_sample, pool_p, pool_s, c_p, c_s, n_p, n_s, m_p, m_s,
            kvc_p, kvc_s, kvs_p, kvs_s, kvw_p, kvw_s)


_drawn_inputs = setup_inputs


def setup_inputs(seed=0):
    import zlib

    import numpy as np

    out = dict(_drawn_inputs(seed))
    spreads = {}
    factors = {'cache_kv_cmp': 4.668, 'cache_kv_sel': 2.693, 'b_gate1': 8.0}
    for name, (base, spread) in spreads.items():
        noise = np.random.default_rng([zlib.crc32(name.encode()), seed]).standard_normal(out[name].shape)
        drawn = base * np.exp(spread * noise) if base else spread * noise
        out[name] = __import__('jax').numpy.asarray(drawn.astype(out[name].dtype))
    for name, factor in factors.items():
        out[name] = (out[name] * factor).astype(out[name].dtype)
    return out
```

```python
from contextlib import ExitStack, contextmanager

import numpy as np

import concourse.bass as bass
from concourse import mybir

F32 = mybir.dt.float32
F32R = mybir.dt.float32r
I32 = mybir.dt.int32
ACT = mybir.ActivationFunctionType
ALU = mybir.AluOpType
AX = mybir.AxisListType.X

P = 128
D = 2048
KT = D // P
TP, NS = 512, 8
TA = TP + NS
HALF = TA // 2
NT = TP // P
GH, HD = 4, 256
NH, NKV, DH = 16, 4, 128
QPK = NH // NKV
PAST, PAGE, NPG = 512, 128, 4
NB = 16
NEG = -1.0e30
SCALE = DH ** -0.5
EPS = 1e-6

C_ID, C_ONE, C_COMMON = 0, 128, 256
C0_MASKT, C0_OH8, C0_PSEL, C0_ICNT, C0_SELI, C0_SELF, C0_N = 0, 128, 1152, 1184, 1248, 1252, 1256
(C1_NEG, C1_COS, C1_SIN, C1_CMP, C1_AVG, C1_EXP, C1_GM, C1_GS, C1_N) = (
    0, 128, 648, 1168, 1232, 1236, 1748, 1876, 1880)

R_G0, R_G1, R_GF, R_PS, R_MH = 0, 16, 32, 48, 56

G0_BASE, P_BASE, M_BASE, O0_BASE, G1_BASE, A_BASE, O1_BASE, N_TILES = 0, 1, 17, 57, 73, 74, 130, 146


def constants():
    cc = np.zeros((P, C_COMMON), np.float32)
    cc[:, 0:128] = np.eye(P)
    cc[:, 128:256] = 1.0
    c0 = np.zeros((P, C0_N), np.float32)
    s = np.arange(P)
    c0[:, C0_MASKT:C0_MASKT + P] = s[None, :] >= s[:, None]
    for b in range(NS):
        c0[b, C0_OH8 + b * P:C0_OH8 + (b + 1) * P] = 1.0
    for g in range(4):
        for b in range(NS):
            for r in range(15):
                if r >= 15 - (2 ** (g + 1) - 1):
                    c0[b * 15 + r, C0_PSEL + g * 8 + b] = 1.0
        c0[:, C0_ICNT + g * 16:C0_ICNT + (g + 1) * 16] = 1.0 / np.minimum(np.arange(1, 17), 2 ** (g + 1))
    for h in range(4):
        c0[120 + h, C0_SELI + h] = 1.0
        c0[124 + h, C0_SELF + h] = 1.0
    c1 = np.zeros((P, C1_N), np.float32)
    c1[:, C1_NEG:C1_NEG + P] = np.where(s[None, :] <= s[:, None], 0.0, NEG)
    half = DH // 2
    inv = (np.float32(10000.0) ** (-np.arange(half, dtype=np.float32) / np.float32(half))).astype(np.float32)
    pos = np.concatenate([np.arange(TP), np.full(NS, PAST)]).astype(np.float32)
    ang = (inv[:, None] * pos[None, :]).astype(np.float32)
    c1[:, C1_COS:C1_COS + TA] = np.concatenate([np.cos(ang), np.cos(ang)])
    c1[:, C1_SIN:C1_SIN + TA] = np.concatenate([-np.sin(ang), np.sin(ang)])
    for i in range(NT):
        for n in range(NB):
            c1[:, C1_CMP + i * NB + n] = np.where((n + 1) * 32 - 1 <= i * P + s, 0.0, NEG)
    for n in range(4):
        c1[n * 32:(n + 1) * 32, C1_AVG + n] = 1.0 / 32
    for pg in range(NPG):
        for n in range(4):
            c1[pg * 4 + n, C1_EXP + pg * P + n * 32:C1_EXP + pg * P + (n + 1) * 32] = 1.0 / 32
    for h in range(NH):
        c1[3 * h:3 * h + 3, C1_GM + h * 8:C1_GM + h * 8 + 8] = 1.0
        for r in range(3):
            c1[3 * h + r, C1_GS + r] = 1.0
    return cc, c0, c1


class Own:

    def __init__(self, eng, S, name):
        self.eng, self.S, self.name = eng, S, name
        self.base, self.n = {}, {}

    def done(self, name):
        self.n[name] = self.n.get(name, 0) + 1
        self.eng.wait_ge(self.S[name], self.base.get(name, 0) + self.n[name])

    def step(self, ins):
        ins.then_inc(self.S[self.name], 1)
        self.done(self.name)

    @contextmanager
    def turns(self, count, per_turn):
        names = set(self.base) | set(self.n) | set(per_turn)
        first = {k: self.base.get(k, 0) + self.n.get(k, 0) for k in names}
        with self.eng.Fori(0, count) as i:
            self.base = {k: first[k] + i * per_turn[k] if k in per_turn else first[k] for k in names}
            self.n = {}
            yield i
            if self.n != per_turn:
                raise AssertionError(("PER", self.n))
        self.base = {k: first[k] + count * per_turn.get(k, 0) for k in names}
        self.n = {}


class Tile:

    def __init__(self, base, j, i=0, per=0):
        self.p = (base + j) % 2
        self.n = base + j + i * per
        self.m = (base + j) // 2 + i * (per // 2)
        self.first = base + j < 2

    def ahead(self, k):
        t = Tile.__new__(Tile)
        t.p, t.n = (self.p + k) % 2, self.n + k
        assert k == 2
        t.m, t.first = self.m + 1, False
        return t


ACT_POOL = {'w_hi': 4}
ACT_HEAD = {'w_hi': 10, 'm_ws': 1, 'm_vr': 1, 'm_D': 4, 'm_abs': 1, 'm_st': 1, 'm_nst': 1, 'c_sc': 8, 'm_sq': 2, 'm_sqrt': 1}
ACT_GROUP = {'w_hi': 14, 'a_row': 6, 'a_sw': 6, 'a_cexp': 1, 'at_exp': 16, 'at_pta': 16}
DVE_HEAD = {'w_split': 10, 'm_wsin': 1, 'm_prod': 1, 'm_dt': 4, 'm_kr': 1, 'm_vd': 1, 'dve_step': 14, 'm_P': 4, 'm_kw': 1, 'm_nT': 1, 'm_decr': 1, 'm_y': 1, 'm_oy': 2, 'm_nev': 1, 'm_cn': 16, 'm_var': 1, 'm_yz': 2}
DVE_GROUP = {'dve_step': 63, 'a_src': 6, 'w_split': 14, 'a_rot': 6, 'a_vcr': 1, 'a_qd': 1, 'a_cin': 1, 'at_nm': 16, 'a_cp': 1, 'at_diag': 32, 'a_ptc': 4, 'at_ptb': 16, 'at_oe': 16, 'a_yz': 4}


def trunk(nc, I, O):
    ctx = ExitStack()
    with ctx:
        def sb(name, shape, dt=F32):
            return ctx.enter_context(nc.sbuf_tensor(name, shape, dt))

        def sem(name):
            return ctx.enter_context(nc.semaphore(name))

        XY = sb("xy", [P, KT, TA])
        WR = sb("w_raw", [P, 2, KT, P])
        WH = sb("w_hi", [P, 2, KT, P], F32R)
        WL = sb("w_lo", [P, 2, KT, P], F32R)
        CC = sb("c_common", [P, C_COMMON])
        PR = sb("params", [P, 64])
        RS = sb("rstd", [P, TA])
        XR = sb("x_res", [P, 2, TA])
        ident, ones = CC[:, C_ID:C_ID + P], CC[:, C_ONE:C_ONE + P]
        PS = ctx.enter_context(nc.psum_tensor("ps", [P, 8, 512], F32))

        with nc.sbuf_tensor("h_hi", [P, KT, TA], F32R) as HH, nc.sbuf_tensor("h_lo", [P, KT, TA], F32R) as HL:
            pass
        DB_LEN = 2 * KT * TA
        DB = sb("sample_cache", [P, DB_LEN])

        def scratch(spec):
            at, out = 0, {}
            for name, shape in spec:
                n = int(np.prod(shape))
                v = SC[:, at:at + n]
                if len(shape) == 2:
                    v = v.rearrange("p (a b) -> p a b", b=shape[1])
                elif len(shape) == 3:
                    v = v.rearrange("p (a b c) -> p a b c", b=shape[1], c=shape[2])
                out[name] = v
                at += n
            assert at <= SC_LEN, (at, SC_LEN)
            return out

        SC_LEN = 18100
        SC = sb("scratch", [P, SC_LEN])
        SMALL0 = 240
        S0 = scratch([("c0", (C0_N,)), ("bg", (4,)), ("acol", (16,)), ("nT", (8, NS)), ("ws", (4,)), ("kdw", (2, NS)),
                      ("pr", (2, 16)), ("dtmp", (10, NS)), ("nTh", (2, NS)), ("pad", (8,)),
                      ("qT", (2, TA)), ("kT", (2, TA)), ("vT", (2, TA)), ("vr", (NT * HD,)), ("kr", (NT * HD,)),
                      ("pt", (2, 512)), ("dt", (2, 512)), ("ad", (512,)), ("gbc", (4, 1048)), ("cb", (NS, 512)),
                      ("vdr", (HD,))])
        S0["nor"], S0["nst"] = S0["vdr"][32:32 + NS], S0["vdr"][64:65]
        S0b = scratch([("c0", (C0_N,)), ("small", (SMALL0,)), ("ub", (2, 536)), ("sa", (2, 528)), ("sb", (2, 528)),
                       ("pl", (2, TA)), ("zt", (2, TA)), ("wp", (2, 256)), ("tail", (1024,)), ("sp", (1024,)),
                       ("us", (2, NS)), ("ss", (8, NS))])
        row0 = C0_N + SMALL0
        XROW = SC[:, row0:row0 + 4096].rearrange("p (a b) -> p a b", b=D)
        XSROW = SC[:, row0 + 4096:row0 + 4096 + D]
        PRROW = SC[:, row0 + 6144:row0 + 6144 + P]
        NROW = SC[:, row0 + 6272:row0 + 6272 + 1024]
        GR0 = SC_LEN - 5300
        IGR, FGR, LFR, T1R = (SC[0:4, GR0 + k * TA:GR0 + (k + 1) * TA] for k in range(4))
        BR, AR = SC[0:4, GR0 + 2080:GR0 + 2592], SC[0:4, GR0 + 2592:GR0 + 3104]
        MR = SC[0:4, GR0 + 3104:GR0 + 3104 + 1048]
        GONE = SC[0:4, GR0 + 4160:GR0 + 4672]
        GM0, GD = SC[0:4, GR0 + 4672:GR0 + 4680], SC[0:4, GR0 + 4680:GR0 + 4720]
        S1 = scratch([("c1", (C1_N,)), ("bg", (4,)), ("kT", (2, TA)), ("vr", (2, NT * DH)), ("rs", (4, NT * DH)),
                      ("qr", (QPK, TA)), ("qt", (QPK, TA)), ("pr", (4, 512)), ("pt", (2, 512)), ("dg", (4, P)),
                      ("kcb", (NB,)), ("vcT", (NB,)), ("vcr", (DH,)), ("ptc", (2, 512)), ("sc", (16, NB)),
                      ("cst", (4, 16)), ("st", (8, 2)), ("gw", (48, NT)), ("kd", (4, NKV, NS)), ("qd", (2, NH * NS)),
                      ("zs", (NH, NS)), ("rd", (6, DH)), ("gd", (P,)), ("gdr", (4,)), ("dst", (8, 4)), ("pc", (P,)),
                      ("pg", (32,))])
        cosT, sinT = S1["c1"][:, C1_COS:C1_COS + TA], S1["c1"][:, C1_SIN:C1_SIN + TA]
        KV = DB[:, 0:12288].rearrange("p (s k a b) -> p s k a b", s=2, k=3, a=NPG)
        ZQ = DB[:, 12288:14336].rearrange("p (r g b c) -> p r g b c", r=2, g=4, b=NS)
        PTD = DB[:, 14336:15872].rearrange("p (k a r) -> p k a r", k=3, a=NPG)
        YROW = DB[:, 0:8192].rearrange("p (s c) -> p s c", s=4)
        YSROW = DB[:, 8192:8192 + D]

        x_scr = nc.dram_tensor("x_scratch", [P, KT, TA], F32).ap()
        g_scr = nc.dram_tensor("gate_scratch", [4, 1048], F32).ap()

        class Signals(dict):

            def __missing__(self, name):
                self[name] = sem(name)
                return self[name]

        S = Signals()
        w_loaded = [S["w_loaded0"], S["w_loaded1"]]
        proj_read = [S["proj_read0"], S["proj_read1"]]
        block = ctx.enter_context(nc.Block())

        STREAM = {}

        def where(n):
            if n < P_BASE:
                return "w_in0", 7176 - P
            if n < M_BASE:
                return at_pool((n - P_BASE) // 4, (n - P_BASE) % 4)
            if n < O0_BASE:
                return at_head((n - M_BASE) // 10, (n - M_BASE) % 10)
            if n < G1_BASE:
                return "w_out0", (n - O0_BASE) * P
            if n < A_BASE:
                return "w_in1", 5120
            if n < O1_BASE:
                return at_group((n - A_BASE) // 14, (n - A_BASE) % 14)
            return "w_out1", (n - O1_BASE) * P

        def at_pool(g, j):
            return "w_in0", (j // 2) * 1024 + g * 256 + (j % 2) * P

        def at_head(h, j):
            return "w_in0", 2048 + 1024 * (j // 2) + 256 * h + P * (j % 2)

        def at_group(g, j):
            if j < 6:
                return "w_in1", 2048 + 512 * j + P * g
            return "w_in1", (512 * g + P * (j - 6) if j < 10 else 5168 + 512 * g + P * (j - 10))

        def load_tile(q, t, w, col):
            if not t.first:
                q.wait_ge(S["w_split"], t.n - 1)
            q.dma_start(WR[:, t.p], I[w].rearrange("(k p) n -> p k n", p=P)[:, :, bass.ds(col, P)]
                        ).then_inc(w_loaded[t.p], 16)

        def load_ahead(sp, base, j, i, per, at, last):
            t = Tile(base, j, i, per).ahead(2)
            if last:
                load_tile(sp, t, *where(base + per * i + j + 2))
            else:
                load_tile(sp, t, *(at(i, j + 2) if j + 2 < per else at(i + 1, j + 2 - per)))

        def sp_turns(sp, count, body):
            if count > 1:
                with sp.Fori(0, count - 1) as i:
                    body(i, False)
            body(count - 1, True)

        def split_hi(act, own, t):
            act.wait_ge(w_loaded[t.p], (t.m + 1) * 16)
            if not t.first:
                act.wait_ge(S["proj_done"], t.n - 1)
            nc.scalar.activation(WH[:, t.p], WR[:, t.p], ACT.Copy).then_inc(S["w_hi"], 1); own.done("w_hi")

        def split_lo(dve, own, t):
            dve.wait_ge(S["w_hi"], t.n + 1)
            nc.vector.tensor_tensor(WL[:, t.p], WR[:, t.p], WH[:, t.p].bitcast(F32), ALU.subtract
                                    ).then_inc(S["w_split"], 1); own.done("w_split")

        def project(pe, t, h_need=None):
            pe.wait_ge(S["w_split"], t.n + 1)
            if not t.first:
                pe.wait_ge(proj_read[t.p], t.m)
            for k in range(KT):
                if h_need is not None and k % 2 == 0:
                    pe.wait_ge(S["h_ready"], h_need + k + 2)
                for x, (w, h) in enumerate(((WH, HH), (WH, HL), (WL, HH))):
                    for c in range(2):
                        mm = nc.tensor.matmul(PS[:, 2 * t.p + c, 0:HALF], lhsT=w[:, t.p, k, :],
                                              rhs=h[:, k, c * HALF:(c + 1) * HALF],
                                              start=(k == 0 and x == 0), stop=(k == KT - 1 and x == 2))
            mm.then_inc(S["proj_done"], 1)

        def halves(ap):
            return ap.rearrange("p (a b) -> p a b", b=HALF)

        def ps2(t, q=slice(0, P)):
            return PS[q, 2 * t.p:2 * t.p + 2, 0:HALF]

        def ps_pair(bank, q=slice(0, P)):
            return PS[q, bank:bank + 2, 0:HALF]

        def norm_act(act, own, r):
            for k in range(KT):
                if r * KT + k >= 2:
                    act.wait_ge(S["nrm_mm"], r * KT + k - 1)
                nc.scalar.activation(XR[:, k % 2], XY[:, k], ACT.Square).then_inc(S["nrm_sq"], 1); own.done("nrm_sq")
            act.wait_ge(S["nrm_var"], r + 1)
            nc.scalar.activation(RS[:], RS[:], ACT.Sqrt).then_inc(S["nrm_sqrt"], 1); own.done("nrm_sqrt")

        def norm_pe(pe, r):
            for k in range(KT):
                pe.wait_ge(S["nrm_sq"], r * KT + k + 1)
                for c in range(2):
                    mm = nc.tensor.matmul(PS[:, 4 + c, 0:HALF], lhsT=ones, rhs=XR[:, k % 2, c * HALF:(c + 1) * HALF],
                                          start=(k == 0), stop=(k == KT - 1))
                mm.then_inc(S["nrm_mm"], 1)

        def norm_dve(dve, own, r):
            dve.wait_ge(S["nrm_mm"], (r + 1) * KT)
            nc.vector.tensor_scalar(halves(RS[:]), ps_pair(4), 1.0 / D, EPS, ALU.mult, ALU.add
                                    ).then_inc(S["nrm_var"], 1); own.done("nrm_var")
            dve.wait_ge(S["nrm_sqrt"], r + 1)
            own.step(nc.vector.reciprocal(RS[:], RS[:]))

        def h_dve(dve, own, r, gcol):
            def low(k):
                dve.wait_ge(S["h_hi"], r * KT + k + 1)
                nc.vector.tensor_tensor(HL[:, k], XR[:, k % 2], HH[:, k].bitcast(F32), ALU.subtract
                                        ).then_inc(S["h_ready"], 1); own.done("h_ready")
            for k in range(KT):
                nc.vector.scalar_tensor_tensor(XR[:, k % 2], XY[:, k], PR[:, gcol + k:gcol + k + 1], RS[:],
                                               ALU.mult, ALU.mult).then_inc(S["h_tmp"], 1); own.done("h_tmp")
                if k:
                    low(k - 1)
            low(KT - 1)

        def h_act(act, own, r):
            for k in range(KT):
                act.wait_ge(S["h_tmp"], r * KT + k + 1)
                nc.scalar.activation(HH[:, k], XR[:, k % 2], ACT.Copy).then_inc(S["h_hi"], 1); own.done("h_hi")

        def y_split_act(act, own, r, done):
            act.wait_ge(S["proj_done"], done)
            for k in range(KT):
                nc.scalar.activation(HH[:, k], XY[:, k], ACT.Copy).then_inc(S["y_hi"], 1); own.done("y_hi")

        def y_split_dve(dve, own, r):
            for k in range(KT):
                dve.wait_ge(S["y_hi"], r * KT + k + 1)
                nc.vector.tensor_tensor(HL[:, k], XY[:, k], HH[:, k].bitcast(F32), ALU.subtract
                                        ).then_inc(S["h_ready"], 1); own.done("h_ready")

        def out_dve(dve, own, r, base):
            def body(i, last):
                for j in range(2):
                    t = Tile(base, j, i, 2)
                    dve.wait_ge(S["proj_done"], t.n + 1)
                    dve.wait_ge(S[f"x_res{j}"], (i + 8 * r + 1) * 16)
                    nc.vector.tensor_tensor(halves(XY[:, 2 * i + j, :]), ps2(t), halves(XR[:, j]), ALU.add
                                            ).then_inc(proj_read[t.p], 1); dve.wait_ge(proj_read[t.p], t.m + 1)
                    if not last:
                        split_lo(dve, own, t.ahead(2))
            with own.turns(8 - r, {"w_split": 2}) as i:
                body(i, False)
            if r:
                body(7, True)

        def out_act(act, own, r, base):
            with own.turns(8 - r, {"w_hi": 2}) as i:
                for j in range(2):
                    split_hi(act, own, Tile(base, j, i, 2).ahead(2))

        def out_pe(pe, r, base, h_need):
            with pe.Fori(0, 8) as i:
                for j in range(2):
                    project(pe, Tile(base, j, i, 2), h_need if j == 0 else None)

        def out_sp(sp, r, base, nxt):
            def body(i, last):
                for j in range(2):
                    t = Tile(base, j, i, 2)
                    if not (last and nxt is None):
                        load_ahead(sp, base, j, i, 2, lambda i, j: ("w_out1" if r else "w_out0", (2 * i + j) * P), last)
                    sp.wait_ge(proj_read[t.p], t.m)
                    sp.dma_start(XR[:, j], x_scr[:, bass.ds(2 * i + j, 1), :].rearrange("p a t -> p (a t)")
                                 ).then_inc(S[f"x_res{j}"], 16)
            sp_turns(sp, 8, body)

        kvout = [("kvc", 0), ("kvc", 1), ("kvs", 0), ("kvs", 1), ("kvw", 0), ("kvw", 1)]

        @block.sync
        def _(sp):
            xp = I["x_prompt"].rearrange("a (i p) d -> (a i) p d", p=P)
            sp.dma_start(CC[:], I["c_common"]).then_inc(S["consts"], 16)
            for i in range(2):
                sp.dma_start(XROW[:, i], xp[i]).then_inc(S[f"xrow_in{i}"], 16)
            load_tile(sp, Tile(G0_BASE, 0), *where(0))
            load_tile(sp, Tile(P_BASE, 0), *where(1))
            for i in range(2, NT):
                sp.wait_ge(S["xt_made"], 4 * (i - 1))
                sp.dma_start(XROW[:, i % 2], xp[i]).then_inc(S[f"xrow_in{i % 2}"], 16)
            sp.dma_start(S0["c0"], I["c_layer0"]).then_inc(S["consts"], 16)
            sp.dma_start(XSROW[0:NS], I["x_sample"].rearrange("b o d -> (b o) d")).then_inc(S["small_in"], 16)
            for name, row, n in (("norm0_g", R_G0, 16), ("norm1_g", R_G1, 16), ("final_g", R_GF, 16),
                                 ("pool_scale", R_PS, 8), ("mh_norm_g", R_MH, 8)):
                sp.dma_start(PRROW[row:row + n], I[name].rearrange("(k p) -> k p", p=P)).then_inc(S["small_in"], 16)
            sp.dma_start(NROW[0:NS], I["state_mlstm_n"].rearrange("b h d -> b (h d)")).then_inc(S["small_in"], 16)
            sp.dma_start(S0["bg"][0:4, 0:2], I["b_gate0"].rearrange("(a h) -> h a", a=2),
                         allow_slow_non_contiguous=True).then_inc(S["small_in"], 16)
            sp.dma_start(GM0, I["state_mlstm_m"].rearrange("b h -> h b"),
                         allow_slow_non_contiguous=True).then_inc(S["small_in"], 16)
            load_ahead(sp, G0_BASE, 0, 0, 1, None, True)
            sp.wait_ge(S["xt_act"], 8)
            sp.wait_ge(S["xt_dve"], 9)
            sp.dma_start(x_scr, XY[:]).then_inc(S["x_saved"], 16)
            sp.wait_ge(S["npt_ready"], 1)
            sp.dma_start(S0b["sp"][0:120], I["state_pool"].rearrange("b r c -> (b r) c")).then_inc(S["sp_in"], 16)
            sp.dma_start(O["pool_s"][:, 0:14], I["state_pool"][:, 1:15]).then_inc(S["pool_out"], 16)

            def load_map(g):
                sp.dma_start(S0b["wp"], I["w_pool"][bass.ds(g, 1)].rearrange("o (c p) d -> p (o c) d", p=P)
                             ).then_inc(S["wp_in"], 16)

            def pool(g, last):
                for j in range(4):
                    load_ahead(sp, P_BASE, j, g, 4, at_pool, last)
                if not last:
                    sp.wait_ge(S["pl_mm"], g + 1)
                    load_map(g + 1)
            load_map(0)
            sp_turns(sp, 4, pool)

            sp.wait_ge(S["g_mr"], 1)
            sp.dma_start(g_scr, MR).then_inc(S["g_saved"], 16)
            sp.dma_start(O["m_p"].rearrange("o h -> h o"), GD[:, 32:33],
                         allow_slow_non_contiguous=True).then_inc(S["m_out"], 16)
            sp.dma_start(O["m_s"].rearrange("b h -> h b"), GD[:, 0:8],
                         allow_slow_non_contiguous=True).then_inc(S["m_out"], 16)
            sp.wait_ge(S["pl_ready"], 4)
            tail = S0b["tail"]
            sp.dma_start(O["pool_p"].rearrange("a r c -> (a r) c"), tail[0:15]).then_inc(S["tail_out"], 16)
            sp.dma_start(O["pool_s"][:, 14], tail[15:23]).then_inc(S["tail_out"], 16)
            sp.wait_ge(S["g_saved"], 16)
            sp.wait_ge(S["m_out"], 32)
            sp.wait_ge(S["pl_y"], 8 + 1)
            sp.wait_ge(S["tail_out"], 32)
            sp.wait_ge(S["g_acolT"], 1)
            for h in range(4):
                sp.dma_start(S0["gbc"][:, h], g_scr[h:h + 1, :].partition_broadcast(P)
                             ).then_inc(S["g_bc"], 16)

            def load_states(h):
                for b in range(NS):
                    sp.dma_start(S0["cb"][:, b].rearrange("p (c e) -> p c e", c=2),
                                 I["state_mlstm_c"][b, bass.ds(h, 1)].rearrange("o (c p) e -> p (o c) e", p=P)
                                 ).then_inc(S["c_in"], 16)

            def head(h, last):
                for j in range(10):
                    load_ahead(sp, M_BASE, j, h, 10, at_head, last)
                sp.wait_ge(S["m_st"], h + 1)
                sp.wait_ge(S["m_nst"], h + 1)
                sp.dma_start(O["c_p"][0, bass.ds(h, 1)].rearrange("o (c p) e -> p (o c) e", p=P),
                             S0["kr"][:, 0:512].rearrange("p (c e) -> p c e", c=2)).then_inc(S["st_out"], 16)
                sp.dma_start(O["n_p"][0, bass.ds(h, 1)], S0["nst"]).then_inc(S["st_out"], 16)
                sp.wait_ge(S["m_nev"], h + 1)
                sp.dma_start(O["n_s"][:, bass.ds(h, 1)].rearrange("b o d -> b (o d)"), S0["nor"]
                             ).then_inc(S["n_out"], 16)
                for b in range(NS):
                    sp.wait_ge(S["m_cn"], h * (2 * NS) + 2 * b + 2)
                    sp.dma_start(O["c_s"][b, bass.ds(h, 1)].rearrange("o (c p) e -> p (o c) e", p=P),
                                 S0["cb"][:, b].rearrange("p (c e) -> p c e", c=2)).then_inc(S["c_out"], 16)
                if not last:
                    sp.wait_ge(S["c_out"], (h + 1) * (16 * NS))
                    load_states(h + 1)
            load_states(0)
            sp_turns(sp, 4, head)

            out_sp(sp, 0, O0_BASE, G1_BASE)
            sp.wait_ge(S["c_out"], 64 * NS)
            sp.wait_ge(S["st_out"], 128)
            sp.wait_ge(S["n_out"], 64)
            sp.dma_start(S1["c1"], I["c_layer1"]).then_inc(S["consts"], 16)
            sp.dma_start(S1["bg"][0:48, 0:1], I["b_gate1"].rearrange("(a o) -> a o", o=1),
                         allow_slow_non_contiguous=True).then_inc(S["consts"], 16)
            sp.dma_start(S1["pg"][0:1].bitcast(I32), I["page_table"].rearrange("(o b) n -> o (b n)", o=1)
                         ).then_inc(S["consts"], 16)
            load_ahead(sp, G1_BASE, 0, 0, 1, None, True)
            sp.wait_ge(proj_read[0], (G1_BASE + 1) // 2)
            sp.wait_ge(proj_read[1], G1_BASE // 2)
            sp.dma_start(x_scr, XY[:]).then_inc(S["x_saved"], 16)

            def group(g, last):
                for j in range(14):
                    load_ahead(sp, A_BASE, j, g, 14, at_group, last)
                    if j == 9:
                        sp.wait_ge(S["a_row"], 6 * g + 6)
                        for x in (1, 0, 2, 3, 4, 5):
                            name, c = kvout[x]
                            src = S1["rs"][:, (0, 1, 2, None, 3)[x]] if x in (0, 1, 2, 4) else S1["vr"][:, x // 4]
                            sp.dma_start(O[name + "_p"][0, :, c, bass.ds(g, 1)].rearrange("(i p) o d -> p i (o d)", p=P),
                                         src.rearrange("p (i d) -> p i d", d=DH)).then_inc(S["row_out"], 16)
                            dst = O["kvw_s"][:, 511, c, bass.ds(g, 1)] if name == "kvw" else \
                                O[name + "_s"][:, 0, c, bass.ds(g, 1)]
                            sp.dma_start(dst.rearrange("b o d -> b (o d)"), S1["rd"][0:NS, x]).then_inc(S["row_out"], 16)
            sp_turns(sp, 4, group)

            sp.wait_ge(S["proj_done"], O1_BASE)
            caches = (I["cache_kv_cmp"], I["cache_kv_sel"], I["cache_kv_win"])
            sp.wait_ge(S["consts"], 16 * 5)

            def move_window(u):
                c, b = u // NS, u % NS
                sp.wait_ge(S[f"d_in{u % 2}"], 144 * (u // 2 + 1))
                out = O["kvw_s"][b, :, c].rearrange("t g d -> t (g d)")
                sp.dma_start(out[0:127], KV[1:P, u % 2, 2, 0]).then_inc(S["win_out"], 16)
                sp.dma_start(out[127:511].rearrange("(a p) d -> p a d", p=P), KV[:, u % 2, 2, 1:NPG]
                             ).then_inc(S["win_out"], 16)

            for c in range(2):
                for b in range(NS):
                    u = c * NS + b
                    if u >= 2:
                        sp.wait_ge(S["d_used"], u - 1)
                        sp.wait_ge(S["win_out"], 32 * (u - 1))
                    for pg in range(NPG):
                        page = sp.value_load(S1["pg"][0:1, b * NPG + pg:b * NPG + pg + 1].bitcast(I32),
                                             min_val=0, max_val=I["cache_kv_cmp"].shape[0] - 1)
                        for kind in range(2):
                            sp.dma_start(KV[:, u % 2, kind, pg],
                                         caches[kind][bass.ds(page, 1), :, c].rearrange("o p g d -> p (o g d)")
                                         ).then_inc(S[f"d_in{u % 2}"], 16)
                    sp.dma_start(KV[:, u % 2, 2],
                                 caches[2][b, :, c].rearrange("(a p) g d -> p a (g d)", p=P)).then_inc(S[f"d_in{u % 2}"], 16)
                    if u:
                        move_window(u - 1)
            move_window(2 * NS - 1)
            sp.wait_ge(S["win_out"], 32 * 2 * NS)
            out_sp(sp, 1, O1_BASE, None)

            for i in range(NT):
                sp.wait_ge(S["fin_act"], 2 * i + 2)
                sp.wait_ge(S["fin_dve"], 2 * i + 2)
                sp.dma_start(O["y_prompt"][0, i * P:(i + 1) * P], YROW[:, i]).then_inc(S["y_out"], 16)
            sp.wait_ge(S["fin_act"], 2 * NT + 2)
            sp.wait_ge(S["fin_dve"], 2 * NT + 2)
            sp.dma_start(O["y_sample"][:, 0], YSROW[0:NS]).then_inc(S["y_out"], 16)
            for name, n in (("y_out", 16 * (NT + 1)), ("row_out", 16 * 48), ("win_out", 512), ("c_out", 64 * NS),
                            ("st_out", 128), ("n_out", 64), ("pool_out", 16), ("tail_out", 32), ("m_out", 32),
                            ("x_saved", 32), ("g_saved", 16)):
                sp.wait_ge(S[name], n)

        @block.tensor
        def _(pe):
            T = nc.tensor.transpose
            M = nc.tensor.matmul
            c0 = S0["c0"]
            pe.wait_ge(S["consts"], 16)
            for i in range(NT):
                pe.wait_ge(S[f"xrow_in{i % 2}"], (i // 2 + 1) * 16)
                for kk in range(4):
                    f = 4 * i + kk
                    if f >= 4:
                        pe.wait_ge(S["xt_dve" if f % 2 else "xt_act"], (f - 4) // 2 + 1)
                    for k in range(4):
                        mm = T(PS[:, f % 4, k * P:(k + 1) * P], XROW[:, i % 2, (4 * kk + k) * P:(4 * kk + k + 1) * P],
                               ident)
                    mm.then_inc(S["xt_made"], 1)
            pe.wait_ge(S["small_in"], 16 * 9)
            for k in range(KT):
                mm = T(PS[:, 4, k * NS:(k + 1) * NS], XSROW[0:NS, k * P:(k + 1) * P], ident[0:NS, 0:NS])
            mm.then_inc(S["xt_made"], 1)
            T(PS[:, 5, 0:64], PRROW[0:64, :], ident[0:64, 0:64]).then_inc(S["xt_made"], 1)
            for k in range(8):
                mm = T(PS[:, 6, k * NS:(k + 1) * NS], NROW[0:NS, k * P:(k + 1) * P], ident[0:NS, 0:NS])
            mm.then_inc(S["xt_made"], 1)
            pe.wait_ge(S["npt_ready"], 1)
            norm_pe(pe, 0)

            project(pe, Tile(G0_BASE, 0), 0)
            pe.wait_ge(S["consts"], 32)
            pe.wait_ge(proj_read[0], 1)
            for x, c in enumerate((C0_SELI, C0_SELF)):
                for a in range(2):
                    mm = M(PS[0:4, 4 + 2 * x + a, 0:HALF], lhsT=c0[:, c:c + 4],
                           rhs=S0b["zt"][:, 0, a * HALF:(a + 1) * HALF], start=True, stop=True)
            mm.then_inc(S["g_sel"], 1)

            pe.wait_ge(S["g_rows"], 1)
            pe.wait_ge(S["sp_in"], 16)
            for k in range(8):
                mm = M(PS[:, 5, k * NS:(k + 1) * NS], lhsT=S0b["sp"][0:120, k * P:(k + 1) * P],
                       rhs=c0[0:120, C0_PSEL + (k // 2) * NS:C0_PSEL + (k // 2 + 1) * NS], start=True, stop=True)
            mm.then_inc(S["pl_ss"], 1)
            with pe.Fori(0, 4) as g:
                for j in range(3):
                    project(pe, Tile(P_BASE, j, g, 4))
                pe.wait_ge(proj_read[Tile(P_BASE, 1).p], Tile(P_BASE, 1, g, 4).m + 1)
                pe.wait_ge(S["pl_y"], 2 * g + 1)
                for j in range(2):
                    mm = T(PS[0:23, 4, j * P:(j + 1) * P], S0b["ub"][:, j, 16 + 497:16 + 520], ident)
                mm.then_inc(S["pl_T"], 1)
                project(pe, Tile(P_BASE, 3, g, 4))
                pe.wait_ge(S["wp_in"], (g + 1) * 16)
                pe.wait_ge(S["pl_ready"], g + 1)
                for d in range(2):
                    for a in range(2):
                        for c in range(2):
                            mm = M(PS[:, 4 + 2 * d + a, 0:HALF], lhsT=S0b["wp"][:, c, d * P:(d + 1) * P],
                                   rhs=S0b["pl"][:, c, a * HALF:(a + 1) * HALF], start=(c == 0), stop=(c == 1))
                mm.then_inc(S["pl_mm"], 1)

            pe.wait_ge(S["pl_y"], 8 + 1)
            for i in range(NT):
                mm = T(PS[:, 4, i * 4:(i + 1) * 4], AR[:, i * P:(i + 1) * P], ident[0:4, 0:4])
            mm.then_inc(S["g_acolT"], 1)

            qT, kT, vT, vr, kr, pt, cb = (S0[n] for n in ("qT", "kT", "vT", "vr", "kr", "pt", "cb"))
            with pe.Fori(0, 4) as h:
                for j in range(6):
                    project(pe, Tile(M_BASE, j, h, 10))
                t5 = Tile(M_BASE, 5, h, 10)
                pe.wait_ge(proj_read[t5.p], t5.m + 1)
                pe.wait_ge(S["g_acol"], 1)
                for x, src in enumerate((kT, vT)):
                    for i in range(NT):
                        for c in range(2):
                            at = (i % 2) * HD + c * P
                            mm = T(PS[:, 4 + 2 * x + i // 2, at:at + P], src[:, c, i * P:(i + 1) * P], ident)
                    mm.then_inc(S["m_rowT"], 1)
                for c in range(2):
                    mm = T(PS[0:NS, 0, c * P:(c + 1) * P], vT[:, c, TP:TA], ident)
                mm.then_inc(S["m_rowT"], 1)
                pe.wait_ge(S["c_in"], (h + 1) * (16 * NS))
                for j in range(2):
                    for b in range(NS):
                        for c in range(2):
                            M(PS[:, 1, j * 8 + b:j * 8 + b + 1], lhsT=cb[:, b, c * HD + j * P:c * HD + (j + 1) * P],
                              rhs=qT[:, c, TP + b:TP + b + 1], start=(c == 0), stop=(c == 1))
                pe.wait_ge(S["m_prod"], h + 1)
                for c in range(2):
                    mm = M(PS[:, 1, 16:32], lhsT=ones, rhs=S0["pr"][:, c], start=(c == 0), stop=(c == 1))
                mm.then_inc(S["m_dec"], 1)

                def scores(i):
                    if i == 0:
                        pe.wait_ge(S["m_kr"], h + 1)
                    if i >= 2:
                        pe.wait_ge(S["m_P"], 4 * h + (i - 1))
                    for c in range(2):
                        mm = M(PS[:, 4 + i % 2, 0:TP - i * P], lhsT=kT[:, c, i * P:(i + 1) * P],
                               rhs=qT[:, c, i * P:TP], start=(c == 0), stop=(c == 1))
                    mm.then_inc(S["m_S"], 1)
                scores(0)
                for i in range(NT):
                    if i < NT - 1:
                        scores(i + 1)
                    if i == 0:
                        pe.wait_ge(S["m_vr"], h + 1)
                        pe.wait_ge(S["m_vd"], h + 1)
                    pe.wait_ge(S["m_P"], 4 * h + (i + 1))
                    L = TP - i * P
                    for j in range(2):
                        M(PS[:, 6 + j, i * P:TP], lhsT=vr[:, i * HD + j * P:i * HD + (j + 1) * P], rhs=pt[:, i % 2, 0:L],
                          start=(i == 0), stop=(i == NT - 1))
                    mm = M(PS[:, 0, i * P:TP], lhsT=ones, rhs=pt[:, i % 2, 0:L], start=(i == 0), stop=(i == NT - 1))
                    mm.then_inc(S["m_PV"], 1)
                pe.wait_ge(S["m_kw"], h + 1)
                for c in range(2):
                    for i in range(NT):
                        M(PS[:, 4, c * HD:(c + 1) * HD], lhsT=kr[:, i * HD + c * P:i * HD + (c + 1) * P],
                          rhs=vr[:, i * HD:(i + 1) * HD], start=(i == 0), stop=(i == NT - 1))
                for i in range(NT):
                    mm = M(PS[0:1, 5, 0:HD], lhsT=ones[:, 0:1], rhs=kr[:, i * HD:(i + 1) * HD],
                           start=(i == 0), stop=(i == NT - 1))
                mm.then_inc(S["m_stT"], 1)

                project(pe, Tile(M_BASE, 6, h, 10))
                pe.wait_ge(S["m_y"], h + 1)
                pe.wait_ge(S["m_decr"], h + 1)
                project(pe, Tile(M_BASE, 7, h, 10))
                pe.wait_ge(S["m_nst"], h + 1)
                pe.wait_ge(S["m_nT"], h + 1)
                for c in range(2):
                    mm = T(PS[0:NS, 5, c * P:(c + 1) * P], S0["nTh"][:, c], ident)
                mm.then_inc(S["m_nr"], 1)
                for q, bank in enumerate((4, 6, 7, 5)):
                    if q == 3:
                        pe.wait_ge(S["m_nev"], h + 1)
                    for y in range(2):
                        b = 2 * q + y
                        mm = M(PS[:, bank, y * HD:(y + 1) * HD], lhsT=c0[0:NS, C0_OH8 + b * P:C0_OH8 + (b + 1) * P],
                               rhs=S0["vdr"][0:NS], start=True, stop=True)
                    mm.then_inc(S["m_vb"], 1)
                project(pe, Tile(M_BASE, 8, h, 10))
                pe.wait_ge(S["m_cn"], (h + 1) * (2 * NS))
                pe.wait_ge(S["m_sq"], 2 * h + 2)
                for a in range(2):
                    for j in range(2):
                        mm = M(PS[:, 4 + a, 0:HALF], lhsT=ones, rhs=qT[:, j, a * HALF:(a + 1) * HALF],
                               start=(j == 0), stop=(j == 1))
                mm.then_inc(S["m_ssq"], 1)
                project(pe, Tile(M_BASE, 9, h, 10))
                pe.wait_ge(S["m_var"], h + 1)

            out_pe(pe, 0, O0_BASE, KT)
            pe.wait_ge(S["m_var"], 4)
            norm_pe(pe, 1)
            project(pe, Tile(G1_BASE, 0), 2 * KT)
            pe.wait_ge(proj_read[1], (G1_BASE + 1) // 2)
            c1 = S1["c1"]
            for i in range(NT):
                mm = T(PS[:, 4, i * 48:(i + 1) * 48], XR[0:48, 0, i * P:(i + 1) * P], ident[0:48, 0:48])
            pe.wait_ge(S["g1_gd"], 1)
            mm = M(PS[:, 5, 0:3], lhsT=S1["gd"][0:48], rhs=c1[0:48, C1_GS:C1_GS + 3], start=True, stop=True)
            mm.then_inc(S["g1_T"], 1)

            kT, vr, qr, qt, pr, pt, dg, ptc = (S1[n] for n in ("kT", "vr", "qr", "qt", "pr", "pt", "dg", "ptc"))
            with pe.Fori(0, 4) as g:
                def rows(x):
                    src = (XR[:, 0], XR[:, 1], kT[:, 0], XR[:, 0], kT[:, 1], XR[:, 1])[x]
                    pe.wait_ge(S["a_src"], 6 * g + (x + 1))
                    if x < 2:
                        pe.wait_ge(S["g1_gw"], 1)
                    else:
                        pe.wait_ge(S["a_row"], 6 * g + (x - 1))
                    for i in range(NT):
                        T(PS[:, 4 + x % 2, i * P:(i + 1) * P], src[:, i * P:(i + 1) * P], ident)
                    T(PS[0:NS, 6 + x % 2, 0:P], src[:, TP:TA], ident).then_inc(S["a_rowT"], 1)

                for j in range(6):
                    project(pe, Tile(A_BASE, j, g, 14))
                    if j:
                        rows(j - 1)
                project(pe, Tile(A_BASE, 6, g, 14))
                rows(5)
                pe.wait_ge(S["a_row"], 6 * g + 5)
                T(PS[0:NB, 4, 0:P], S1["vcT"], ident).then_inc(S["a_vcm"], 1)
                for j in range(7, 10):
                    project(pe, Tile(A_BASE, j, g, 14))
                pe.wait_ge(S["a_rot"], 6 * g + 6)
                pe.wait_ge(S["a_row"], 6 * g + 6)
                for jj in range(QPK):
                    for i in range(NT):
                        at = (4 * jj + i) * NB
                        mm = M(PS[:, 7, at:at + NB], lhsT=qr[:, jj, i * P:(i + 1) * P], rhs=S1["kcb"],
                               start=True, stop=True)
                mm.then_inc(S["a_cs"], 1)

                def scores(n):
                    jj, i = n // 4, n % 4
                    if n >= 2:
                        pe.wait_ge(S["at_exp"], 16 * g + (n - 1))
                    for r in range(2):
                        mm = M(PS[:, 2 * (n % 2) + r, 0:(i + 1) * P], lhsT=qt[:, jj, i * P:(i + 1) * P],
                               rhs=kT[:, r, 0:(i + 1) * P], start=True, stop=True)
                    mm.then_inc(S["at_s"], 1)

                def cmp_turn(jj):
                    pe.wait_ge(S["a_cp"], g + 1)
                    if jj >= 1:
                        pe.wait_ge(S["a_ptc"], 4 * g + jj)
                    for i in range(NT):
                        mm = T(PS[0:NB, 7, i * P:(i + 1) * P], S1["sc"][:, 4 * jj + i], ident)
                    mm.then_inc(S["a_ctT"], 1)

                scores(0)
                scores(1)
                cmp_turn(0)
                for n in range(16):
                    jj, i = n // 4, n % 4
                    pe.wait_ge(S["at_diag"], 32 * g + (2 * n + 2))
                    for r in range(2):
                        for s in range(i + 1):
                            mm = M(PS[:, 4 + r, s * P:(s + 1) * P],
                                   lhsT=pr[:, 2 * (n % 2) + r, s * P:(s + 1) * P], rhs=dg[:, 2 * (n % 2) + r],
                                   start=True, stop=True)
                    mm.then_inc(S["at_T"], 1)
                    if n < 14:
                        scores(n + 2)
                    if i == 0:
                        pe.wait_ge(S["a_ptc"], 4 * g + (jj + 1))
                    if n:
                        pe.wait_ge(S["at_oe"], 16 * g + n)
                    M(PS[:, 6, 0:P], lhsT=S1["vcr"][0:NB], rhs=ptc[0:NB, jj % 2, i * P:(i + 1) * P],
                      start=True, stop=False)
                    pe.wait_ge(S["at_pta"], 16 * g + (n + 1))
                    for s in range(i + 1):
                        M(PS[:, 6, 0:P], lhsT=vr[:, 0, s * P:(s + 1) * P], rhs=pt[:, 0, s * P:(s + 1) * P],
                          start=False, stop=False)
                    pe.wait_ge(S["at_ptb"], 16 * g + (n + 1))
                    for s in range(i + 1):
                        mm = M(PS[:, 6, 0:P], lhsT=vr[:, 1, s * P:(s + 1) * P], rhs=pt[:, 1, s * P:(s + 1) * P],
                               start=False, stop=(s == i))
                    mm.then_inc(S["at_o"], 1)
                    if i == 2 and jj < 3:
                        cmp_turn(jj + 1)
                for j in range(10, 14):
                    project(pe, Tile(A_BASE, j, g, 14))
                pe.wait_ge(S["at_oe"], 16 * g + 16)

            KTB = S1["qt"]
            pe.wait_ge(S["d_z"], 1)
            pe.wait_ge(S["at_oe"], 64)
            pe.wait_ge(S["a_yz"], 16)

            def key_score(x):
                b, kind, g = x // 8, (x // 4) % 2, x % 4
                pe.wait_ge(S[f"d_kt{x % 2}"], x // 2 + 1)
                M(PS[32 * g:32 * g + 32, kind, :], lhsT=ZQ[:, 1, g, b], rhs=KTB[:, x % 2, 0:512],
                  start=(b == 0), stop=(b == NS - 1), skip_group_check=True).then_inc(S["d_ks"], 1)
            for b in range(NS):
                pe.wait_ge(S[f"d_in{b % 2}"], 144 * (b // 2 + 1))
                for kind in range(2):
                    for g in range(4):
                        x = b * 8 + kind * 4 + g
                        if x >= 2:
                            pe.wait_ge(S[f"d_kt{x % 2}"], x // 2)
                        for pg in range(NPG):
                            mm = T(PS[:, 4 + x % 2, pg * P:(pg + 1) * P],
                                   KV[:, b % 2, 1 + kind, pg, g * P:(g + 1) * P], ident)
                        mm.then_inc(S["d_kT"], 1)
                        if x:
                            key_score(x - 1)
                if b:
                    pe.wait_ge(S["d_km"], b)
                for g in range(4):
                    for pg in range(NPG):
                        at = g * NB + pg * 4
                        mm = M(PS[:, 6, at:at + 4], lhsT=KV[:, b % 2, 0, pg, g * P:(g + 1) * P],
                               rhs=c1[:, C1_AVG:C1_AVG + 4], start=True, stop=True)
                mm.then_inc(S["d_used"], 1)
                if b:
                    pass
                pe.wait_ge(S["d_km"], b + 1)
                for g in range(4):
                    mm = M(PS[32 * g:32 * g + 32, 2, 0:NB], lhsT=ZQ[:, 0, g, b], rhs=S1["pr"][:, 3, g * NB:(g + 1) * NB],
                           start=(b == 0), stop=(b == NS - 1), skip_group_check=True)
                mm.then_inc(S["d_cs"], 1)
            key_score(63)
            pe.wait_ge(S["d_prod"], 1)
            for r in range(2):
                mm = M(PS[:, 3, r:r + 1], lhsT=S1["qr"][:, r, 0:P], rhs=ones[:, 0:1], start=True, stop=True)
            mm.then_inc(S["d_snew"], 1)
            pe.wait_ge(S["d_diag"], 1)
            for kind in range(2):
                for pg in range(NPG):
                    mm = M(PS[:, 4 + kind, pg * P:(pg + 1) * P], lhsT=S1["pr"][:, 1 + kind, pg * P:(pg + 1) * P],
                           rhs=dg[:, 1 + kind], start=True, stop=True)
                mm.then_inc(S["d_pT"], 1)
            M(PS[0:NB, 6, 0:P], lhsT=S1["pr"][:, 0, 0:NB], rhs=dg[:, 0], start=True, stop=True).then_inc(S["d_pT"], 1)
            for kind in range(2):
                mm = M(PS[:, 3, P + kind * P:2 * P + kind * P], lhsT=S1["qt"][:, 2, kind * P:(kind + 1) * P],
                       rhs=dg[:, 1 + kind], start=True, stop=True)
            mm.then_inc(S["d_pT"], 1)
            pe.wait_ge(S["d_pc"], 1)
            for pg in range(NPG):
                mm = M(PS[:, 7, pg * P:(pg + 1) * P], lhsT=c1[0:NB, C1_EXP + pg * P:C1_EXP + (pg + 1) * P],
                       rhs=S1["pc"][0:NB], start=True, stop=True)
            mm.then_inc(S["d_pT"], 1)
            pe.wait_ge(S["d_ptd"], 2)
            pe.wait_ge(S["d_ptc"], 1)
            for b in range(NS):
                u = NS + b
                pe.wait_ge(S[f"d_in{u % 2}"], 144 * (u // 2 + 1))
                for g in range(4):
                    for kind in range(3):
                        for pg in range(NPG):
                            mm = M(PS[:, 0, 32 * g + b:32 * g + 32:8], lhsT=KV[:, u % 2, kind, pg, g * P:(g + 1) * P],
                                   rhs=PTD[:, kind, pg, 32 * g + b:32 * g + 32:8],
                                   start=(kind == 0 and pg == 0), stop=(kind == 2 and pg == NPG - 1))
                mm.then_inc(S["d_used"], 1)
            pe.wait_ge(S["d_y"], 1)
            out_pe(pe, 1, O1_BASE, 3 * KT)
            norm_pe(pe, 2)
            for f in range(20):
                i, kk = f // 4, f % 4
                if f == 0:
                    pe.wait_ge(S["fin_y"], KT)
                if f >= 4:
                    pe.wait_ge(S["fin_dve" if f % 2 else "fin_act"], (f - 4) // 2 + 1)
                for k in range(4):
                    if i < NT:
                        mm = T(PS[:, f % 4, k * P:(k + 1) * P], XY[:, 4 * kk + k, i * P:(i + 1) * P], ident)
                    else:
                        mm = T(PS[0:NS, f % 4, k * P:(k + 1) * P], XY[:, 4 * kk + k, TP:TA], ident)
                mm.then_inc(S["fin_T"], 1)

        @block.scalar
        def _(act):
            A = nc.scalar.activation
            own = Own(act, S, "act_step")
            for f in range(0, 16, 2):
                act.wait_ge(S["xt_made"], f + 1)
                A(XY[:, 4 * (f % 4):4 * (f % 4) + 4, (f // 4) * P:(f // 4 + 1) * P],
                  PS[:, f % 4, :].rearrange("p (k t) -> p k t", k=4), ACT.Copy).then_inc(S["xt_act"], 1); own.done("xt_act")
            split_hi(act, own, Tile(G0_BASE, 0))
            split_hi(act, own, Tile(P_BASE, 0))
            act.wait_ge(S["xt_act"], 8)
            act.wait_ge(S["xt_dve"], 9)
            norm_act(act, own, 0)
            h_act(act, own, 0)
            act.wait_ge(S["proj_done"], 1)
            act.wait_ge(S["npt_ready"], 1)
            A(halves(S0b["zt"][:, 0]), ps2(Tile(G0_BASE, 0)), ACT.Copy).then_inc(proj_read[0], 1); act.wait_ge(proj_read[0], 1)
            split_hi(act, own, Tile(P_BASE, 1))
            act.wait_ge(S["g_abs"], 1)
            A(T1R, T1R, ACT.Exp, scale=-1.0).then_inc(S["g_exp"], 1); own.done("g_exp")
            act.wait_ge(S["g_1p"], 1)
            A(T1R, T1R, ACT.Ln).then_inc(S["g_ln"], 1); own.done("g_ln")
            act.wait_ge(S["g_pre"], 1)
            A(MR[:, 512:1024], MR[:, 512:1024], ACT.Exp, scale=-1.0)
            A(MR[:, 1024:1048], MR[:, 1024:1048], ACT.Exp).then_inc(S["g_mr"], 1); own.done("g_mr")
            with own.turns(4, ACT_POOL) as g:
                for j in range(4):
                    t = Tile(P_BASE, j, g, 4)
                    act.wait_ge(S["proj_done"], t.n + 1)
                    if j == 0:
                        act.wait_ge(S["ub_zero"], 1)
                    if j == 2:
                        act.wait_ge(S["pl_y"], 2 * g + 1)
                        act.wait_ge(S["g_rows"], 1)
                    if j < 2:
                        A(halves(S0b["ub"][:, j, 16:536]), ps2(t), ACT.Copy).then_inc(proj_read[t.p], 1); act.wait_ge(proj_read[t.p], t.m + 1)
                    else:
                        A(halves(S0b["zt"][:, j - 2]), ps2(t), ACT.Silu).then_inc(proj_read[t.p], 1); act.wait_ge(proj_read[t.p], t.m + 1)
                    split_hi(act, own, t.ahead(2))
                act.wait_ge(S["pl_ready"], g + 1)
                act.wait_ge(S["pl_T"], g + 1)
            act.wait_ge(S["g_bc"], 64)
            act.wait_ge(S["pl_y"], 8 + 1)
            gbc = S0["gbc"]
            with own.turns(4, ACT_HEAD) as h:
                for j in range(6):
                    t = Tile(M_BASE, j, h, 10)
                    act.wait_ge(S["proj_done"], t.n + 1)
                    A(halves(S0[("qT", "kT", "vT")[j // 2]][:, j % 2]), ps2(t), ACT.Copy,
                      scale=(HD ** -0.5 if j // 2 == 1 else 1.0)).then_inc(proj_read[t.p], 1); act.wait_ge(proj_read[t.p], t.m + 1)
                    split_hi(act, own, t.ahead(2))
                act.wait_ge(S["m_wsin"], h + 1)
                A(S0["ws"], S0["ws"], ACT.Exp).then_inc(S["m_ws"], 1); own.done("m_ws")
                act.wait_ge(S["m_rowT"], 3 * h + 2)
                A(S0["vr"].rearrange("p (a b) -> p a b", a=2), PS[:, 6:8, :], ACT.Copy).then_inc(S["m_vr"], 1); own.done("m_vr")
                for i in range(NT):
                    act.wait_ge(S["m_dt"], 4 * h + (i + 1))
                    A(S0["dt"][:, i % 2, 0:TP - i * P], S0["dt"][:, i % 2, 0:TP - i * P], ACT.Exp, scale=-1.0
                      ).then_inc(S["m_D"], 1); own.done("m_D")
                act.wait_ge(S["m_PV"], 4 * h + 4)
                A(S0["ad"], PS[:, 0, :], ACT.Abs).then_inc(S["m_abs"], 1); own.done("m_abs")
                act.wait_ge(S["m_stT"], h + 1)
                A(S0["kr"][:, 0:512], PS[:, 4, :], ACT.Copy).then_inc(S["m_st"], 1); own.done("m_st")
                A(S0["nst"], PS[0:1, 5, 0:HD], ACT.Copy).then_inc(S["m_nst"], 1); own.done("m_nst")
                act.wait_ge(S["m_dec"], h + 1)
                for b in range(NS):
                    A(S0["cb"][:, b], S0["cb"][:, b], ACT.Copy, scale=gbc[:, h, 1024 + b:1025 + b]).then_inc(S["c_sc"], 1); own.done("c_sc")
                act.wait_ge(S["m_decr"], h + 1)
                for j in range(2):
                    t = Tile(M_BASE, 6 + j, h, 10)
                    act.wait_ge(S["proj_done"], t.n + 1)
                    A(halves(S0["vT"][:, j]), ps2(t), ACT.Sigmoid).then_inc(proj_read[t.p], 1); act.wait_ge(proj_read[t.p], t.m + 1)
                    split_hi(act, own, t.ahead(2))
                for j in range(2):
                    act.wait_ge(S["m_oy"], 2 * h + j + 1)
                    A(S0["qT"][:, j], XY[:, 8 + 2 * h + j, :], ACT.Square).then_inc(S["m_sq"], 1); own.done("m_sq")
                t = Tile(M_BASE, 8, h, 10)
                act.wait_ge(S["proj_done"], t.n + 1)
                A(halves(S0["kT"][:, 0]), ps2(t), ACT.Silu).then_inc(proj_read[t.p], 1); act.wait_ge(proj_read[t.p], t.m + 1)
                split_hi(act, own, t.ahead(2))
                act.wait_ge(S["m_var"], h + 1)
                A(RS[:], RS[:], ACT.Sqrt).then_inc(S["m_sqrt"], 1); own.done("m_sqrt")
                t = Tile(M_BASE, 9, h, 10)
                act.wait_ge(S["proj_done"], t.n + 1)
                A(halves(S0["kT"][:, 1]), ps2(t), ACT.Silu).then_inc(proj_read[t.p], 1); act.wait_ge(proj_read[t.p], t.m + 1)
                split_hi(act, own, t.ahead(2))
                act.wait_ge(S["m_yz"], 2 * h + 2)
            act.wait_ge(S["m_yz"], 8)
            y_split_act(act, own, 0, O0_BASE)
            out_act(act, own, 0, O0_BASE)
            act.wait_ge(proj_read[0], (G1_BASE + 1) // 2)
            act.wait_ge(proj_read[1], G1_BASE // 2)
            norm_act(act, own, 1)
            h_act(act, own, 1)
            t = Tile(G1_BASE, 0)
            act.wait_ge(S["proj_done"], t.n + 1)
            act.wait_ge(S["consts"], 16 * 5)
            act.wait_ge(S["h_ready"], 3 * KT)
            A(halves(XR[0:48, 0]), ps2(t, slice(0, 48)), ACT.Sigmoid, bias=S1["bg"][0:48, 0:1]).then_inc(proj_read[t.p], 1); act.wait_ge(proj_read[t.p], t.m + 1)
            split_hi(act, own, t.ahead(2))

            kT, qr, qt, pr, pt, vr, rs, rd = (S1[n] for n in ("kT", "qr", "qt", "pr", "pt", "vr", "rs", "rd"))
            with own.turns(4, ACT_GROUP) as g:
                def rows(x):
                    dst = vr[:, x // 4] if x in (3, 5) else rs[:, (0, 1, 2, None, 3)[x]]
                    act.wait_ge(S["a_rowT"], 6 * g + (x + 1))
                    A(dst, PS[:, 4 + x % 2, :], ACT.Copy)
                    A(rd[0:NS, x], PS[0:NS, 6 + x % 2, 0:P], ACT.Copy).then_inc(S["a_row"], 1); own.done("a_row")

                for j in range(10):
                    t = Tile(A_BASE, j, g, 14)
                    act.wait_ge(S["proj_done"], t.n + 1)
                    if j in (0, 1, 3, 5):
                        if j == 0:
                            act.wait_ge(S["g1_T"], 1)
                        if j in (3, 5):
                            act.wait_ge(S["a_src"], 6 * g + (j // 2))
                            act.wait_ge(S["a_rowT"], 6 * g + (j // 2))
                        A(halves(XR[:, (0, 1, None, 0, None, 1)[j]]), ps2(t), ACT.Copy).then_inc(proj_read[t.p], 1); act.wait_ge(proj_read[t.p], t.m + 1)
                    else:
                        r = (None, None, 0, None, 1, None, 2, 3, 4, 5)[j]
                        if r:
                            act.wait_ge(S["a_rot"], 6 * g + r)
                        if j >= 6:
                            A(halves(qr[:, j - 6]), ps2(t), ACT.Copy)
                        A(halves(RS[0:64]), ps2(t, slice(64, 128)), ACT.Copy)
                        A(halves(RS[64:128]), ps2(t, slice(0, 64)), ACT.Copy).then_inc(S["a_sw"], 1); own.done("a_sw")
                    split_hi(act, own, t.ahead(2))
                    if 1 <= j <= 6:
                        rows(j - 1)
                act.wait_ge(S["a_cin"], g + 1)
                A(S1["sc"], S1["sc"], ACT.Exp).then_inc(S["a_cexp"], 1); own.done("a_cexp")

                def expo(n):
                    act.wait_ge(S["at_nm"], 16 * g + (n + 1))
                    L = (n % 4 + 1) * P
                    for r in range(2):
                        ins = A(pr[:, 2 * (n % 2) + r, 0:L], PS[:, 2 * (n % 2) + r, 0:L], ACT.Exp,
                                bias=S1["st"][:, 4 + n % 2, r:r + 1], scale=SCALE,
                                accum_out=S1["st"][:, n % 2, r:r + 1])
                    ins.then_inc(S["at_exp"], 1); own.done("at_exp")
                expo(0)
                expo(1)
                for n in range(16):
                    L = (n % 4 + 1) * P
                    act.wait_ge(S["at_T"], 16 * g + (n + 1))
                    if n:
                        act.wait_ge(S["at_o"], 16 * g + n)
                    A(pt[:, 0, 0:L], PS[:, 4, 0:L], ACT.Copy).then_inc(S["at_pta"], 1); own.done("at_pta")
                    if n < 14:
                        expo(n + 2)
                for j in range(4):
                    t = Tile(A_BASE, 10 + j, g, 14)
                    act.wait_ge(S["proj_done"], t.n + 1)
                    act.wait_ge(S["a_src"], 6 * g + 6)
                    if j >= 2:
                        act.wait_ge(S["a_yz"], 4 * g + (j - 1))
                    A(halves(XR[:, j % 2]), ps2(t), ACT.Silu).then_inc(proj_read[t.p], 1); act.wait_ge(proj_read[t.p], t.m + 1)
                    split_hi(act, own, t.ahead(2))
                act.wait_ge(S["a_yz"], 4 * g + 4)
                act.wait_ge(S["row_out"], 192 * g + 192)
                act.wait_ge(S["at_o"], 16 * g + 16)
                act.wait_ge(S["a_qd"], g + 1)

            for x in range(0, 64, 2):
                act.wait_ge(S["d_kT"], x + 1)
                if x >= 2:
                    act.wait_ge(S["d_ks"], x - 1)
                else:
                    act.wait_ge(S["a_yz"], 16)
                    act.wait_ge(S["d_z"], 1)
                A(S1["qt"][:, 0, 0:512], PS[:, 4, :], ACT.Copy).then_inc(S["d_kt0"], 1); own.done("d_kt0")
            act.wait_ge(S["d_nm"], 1)
            for k, (bank, L) in enumerate(((2, NB), (0, 512), (1, 512))):
                ins = A(pr[:, k, 0:L], PS[:, bank, 0:L], ACT.Exp, bias=S1["dst"][:, 1, k:k + 1], scale=SCALE,
                        accum_out=S1["dst"][:, 2, k:k + 1])
            ins = A(S1["dst"][:, 5, 0:1], PS[:, 3, 0:1], ACT.Exp, bias=S1["dst"][:, 1, 1:2], scale=SCALE)
            A(S1["dst"][:, 5, 1:2], PS[:, 3, 1:2], ACT.Exp, bias=S1["dst"][:, 1, 2:3], scale=SCALE
              ).then_inc(S["d_exp"], 1); own.done("d_exp")
            act.wait_ge(S["d_pT"], 5)
            act.wait_ge(S["d_pc"], 1)
            A(PTD[:, 0].rearrange("p a r -> p (a r)"), PS[:, 7, :], ACT.Copy).then_inc(S["d_ptc"], 1); own.done("d_ptc")
            act.wait_ge(S["d_y"], 1)
            act.wait_ge(S["win_out"], 64 * NS)
            y_split_act(act, own, 1, O1_BASE)
            out_act(act, own, 1, O1_BASE)
            act.wait_ge(proj_read[0], N_TILES // 2)
            act.wait_ge(proj_read[1], N_TILES // 2)
            norm_act(act, own, 2)
            for f in range(0, 20, 2):
                i, kk = f // 4, f % 4
                act.wait_ge(S["fin_T"], f + 1)
                if f == 0:
                    act.wait_ge(S["proj_done"], N_TILES)
                q = slice(0, P if i < NT else NS)
                dst = YROW[:, i] if i < NT else YSROW
                A(dst[q, kk * 512:(kk + 1) * 512], PS[q, f % 4, :], ACT.Copy).then_inc(S["fin_act"], 1); own.done("fin_act")

        @block.vector
        def _(dve):
            V = nc.vector
            own = Own(dve, S, "dve_step")
            step = own.step
            dve.sem_inc(S["pl_y"], 1)
            own.done("pl_y")
            TT, TS, STT, CP = V.tensor_tensor, V.tensor_scalar, V.scalar_tensor_tensor, V.tensor_copy

            def CPR(out, in_):
                return TS(out, in_, 1.0, None, ALU.mult)
            for f in range(1, 16, 2):
                dve.wait_ge(S["xt_made"], f + 1)
                CP(XY[:, 4 * (f % 4):4 * (f % 4) + 4, (f // 4) * P:(f // 4 + 1) * P],
                   PS[:, f % 4, :].rearrange("p (k t) -> p k t", k=4)).then_inc(S["xt_dve"], 1); own.done("xt_dve")
            dve.wait_ge(S["xt_made"], 17)
            CP(XY[:, :, TP:TA], PS[:, 4, 0:KT * NS].rearrange("p (k b) -> p k b", b=NS)).then_inc(S["xt_dve"], 1); own.done("xt_dve")
            dve.wait_ge(S["xt_made"], 19)
            step(CP(PR[:], PS[:, 5, 0:64]))
            CP(S0["nT"], PS[:, 6, 0:64].rearrange("p (k b) -> p k b", b=NS)).then_inc(S["npt_ready"], 1); own.done("npt_ready")
            dve.wait_ge(S["npt_ready"], 1)
            dve.wait_ge(S["xt_act"], 8)
            dve.wait_ge(S["xt_dve"], 9)
            split_lo(dve, own, Tile(G0_BASE, 0))
            split_lo(dve, own, Tile(P_BASE, 0))
            step(V.memset(S0b["ub"][:, :, 0:16], 0.0))
            V.memset(GONE, 1.0).then_inc(S["ub_zero"], 1); own.done("ub_zero")
            norm_dve(dve, own, 0)
            h_dve(dve, own, 0, R_G0)
            dve.wait_ge(S["g_sel"], 1)
            dve.wait_ge(S["ub_zero"], 1)
            bg = S0["bg"]
            TS(halves(IGR), ps_pair(4, slice(0, 4)), bg[0:4, 0:1], None, ALU.add)
            TS(halves(FGR), ps_pair(6, slice(0, 4)), bg[0:4, 1:2], None, ALU.add).then_inc(S["g_rows"], 1); own.done("g_rows")
            dve.wait_ge(S["g_rows"], 1)
            split_lo(dve, own, Tile(P_BASE, 1))
            step(TS(LFR, FGR, -1.0, None, ALU.mult))
            TT(T1R, FGR, LFR, ALU.max).then_inc(S["g_abs"], 1); own.done("g_abs")
            dve.wait_ge(S["g_exp"], 1)
            TS(T1R, T1R, 1.0, None, ALU.add).then_inc(S["g_1p"], 1); own.done("g_1p")
            dve.wait_ge(S["g_ln"], 1)
            step(STT(LFR, FGR, 0.0, T1R, ALU.min, ALU.subtract))
            step(V.tensor_tensor_scan(BR, GONE, LFR[:, 0:TP], 0.0, ALU.mult, ALU.add))
            step(TT(AR, IGR[:, 0:TP], BR, ALU.subtract))
            step(V.tensor_tensor_scan(MR[:, 0:TP], AR, AR, 0.0, ALU.max, ALU.max))
            step(TT(MR[:, TP:2 * TP], BR, MR[:, 0:TP], ALU.add))
            step(CP(GD[:, 32:33], MR[:, 2 * TP - 1:2 * TP]))
            step(TT(GD[:, 8:16], LFR[:, TP:TA], GM0, ALU.add))
            step(TT(GD[:, 0:8], GD[:, 8:16], IGR[:, TP:TA], ALU.max))
            TT(MR[:, 1024:1032], GD[:, 8:16], GD[:, 0:8], ALU.subtract)
            TT(MR[:, 1032:1040], IGR[:, TP:TA], GD[:, 0:8], ALU.subtract)
            TS(MR[:, 1040:1048], GD[:, 0:8], -1.0, None, ALU.mult).then_inc(S["g_pre"], 1); own.done("g_pre")
            dve.wait_ge(S["pl_ss"], 1)
            step(CP(S0b["ss"], PS[:, 5, 0:64].rearrange("p (k b) -> p k b", b=NS)))
            dve.wait_ge(S["x_saved"], 16)
            ub, sa, sb_, pl, zt, us = (S0b[n] for n in ("ub", "sa", "sb", "pl", "zt", "us"))
            for g in range(4):
                t0 = Tile(P_BASE, 4 * g)
                w = 2 ** (g + 1)
                split_lo(dve, own, Tile(P_BASE, 4 * g).ahead(2))
                split_lo(dve, own, Tile(P_BASE, 4 * g + 1).ahead(2))
                t1 = Tile(P_BASE, 4 * g + 1)
                dve.wait_ge(proj_read[t1.p], t1.m + 1)
                if g:
                    dve.wait_ge(S["pl_mm"], g)
                src, dst = ub, sa
                for lvl in range(g + 1):
                    lo, sh = 2 ** (lvl + 1) - 1, 2 ** lvl
                    step(TT(dst[:, :, lo:528], src[:, :, lo:528], src[:, :, lo - sh:528 - sh], ALU.add))
                    src, dst = dst, (sb_ if dst is sa else sa)
                step(STT(pl[:, :, 0:TP], src[:, :, 16:528], 1.0 / w, ub[:, :, 16:528], ALU.mult, ALU.subtract))
                ic = S0["c0"][:, C0_ICNT + g * 16:C0_ICNT + g * 16 + w]
                for j in range(2):
                    step(TT(dst[:, j, 0:w], src[:, j, 16:16 + w], ic, ALU.mult))
                step(TT(pl[:, :, 0:w], dst[:, :, 0:w], ub[:, :, 16:16 + w], ALU.subtract))
                split_lo(dve, own, Tile(P_BASE, 4 * g + 2).ahead(2))
                dve.wait_ge(S["pl_T"], g + 1)
                step(TT(us, S0b["ss"][:, 2 * g:2 * g + 2], ub[:, :, 528:536], ALU.add))
                step(CP(S0b["tail"][0:23, g * 256:(g + 1) * 256], PS[0:23, 4, 0:256]))
                STT(pl[:, :, TP:TA], us, 1.0 / w, ub[:, :, 528:536], ALU.mult, ALU.subtract
                    ).then_inc(S["pl_ready"], 1); own.done("pl_ready")
                split_lo(dve, own, Tile(P_BASE, 4 * g + 3).ahead(2))
                dve.wait_ge(S["pl_mm"], g + 1)
                t3 = Tile(P_BASE, 4 * g + 3)
                dve.wait_ge(proj_read[t3.p], t3.m + 1)
                for d in range(2):
                    STT(halves(XY[:, 2 * g + d]), ps_pair(4 + 2 * d), PR[:, R_PS + 2 * g + d:R_PS + 2 * g + d + 1],
                        halves(zt[:, d]), ALU.mult, ALU.mult).then_inc(S["pl_y"], 1); own.done("pl_y")
            dve.wait_ge(S["g_acolT"], 1)
            CP(S0["acol"].rearrange("p (h i) -> p i h", i=NT), PS[:, 4, 0:16].rearrange("p (i h) -> p i h", h=4)
               ).then_inc(S["g_acol"], 1); own.done("g_acol")
            dve.wait_ge(S["g_acol"], 1)
            dve.wait_ge(S["g_bc"], 64)

            qT, kT, vT, kr, pt, dt, gbc, acol = (S0[n] for n in ("qT", "kT", "vT", "kr", "pt", "dt", "gbc", "acol"))
            PD, DT, KDW, cb = S0["pr"], S0["dtmp"], S0["kdw"], S0["cb"]
            with own.turns(4, DVE_HEAD) as h:
                for j in range(6):
                    split_lo(dve, own, Tile(M_BASE, j, h, 10).ahead(2))
                t5 = Tile(M_BASE, 5, h, 10)
                dve.wait_ge(proj_read[t5.p], t5.m + 1)
                TS(S0["ws"], acol[:, bass.ds(4 * h, 4)], gbc[:, h, 511:512], None, ALU.subtract).then_inc(S["m_wsin"], 1); own.done("m_wsin")
                nTh = S0["nT"][:, bass.ds(2 * h, 2), :]
                TT(PD[:, :, 0:8], qT[:, :, TP:TA], kT[:, :, TP:TA], ALU.mult)
                TT(PD[:, :, 8:16], qT[:, :, TP:TA], nTh, ALU.mult).then_inc(S["m_prod"], 1); own.done("m_prod")

                def decay(i):
                    L = TP - i * P
                    TS(dt[:, i % 2, 0:L], gbc[:, h, i * P:TP], acol[:, bass.ds(4 * h + i, 1)], 0.0,
                       ALU.subtract, ALU.max).then_inc(S["m_dt"], 1); own.done("m_dt")
                decay(0)
                decay(1)
                dve.wait_ge(S["m_rowT"], 3 * h + 1)
                CP(kr.rearrange("p (a b) -> p a b", a=2), PS[:, 4:6, :]).then_inc(S["m_kr"], 1); own.done("m_kr")
                dve.wait_ge(S["m_rowT"], 3 * h + 3)
                CP(S0["vdr"][0:NS], PS[0:NS, 0, 0:HD]).then_inc(S["m_vd"], 1); own.done("m_vd")
                for i in range(NT):
                    L = TP - i * P
                    dve.wait_ge(S["m_D"], 4 * h + (i + 1))
                    dve.wait_ge(S["m_S"], 4 * h + (i + 1))
                    if i >= 2:
                        dve.wait_ge(S["m_PV"], 4 * h + (i - 1))
                    step(TT(pt[:, i % 2, 0:L], PS[:, 4 + i % 2, 0:L], dt[:, i % 2, 0:L], ALU.mult))
                    TT(pt[:, i % 2, 0:P], pt[:, i % 2, 0:P], S0["c0"][:, C0_MASKT:C0_MASKT + P], ALU.mult
                       ).then_inc(S["m_P"], 1); own.done("m_P")
                    if i < 2:
                        decay(i + 2)
                dve.wait_ge(S["m_ws"], h + 1)
                dve.wait_ge(S["m_kr"], h + 1)
                for i in range(NT):
                    ins = TS(kr[:, i * HD:(i + 1) * HD], kr[:, i * HD:(i + 1) * HD], S0["ws"][:, i:i + 1], None, ALU.mult)
                ins.then_inc(S["m_kw"], 1); own.done("m_kw")
                dve.wait_ge(S["m_dec"], h + 1)
                iw, dw, fl = (gbc[:, h, 1024 + 8 * x:1032 + 8 * x] for x in range(3))
                TT(DT[:, 0], PS[:, 1, 16:24], dw, ALU.mult)
                TT(DT[:, 1], PS[:, 1, 24:32], iw, ALU.mult)
                TT(DT[:, 4], PS[:, 1, 0:8], iw, ALU.mult)
                TT(DT[:, 5], PS[:, 1, 8:16], iw, ALU.mult)
                TT(KDW[:, 0], kT[:, 0, TP:TA], dw, ALU.mult)
                TT(KDW[:, 1], kT[:, 1, TP:TA], dw, ALU.mult)
                TT(nTh[:, 0], nTh[:, 0], iw, ALU.mult)
                step(TT(nTh[:, 1], nTh[:, 1], iw, ALU.mult))
                TT(DT[:, 1], DT[:, 1], DT[:, 0], ALU.add)
                TT(DT[:, 6], vT[:, 0, TP:TA], DT[:, 0], ALU.mult)
                TT(DT[:, 7], vT[:, 1, TP:TA], DT[:, 0], ALU.mult)
                step(TT(nTh, nTh, KDW, ALU.add))
                CPR(S0["nTh"], nTh).then_inc(S["m_nT"], 1); own.done("m_nT")
                TT(DT[:, 4:6], DT[:, 4:6], DT[:, 6:8], ALU.add)
                step(TS(DT[:, 2], DT[:, 1], -1.0, None, ALU.mult))
                step(TT(DT[:, 1], DT[:, 1], DT[:, 2], ALU.max))
                step(TT(DT[:, 1], DT[:, 1], fl, ALU.max))
                step(V.reciprocal(DT[:, 1], DT[:, 1]))
                TT(XY[:, bass.ds(8 + 2 * h, 1), TP:TA], DT[:, 4:5], DT[:, 1:2], ALU.mult)
                TT(XY[:, bass.ds(9 + 2 * h, 1), TP:TA], DT[:, 5:6], DT[:, 1:2], ALU.mult).then_inc(S["m_decr"], 1); own.done("m_decr")
                dve.wait_ge(S["m_abs"], h + 1)
                step(TT(S0["ad"], S0["ad"], gbc[:, h, TP:2 * TP], ALU.max))
                step(V.reciprocal(S0["ad"], S0["ad"]))
                for j in range(2):
                    ins = TT(XY[:, bass.ds(8 + 2 * h + j, 1), 0:TP], PS[:, 6 + j:7 + j, :],
                             S0["ad"].rearrange("p (o t) -> p o t", o=1), ALU.mult)
                ins.then_inc(S["m_y"], 1); own.done("m_y")
                dve.wait_ge(S["m_y"], h + 1)
                dve.wait_ge(S["m_decr"], h + 1)
                for j in range(2):
                    t = Tile(M_BASE, 6 + j, h, 10)
                    dve.wait_ge(proj_read[t.p], t.m + 1)
                    y = XY[:, bass.ds(8 + 2 * h + j, 1), :]
                    TT(y, y, vT[:, j:j + 1], ALU.mult).then_inc(S["m_oy"], 1); own.done("m_oy")
                    split_lo(dve, own, t.ahead(2))
                dve.wait_ge(S["m_nr"], h + 1)
                CP(S0["nor"], PS[0:NS, 5, 0:HD]).then_inc(S["m_nev"], 1); own.done("m_nev")
                dve.wait_ge(S["c_sc"], 8 * h + 8)
                for q, bank in enumerate((4, 6, 7, 5)):
                    dve.wait_ge(S["m_vb"], 4 * h + (q + 1))
                    for y in range(2):
                        b = 2 * q + y
                        for c in range(2):
                            STT(cb[:, b, c * HD:(c + 1) * HD], PS[:, bank, y * HD:(y + 1) * HD], KDW[:, c, b:b + 1],
                                cb[:, b, c * HD:(c + 1) * HD], ALU.mult, ALU.add).then_inc(S["m_cn"], 1); own.done("m_cn")
                split_lo(dve, own, Tile(M_BASE, 8, h, 10).ahead(2))
                dve.wait_ge(S["m_ssq"], h + 1)
                TS(halves(RS[:]), ps_pair(4), 1.0 / HD, EPS, ALU.mult, ALU.add).then_inc(S["m_var"], 1); own.done("m_var")
                dve.wait_ge(S["m_sqrt"], h + 1)
                step(V.reciprocal(RS[:], RS[:]))
                for j in range(2):
                    y = XY[:, bass.ds(8 + 2 * h + j, 1), :]
                    ins = STT(y, y, PR[:, bass.ds(R_MH + 2 * h + j, 1)], RS[:].rearrange("p (o t) -> p o t", o=1),
                              ALU.mult, ALU.mult)
                step(ins)
                split_lo(dve, own, Tile(M_BASE, 9, h, 10).ahead(2))
                t9 = Tile(M_BASE, 9, h, 10)
                dve.wait_ge(proj_read[t9.p], t9.m + 1)
                for j in range(2):
                    y = XY[:, bass.ds(8 + 2 * h + j, 1), :]
                    TT(y, y, kT[:, j:j + 1], ALU.mult).then_inc(S["m_yz"], 1); own.done("m_yz")
                dve.wait_ge(S["st_out"], 32 * h + 32)
                dve.wait_ge(S["n_out"], 16 * h + 16)

            dve.wait_ge(S["m_yz"], 8)
            y_split_dve(dve, own, 0)
            out_dve(dve, own, 0, O0_BASE)
            dve.wait_ge(proj_read[0], (G1_BASE + 1) // 2)
            dve.wait_ge(proj_read[1], G1_BASE // 2)
            norm_dve(dve, own, 1)
            h_dve(dve, own, 1, R_G1)
            dve.wait_ge(S["consts"], 16 * 5)
            dve.wait_ge(S["x_saved"], 32)
            dve.wait_ge(proj_read[1], (G1_BASE + 1) // 2)
            c1 = S1["c1"]
            TT(S1["gd"][0:48].rearrange("p (h b) -> p h b", b=NS),
               XR[0:48, 0, TP:TA].rearrange("p (o b) -> p o b", o=1).broadcast_to([48, NH, NS]),
               c1[0:48, C1_GM:C1_GM + P].rearrange("p (h b) -> p h b", b=NS), ALU.mult).then_inc(S["g1_gd"], 1); own.done("g1_gd")
            dve.wait_ge(S["g1_gd"], 1)
            split_lo(dve, own, Tile(G1_BASE, 0).ahead(2))
            dve.wait_ge(S["g1_T"], 1)
            CP(S1["gw"].rearrange("p c i -> p i c"), PS[:, 4, 0:192].rearrange("p (i c) -> p i c", i=NT))
            CP(S1["gdr"][:, 0:3], PS[:, 5, 0:3]).then_inc(S["g1_gw"], 1); own.done("g1_gw")
            dve.wait_ge(S["g1_gw"], 1)

            kT, qr, qt, pr, pt, st, sc, cst, dg, kd, qd = (
                S1[n] for n in ("kT", "qr", "qt", "pr", "pt", "st", "sc", "cst", "dg", "kd", "qd"))
            with own.turns(4, DVE_GROUP) as g:
                for j in range(10):
                    t = Tile(A_BASE, j, g, 14)
                    if j in (0, 1, 3, 5):
                        dve.wait_ge(proj_read[t.p], t.m + 1)
                        if j == 0:
                            step(V.tensor_reduce(S1["kcb"], XR[:, 0, 0:TP].rearrange("p (n t) -> p n t", t=32), AX, ALU.add))
                            TS(S1["kcb"], S1["kcb"], 1.0 / 32, None, ALU.mult).then_inc(S["a_src"], 1); own.done("a_src")
                        elif j == 1:
                            step(V.tensor_reduce(S1["vcT"], XR[:, 1, 0:TP].rearrange("p (n t) -> p n t", t=32), AX, ALU.add))
                            TS(S1["vcT"], S1["vcT"], 1.0 / 32, None, ALU.mult).then_inc(S["a_src"], 1); own.done("a_src")
                        else:
                            CPR(kd[:, 1 + (j - 1) // 2, bass.ds(g, 1), :], XR[:, j // 4:j // 4 + 1, TP:TA]
                               ).then_inc(S["a_src"], 1); own.done("a_src")
                    else:
                        r = (None, None, 0, None, 1, None, 2, 3, 4, 5)[j]
                        dst = kT[:, r] if r < 2 else qt[:, r - 2]
                        dve.wait_ge(S["a_sw"], 6 * g + (r + 1))
                        TT(halves(dst), ps2(t), halves(cosT), ALU.mult).then_inc(proj_read[t.p], 1); dve.wait_ge(proj_read[t.p], t.m + 1)
                        step(TT(RS[:], RS[:], sinT, ALU.mult))
                        dve.wait_ge(proj_read[t.p], t.m + 1)
                        TT(dst, dst, RS[:], ALU.add).then_inc(S["a_rot"], 1); own.done("a_rot")
                        dve.wait_ge(S["a_rot"], 6 * g + (r + 1))
                        if r < 2:
                            CPR(kd[:, 2 * r, bass.ds(g, 1), :], kT[:, r:r + 1, TP:TA]).then_inc(S["a_src"], 1); own.done("a_src")
                    split_lo(dve, own, t.ahead(2))
                    if j == 7:
                        dve.wait_ge(S["a_vcm"], g + 1)
                        CP(S1["vcr"][0:NB], PS[0:NB, 4, 0:P]).then_inc(S["a_vcr"], 1); own.done("a_vcr")
                CPR(qd[:, 0, bass.ds(32 * g, 32)].rearrange("p (h b) -> p h b", b=NS), qr[:, :, TP:TA])
                CPR(qd[:, 1, bass.ds(32 * g, 32)].rearrange("p (h b) -> p h b", b=NS), qt[:, :, TP:TA]
                   ).then_inc(S["a_qd"], 1); own.done("a_qd")

                dve.wait_ge(S["a_cs"], g + 1)
                for jj in range(QPK):
                    ins = TT(sc[:, 4 * jj:4 * jj + 4], PS[:, 7, jj * 64:(jj + 1) * 64].rearrange("p (i n) -> p i n", n=NB),
                             c1[:, C1_CMP:C1_CMP + 64].rearrange("p (i n) -> p i n", n=NB), ALU.add)
                step(ins)
                step(V.tensor_reduce(cst[:, 0], sc, AX, ALU.max))
                step(TS(cst[:, 1], cst[:, 0], -SCALE, 1.0e20, ALU.mult, ALU.min))
                STT(sc, sc, SCALE, cst[:, 1].rearrange("p (n o) -> p n o", o=1).broadcast_to([P, 16, NB]),
                    ALU.mult, ALU.add).then_inc(S["a_cin"], 1); own.done("a_cin")

                def maxima(n):
                    i = n % 4
                    dve.wait_ge(S["at_s"], 16 * g + (n + 1))
                    for r in range(2):
                        blk = PS[:, 2 * (n % 2) + r, i * P:(i + 1) * P]
                        ins = TT(blk, blk, c1[:, C1_NEG:C1_NEG + P], ALU.add)
                    step(ins)
                    step(V.tensor_reduce(st[:, 2 + n % 2], PS[:, 2 * (n % 2):2 * (n % 2) + 2, 0:(i + 1) * P], AX, ALU.max))
                    TS(st[:, 4 + n % 2], st[:, 2 + n % 2], -SCALE, None, ALU.mult).then_inc(S["at_nm"], 1); own.done("at_nm")

                def diagonal(n):
                    jj, i = n // 4, n % 4
                    dve.wait_ge(S["at_exp"], 16 * g + (n + 1))
                    if n >= 2:
                        dve.wait_ge(S["at_T"], 16 * g + (n - 1))
                    step(V.reciprocal(st[:, n % 2], st[:, n % 2]))
                    for r in range(2):
                        TS(dg[:, 2 * (n % 2) + r], ident, st[:, n % 2, r:r + 1],
                           S1["gw"][:, bass.ds(12 * g + (3 * jj + 1 + r), 1), i:i + 1].rearrange("p a b -> p (a b)"),
                           ALU.mult, ALU.mult).then_inc(S["at_diag"], 1); own.done("at_diag")

                maxima(0)
                maxima(1)
                dve.wait_ge(S["a_cexp"], g + 1)
                step(V.tensor_reduce(cst[:, 2], sc, AX, ALU.add))
                step(TS(cst[:, 2], cst[:, 2], 1e-30, None, ALU.max))
                step(V.reciprocal(cst[:, 2], cst[:, 2]))
                for jj in range(QPK):
                    ins = TT(cst[:, 3:4, 4 * jj:4 * jj + 4], cst[:, 2:3, 4 * jj:4 * jj + 4],
                             S1["gw"][:, bass.ds(12 * g + 3 * jj, 1), :], ALU.mult)
                step(ins)
                TT(sc, sc, cst[:, 3].rearrange("p (n o) -> p n o", o=1).broadcast_to([P, 16, NB]), ALU.mult
                   ).then_inc(S["a_cp"], 1); own.done("a_cp")
                diagonal(0)
                dve.wait_ge(S["a_vcr"], g + 1)

                def cmp_rows(jj):
                    dve.wait_ge(S["a_ctT"], 4 * g + (jj + 1))
                    CP(S1["ptc"][0:NB, jj % 2], PS[0:NB, 7, :]).then_inc(S["a_ptc"], 1); own.done("a_ptc")
                cmp_rows(0)
                for n in range(16):
                    jj, i = n // 4, n % 4
                    L = (i + 1) * P
                    dve.wait_ge(S["at_T"], 16 * g + (n + 1))
                    if n:
                        dve.wait_ge(S["at_o"], 16 * g + n)
                    CP(pt[:, 1, 0:L], PS[:, 5, 0:L]).then_inc(S["at_ptb"], 1); own.done("at_ptb")
                    if n < 14:
                        maxima(n + 2)
                    if n < 15:
                        diagonal(n + 1)
                    dve.wait_ge(S["at_o"], 16 * g + (n + 1))
                    CPR(XY[:, bass.ds(4 * g + jj, 1), i * P:(i + 1) * P], PS[:, 6:7, 0:P]).then_inc(S["at_oe"], 1); own.done("at_oe")
                    if i == 2 and jj < 3:
                        cmp_rows(jj + 1)
                dve.wait_ge(S["at_oe"], 16 * g + 16)
                for j in range(4):
                    t = Tile(A_BASE, 10 + j, g, 14)
                    dve.wait_ge(proj_read[t.p], t.m + 1)
                    y = XY[:, bass.ds(4 * g + j, 1), 0:TP]
                    TT(y, y, XR[:, j % 2:j % 2 + 1, 0:TP], ALU.mult)
                    CPR(S1["zs"][:, bass.ds(4 * g + j, 1), :], XR[:, j % 2:j % 2 + 1, TP:TA]).then_inc(S["a_yz"], 1); own.done("a_yz")
                    split_lo(dve, own, t.ahead(2))

            dve.wait_ge(S["proj_done"], O1_BASE)
            dve.wait_ge(S["a_qd"], 4)
            step(V.memset(ZQ, 0.0))
            for r in range(2):
                for b in range(NS):
                    src = qd[:, r].rearrange("p (g j b) -> p g j b", g=4, b=NS)[:, :, :, b]
                    dst = ZQ[:, r, :, b].rearrange("p g (j b) -> p g j b", b=NS)[:, :, :, b]
                    ins = CP(dst, src)
            ins.then_inc(S["d_z"], 1); own.done("d_z")
            dve.wait_ge(S["a_yz"], 16)
            for r in range(2):
                for j in range(QPK):
                    q4 = qd[:, 1].rearrange("p (g j b) -> p g j b", g=4, b=NS)
                    d4 = qr[:, r, 0:P].rearrange("p (g j b) -> p g j b", g=4, b=NS)
                    ins = TT(d4[:, :, j], q4[:, :, j], kd[:, 2 * r], ALU.mult)
            ins.then_inc(S["d_prod"], 1); own.done("d_prod")
            dve.wait_ge(S["at_o"], 64)

            def means(b):
                dve.wait_ge(S["d_used"], b + 1)
                if b:
                    dve.wait_ge(S["d_cs"], b)
                CP(pr[:, 3, 0:64], PS[:, 6, 0:64]).then_inc(S["d_km"], 1); own.done("d_km")
            for x in range(1, 64, 2):
                dve.wait_ge(S["d_kT"], x + 1)
                if x >= 3:
                    dve.wait_ge(S["d_ks"], x - 1)
                CP(qt[:, 1, 0:512], PS[:, 5, :]).then_inc(S["d_kt1"], 1); own.done("d_kt1")
                if x % 8 == 7:
                    means(x // 8)
            dst = S1["dst"]
            dve.wait_ge(S["d_snew"], 1)
            dve.wait_ge(S["d_ks"], 64)
            dve.wait_ge(S["d_cs"], 8)
            V.tensor_reduce(dst[:, 0, 1:3], PS[:, 0:2, :], AX, ALU.max)
            step(V.tensor_reduce(dst[:, 0, 0:1], PS[:, 2, 0:NB], AX, ALU.max))
            step(TT(dst[:, 0, 1:3], dst[:, 0, 1:3], PS[:, 3, 0:2], ALU.max))
            TS(dst[:, 1, 0:3], dst[:, 0, 0:3], -SCALE, None, ALU.mult).then_inc(S["d_nm"], 1); own.done("d_nm")
            dve.wait_ge(S["d_exp"], 1)
            step(TT(dst[:, 2, 1:3], dst[:, 2, 1:3], dst[:, 5, 0:2], ALU.add))
            step(V.reciprocal(dst[:, 3, 0:3], dst[:, 2, 0:3]))
            step(TT(dst[:, 3, 0:3], dst[:, 3, 0:3], S1["gdr"][:, 0:3], ALU.mult))
            for k in range(3):
                TS(dg[:, k], ident, dst[:, 3, k:k + 1], None, ALU.mult)
            for k in range(2):
                ins = TS(qt[:, 2, k * P:(k + 1) * P], ones, dst[:, 5, k:k + 1], None, ALU.mult)
            ins.then_inc(S["d_diag"], 1); own.done("d_diag")
            dve.wait_ge(S["d_pT"], 3)
            CP(S1["pc"][0:NB], PS[0:NB, 6, 0:P]).then_inc(S["d_pc"], 1); own.done("d_pc")
            for k in range(2):
                CP(PTD[:, 1 + k].rearrange("p a r -> p (a r)"), PS[:, 4 + k, :]).then_inc(S["d_ptd"], 1); own.done("d_ptd")
            dve.wait_ge(S["d_pT"], 4)
            for k in range(2):
                for j in range(QPK):
                    p4 = PS[:, 3, P + k * P:2 * P + k * P].rearrange("p (g j b) -> p g j b", g=4, b=NS)
                    d4 = qr[:, k, 0:P].rearrange("p (g j b) -> p g j b", g=4, b=NS)
                    ins = TT(d4[:, :, j], p4[:, :, j], kd[:, 1 + 2 * k], ALU.mult)
            step(ins)
            step(TT(qr[:, 0, 0:P], qr[:, 0, 0:P], qr[:, 1, 0:P], ALU.add))
            dve.wait_ge(S["d_used"], 16)
            step(TT(qr[:, 0, 0:P], PS[:, 0, 0:P], qr[:, 0, 0:P], ALU.add))
            TT(XY[:, :, TP:TA], qr[:, 0, 0:P].rearrange("p (h b) -> p h b", b=NS), S1["zs"], ALU.mult
               ).then_inc(S["d_y"], 1); own.done("d_y")
            dve.wait_ge(S["d_y"], 1)
            dve.wait_ge(S["win_out"], 64 * NS)
            y_split_dve(dve, own, 1)
            out_dve(dve, own, 1, O1_BASE)
            dve.wait_ge(proj_read[0], N_TILES // 2)
            dve.wait_ge(proj_read[1], N_TILES // 2)
            norm_dve(dve, own, 2)
            for k in range(KT):
                STT(XY[:, k], XY[:, k], PR[:, R_GF + k:R_GF + k + 1], RS[:], ALU.mult, ALU.mult).then_inc(S["fin_y"], 1); own.done("fin_y")
            for f in range(1, 20, 2):
                i, kk = f // 4, f % 4
                dve.wait_ge(S["fin_T"], f + 1)
                q = slice(0, P if i < NT else NS)
                d = YROW[:, i] if i < NT else YSROW
                CP(d[q, kk * 512:(kk + 1) * 512], PS[q, f % 4, :]).then_inc(S["fin_dve"], 1); own.done("fin_dve")


_INS = ["x_prompt", "x_sample", "state_pool", "state_mlstm_c", "state_mlstm_n", "state_mlstm_m", "cache_kv_cmp",
        "cache_kv_sel", "cache_kv_win", "page_table", "norm0_g", "w_in0", "b_gate0", "w_pool", "pool_scale",
        "mh_norm_g", "w_out0", "norm1_g", "w_in1", "b_gate1", "w_out1", "final_g"]
_OUTS = [("y_prompt", (1, TP, D)), ("y_sample", (NS, 1, D)), ("pool_p", (1, 15, 1024)), ("pool_s", (NS, 15, 1024)),
         ("c_p", (1, GH, HD, HD)), ("c_s", (NS, GH, HD, HD)), ("n_p", (1, GH, HD)), ("n_s", (NS, GH, HD)),
         ("m_p", (1, GH)), ("m_s", (NS, GH)),
         ("kvc_p", (1, TP, 2, NKV, DH)), ("kvc_s", (NS, 1, 2, NKV, DH)),
         ("kvs_p", (1, TP, 2, NKV, DH)), ("kvs_s", (NS, 1, 2, NKV, DH)),
         ("kvw_p", (1, 512, 2, NKV, DH)), ("kvw_s", (NS, 512, 2, NKV, DH))]


def kernel(**inputs):
    import numpy as _np
    import concourse.bacc as _bacc
    from concourse import mybir as _mybir
    from concourse.bass_utils import run_bass_kernel_spmd as _run

    nc = _bacc.Bacc("TRN2", target_bir_lowering=False, num_devices=1,
                     dynamic_dma_scratch_size=256)
    arrays, ins, outs = {}, {}, {}
    for name in _INS:
        arrays[f"in_{name}"] = _np.ascontiguousarray(inputs[name])
    for name, c in zip(("c_common", "c_layer0", "c_layer1"), constants()):
        arrays[f"in_{name}"] = c
    for name, a in arrays.items():
        ins[name[3:]] = nc.dram_tensor(name, a.shape, _mybir.dt.from_np(a.dtype), kind="ExternalInput").ap()
    for name, shape in _OUTS:
        outs[name] = nc.dram_tensor(f"out_{name}", shape, _mybir.dt.float32, kind="ExternalOutput").ap()
    trunk(nc, ins, outs)
    r = _run(nc, [arrays], core_ids=[0])
    return tuple(r.results[0][f"out_{name}"] for name, _ in _OUTS)
```

```python
from contextlib import ExitStack, contextmanager

import numpy as np

import concourse.bass as bass
from concourse import mybir

F32 = mybir.dt.float32
F32R = mybir.dt.float32r
I32 = mybir.dt.int32
ACT = mybir.ActivationFunctionType
ALU = mybir.AluOpType
AX = mybir.AxisListType.X

P = 128
D = 2048
KT = D // P
TP, NS = 512, 8
TA = TP + NS
HALF = TA // 2
NT = TP // P
GH, HD = 4, 256
NH, NKV, DH = 16, 4, 128
QPK = NH // NKV
PAST, PAGE, NPG = 512, 128, 4
NB = 16
NEG = -1.0e30
SCALE = DH ** -0.5
EPS = 1e-6

C_ID, C_ONE, C_COMMON = 0, 128, 256
C0_MASKT, C0_OH8, C0_PSEL, C0_ICNT, C0_SELI, C0_SELF, C0_N = 0, 128, 1152, 1184, 1248, 1252, 1256
C1_NEG, C1_COS, C1_SIN, C1_CMP, C1_AVG, C1_GM, C1_GS, C1_N = 0, 128, 648, 1168, 1232, 1236, 1332, 1336

R_G0, R_G1, R_GF, R_PS, R_MH = 0, 16, 32, 48, 56

G0_BASE, P_BASE, M_BASE, O0_BASE, G1_BASE, A_BASE, O1_BASE, N_TILES = 0, 1, 17, 57, 73, 74, 130, 146


def constants():
    cc = np.zeros((P, C_COMMON), np.float32)
    cc[:, 0:128] = np.eye(P)
    cc[:, 128:256] = 1.0
    c0 = np.zeros((P, C0_N), np.float32)
    s = np.arange(P)
    c0[:, C0_MASKT:C0_MASKT + P] = s[None, :] >= s[:, None]
    for b in range(NS):
        c0[b, C0_OH8 + b * P:C0_OH8 + (b + 1) * P] = 1.0
    for g in range(4):
        for b in range(NS):
            for r in range(15):
                if r >= 15 - (2 ** (g + 1) - 1):
                    c0[b * 15 + r, C0_PSEL + g * 8 + b] = 1.0
        c0[:, C0_ICNT + g * 16:C0_ICNT + (g + 1) * 16] = 1.0 / np.minimum(np.arange(1, 17), 2 ** (g + 1))
    for h in range(4):
        c0[120 + h, C0_SELI + h] = 1.0
        c0[124 + h, C0_SELF + h] = 1.0
    c1 = np.zeros((P, C1_N), np.float32)
    c1[:, C1_NEG:C1_NEG + P] = np.where(s[None, :] <= s[:, None], 0.0, NEG)
    half = DH // 2
    inv = (np.float32(10000.0) ** (-np.arange(half, dtype=np.float32) / np.float32(half))).astype(np.float32)
    pos = np.concatenate([np.arange(TP), np.full(NS, PAST)]).astype(np.float32)
    ang = (inv[:, None] * pos[None, :]).astype(np.float32)
    c1[:, C1_COS:C1_COS + TA] = np.concatenate([np.cos(ang), np.cos(ang)])
    c1[:, C1_SIN:C1_SIN + TA] = np.concatenate([-np.sin(ang), np.sin(ang)])
    for i in range(NT):
        for n in range(NB):
            c1[:, C1_CMP + i * NB + n] = np.where((n + 1) * 32 - 1 <= i * P + s, 0.0, NEG)
    for n in range(4):
        c1[n * 32:(n + 1) * 32, C1_AVG + n] = 1.0 / 32
    for c in range(48):
        for x, branch in enumerate((1, 2, 0)):
            if c % 3 == branch:
                c1[c, C1_GM + x * 32 + (c % 12) // 3 * 8:C1_GM + x * 32 + (c % 12) // 3 * 8 + 8] = 1.0
        c1[c, C1_GS + c // 12] = 1.0
    ce = np.zeros((NB, NPG * P), np.float32)
    for s in range(NPG * P):
        ce[s // 32, s] = 1.0 / 32
    return cc, c0, c1, ce


class Own:

    def __init__(self, eng, S, name):
        self.eng, self.S, self.name = eng, S, name
        self.base, self.n = {}, {}

    def done(self, name):
        self.n[name] = self.n.get(name, 0) + 1
        self.eng.wait_ge(self.S[name], self.base.get(name, 0) + self.n[name])

    def step(self, ins):
        ins.then_inc(self.S[self.name], 1)
        self.done(self.name)

    @contextmanager
    def turns(self, count, per_turn):
        names = set(self.base) | set(self.n) | set(per_turn)
        first = {k: self.base.get(k, 0) + self.n.get(k, 0) for k in names}
        with self.eng.Fori(0, count) as i:
            self.base = {k: first[k] + i * per_turn[k] if k in per_turn else first[k] for k in names}
            self.n = {}
            yield i
            if self.n != per_turn:
                raise AssertionError(("PER", self.n))
        self.base = {k: first[k] + count * per_turn.get(k, 0) for k in names}
        self.n = {}


class Tile:

    def __init__(self, base, j, i=0, per=0):
        self.p = (base + j) % 2
        self.n = base + j + i * per
        self.m = (base + j) // 2 + i * (per // 2)
        self.first = base + j < 2

    def ahead(self, k):
        t = Tile.__new__(Tile)
        t.p, t.n = (self.p + k) % 2, self.n + k
        assert k == 2
        t.m, t.first = self.m + 1, False
        return t


ACT_POOL = {'w_hi': 4}
ACT_HEAD = {'w_hi': 10, 'm_ws': 1, 'm_vr': 1, 'm_D': 4, 'm_abs': 1, 'm_st': 1, 'm_nst': 1, 'c_sc': 8, 'm_sq': 2, 'm_sqrt': 1}
ACT_GROUP = {'a_sw': 6, 'w_hi': 14, 'd_ka': 8, 'a_row': 6, 'd_exp': 1, 'a_cexp': 1, 'at_exp': 16, 'at_sc': 16, 'at_pta': 16}
DVE_HEAD = {'w_split': 10, 'm_wsin': 1, 'm_prod': 1, 'm_dt': 4, 'm_kr': 1, 'm_vd': 1, 'dve_step': 14, 'm_P': 4, 'm_kw': 1, 'm_nT': 1, 'm_decr': 1, 'm_y': 1, 'm_oy': 2, 'm_nev': 1, 'm_cn': 16, 'm_var': 1, 'm_yz': 2}
DVE_GROUP = {'dve_step': 74, 'a_rot': 6, 'w_split': 14, 'd_z': 1, 'd_kb': 8, 'd_km': 8, 'a_src': 6, 'd_prod': 1, 'd_nm': 1, 'd_pd': 1, 'd_pc': 1, 'a_cin': 1, 'at_nm': 16, 'a_cp': 1, 'at_w': 16, 'd_ptd': 1, 'a_ptc': 4, 'at_ptb': 16, 'at_oe': 16, 'a_yz': 4, 'a_rd': 2, 'a_ys': 1}


def trunk(nc, I, O):
    ctx = ExitStack()
    with ctx:
        def sb(name, shape, dt=F32):
            return ctx.enter_context(nc.sbuf_tensor(name, shape, dt))

        def sem(name):
            return ctx.enter_context(nc.semaphore(name))

        XY = sb("xy", [P, KT, TA])
        WR = sb("w_raw", [P, 2, KT, P])
        WH = sb("w_hi", [P, 2, KT, P], F32R)
        WL = sb("w_lo", [P, 2, KT, P], F32R)
        CC = sb("c_common", [P, C_COMMON])
        PR = sb("params", [P, 64])
        RS = sb("rstd", [P, TA])
        XR = sb("x_res", [P, 2, TA])
        ident, ones = CC[:, C_ID:C_ID + P], CC[:, C_ONE:C_ONE + P]
        PS = ctx.enter_context(nc.psum_tensor("ps", [P, 8, 512], F32))

        with nc.sbuf_tensor("h_hi", [P, KT, TA], F32R) as HH, nc.sbuf_tensor("h_lo", [P, KT, TA], F32R) as HL:
            pass
        DB_LEN = 2 * KT * TA
        DB = sb("sample_cache", [P, DB_LEN])

        def scratch(spec):
            at, out = 0, {}
            for name, shape in spec:
                n = int(np.prod(shape))
                v = SC[:, at:at + n]
                if len(shape) == 2:
                    v = v.rearrange("p (a b) -> p a b", b=shape[1])
                elif len(shape) == 3:
                    v = v.rearrange("p (a b c) -> p a b c", b=shape[1], c=shape[2])
                out[name] = v
                at += n
            assert at <= SC_LEN, (at, SC_LEN)
            return out

        SC_LEN = 18100
        SC = sb("scratch", [P, SC_LEN])
        SMALL0 = 240
        S0 = scratch([("c0", (C0_N,)), ("bg", (4,)), ("acol", (16,)), ("nT", (8, NS)), ("ws", (4,)), ("kdw", (2, NS)),
                      ("pr", (2, 16)), ("dtmp", (10, NS)), ("nTh", (2, NS)), ("pad", (8,)),
                      ("qT", (2, TA)), ("kT", (2, TA)), ("vT", (2, TA)), ("vr", (NT * HD,)), ("kr", (NT * HD,)),
                      ("pt", (2, 512)), ("dt", (2, 512)), ("ad", (512,)), ("gbc", (4, 1048)), ("cb", (NS, 512)),
                      ("vdr", (HD,))])
        S0["nor"], S0["nst"] = S0["vdr"][32:32 + NS], S0["vdr"][64:65]
        S0b = scratch([("c0", (C0_N,)), ("small", (SMALL0,)), ("ub", (2, 536)), ("sa", (2, 528)), ("sb", (2, 528)),
                       ("pl", (2, TA)), ("zt", (2, TA)), ("wp", (2, 256)), ("tail", (1024,)), ("sp", (1024,)),
                       ("us", (2, NS)), ("ss", (8, NS))])
        row0 = C0_N + SMALL0
        XROW = SC[:, row0:row0 + 4096].rearrange("p (a b) -> p a b", b=D)
        XSROW = SC[:, row0 + 4096:row0 + 4096 + D]
        PRROW = SC[:, row0 + 6144:row0 + 6144 + P]
        NROW = SC[:, row0 + 6272:row0 + 6272 + 1024]
        GR0 = SC_LEN - 5300
        IGR, FGR, LFR, T1R = (SC[0:4, GR0 + k * TA:GR0 + (k + 1) * TA] for k in range(4))
        BR, AR = SC[0:4, GR0 + 2080:GR0 + 2592], SC[0:4, GR0 + 2592:GR0 + 3104]
        MR = SC[0:4, GR0 + 3104:GR0 + 3104 + 1048]
        GONE = SC[0:4, GR0 + 4160:GR0 + 4672]
        GM0, GD = SC[0:4, GR0 + 4672:GR0 + 4680], SC[0:4, GR0 + 4680:GR0 + 4720]
        S1 = scratch([("c1", (C1_N,)), ("bg", (4,)), ("pg", (32,)), ("few", (1152,)), ("kT", (2, TA)),
                      ("vr", (2, NT * DH)), ("rs", (4, NT * DH)), ("qr", (QPK, TA)), ("qt", (QPK, TA)),
                      ("pr", (4, 512)), ("pt", (2, 512)), ("kcb", (NB,)), ("vcT", (NB,)), ("sc", (16, NB)),
                      ("cst", (4, 16)), ("st", (8, 2)), ("gw", (48, NT)), ("kd", (6, NS)), ("zq", (2, 264)),
                      ("zs", (QPK, NS)), ("kv", (4, NPG, DH)), ("ptd", (NPG, 64)), ("ptc2", (NPG, 32)), ("km", (NB,)),
                      ("pn", (2, 32)), ("on", (3, 32)), ("gdr", (4,)), ("dst", (8,)), ("pnb", (P,))])
        few = S1["few"]
        S1["ptc"] = few[0:NB, 0:1024].rearrange("p (a b) -> p a b", a=2)
        S1["vcr"] = few[0:NB, 1024:1152]
        S1["rd"] = few[32:32 + NS, 0:6 * DH].rearrange("p (a b) -> p a b", a=6)
        S1["ex"], S1["pc"] = few[64:64 + NB, 0:NPG * P], few[64:64 + NB, 512:544]
        S1["gd"] = S1["pt"].rearrange("p a b -> p (a b)")[0:48, 0:96]
        cosT, sinT = S1["c1"][:, C1_COS:C1_COS + TA], S1["c1"][:, C1_SIN:C1_SIN + TA]
        SQ = SC[:, 6664:7704].rearrange("p (a b) -> p a b", a=2)
        YROW = DB[:, 0:8192].rearrange("p (s c) -> p s c", s=4)
        YSROW = DB[:, 8192:8192 + D]

        x_scr = nc.dram_tensor("x_scratch", [P, KT, TA], F32).ap()
        g_scr = nc.dram_tensor("gate_scratch", [4, 1048], F32).ap()

        class Signals(dict):

            def __missing__(self, name):
                self[name] = sem(name)
                return self[name]

        S = Signals()
        w_loaded = [S["w_loaded0"], S["w_loaded1"]]
        proj_read = [S["proj_read0"], S["proj_read1"]]
        block = ctx.enter_context(nc.Block())

        STREAM = {}

        def where(n):
            if n < P_BASE:
                return "w_in0", 7176 - P
            if n < M_BASE:
                return at_pool((n - P_BASE) // 4, (n - P_BASE) % 4)
            if n < O0_BASE:
                return at_head((n - M_BASE) // 10, (n - M_BASE) % 10)
            if n < G1_BASE:
                return "w_out0", (n - O0_BASE) * P
            if n < A_BASE:
                return "w_in1", 5120
            if n < O1_BASE:
                return at_group((n - A_BASE) // 14, (n - A_BASE) % 14)
            return "w_out1", (n - O1_BASE) * P

        def at_pool(g, j):
            return "w_in0", (j // 2) * 1024 + g * 256 + (j % 2) * P

        def at_head(h, j):
            return "w_in0", 2048 + 1024 * (j // 2) + 256 * h + P * (j % 2)

        def at_group(g, j):
            if 4 <= j < 10:
                return "w_in1", 2048 + 512 * (j - 4) + P * g
            return "w_in1", (512 * g + P * j if j < 4 else 5168 + 512 * g + P * (j - 10))

        def load_tile(q, t, w, col):
            if not t.first:
                q.wait_ge(S["w_split"], t.n - 1)
            q.dma_start(WR[:, t.p], I[w].rearrange("(k p) n -> p k n", p=P)[:, :, bass.ds(col, P)]
                        ).then_inc(w_loaded[t.p], 16)

        def load_ahead(sp, base, j, i, per, at, last):
            t = Tile(base, j, i, per).ahead(2)
            if last:
                load_tile(sp, t, *where(base + per * i + j + 2))
            else:
                load_tile(sp, t, *(at(i, j + 2) if j + 2 < per else at(i + 1, j + 2 - per)))

        def sp_turns(sp, count, body):
            if count > 1:
                with sp.Fori(0, count - 1) as i:
                    body(i, False)
            body(count - 1, True)

        def split_hi(act, own, t):
            act.wait_ge(w_loaded[t.p], (t.m + 1) * 16)
            if not t.first:
                act.wait_ge(S["proj_done"], t.n - 1)
            nc.scalar.activation(WH[:, t.p], WR[:, t.p], ACT.Copy).then_inc(S["w_hi"], 1); own.done("w_hi")

        def split_lo(dve, own, t):
            dve.wait_ge(S["w_hi"], t.n + 1)
            nc.vector.tensor_tensor(WL[:, t.p], WR[:, t.p], WH[:, t.p].bitcast(F32), ALU.subtract
                                    ).then_inc(S["w_split"], 1); own.done("w_split")

        def project(pe, t, h_need=None, part=(0, KT), bank=None, between=None):
            if part[0] == 0:
                pe.wait_ge(S["w_split"], t.n + 1)
                if bank is not None:
                    pe.wait_ge(proj_read[1 - t.p], t.m + t.p)
                elif not t.first:
                    pe.wait_ge(proj_read[t.p], t.m)
            bank = 2 * t.p if bank is None else bank
            for k in range(*part):
                if k == KT // 2 and between is not None:
                    between()
                if h_need is not None and k % 2 == 0:
                    pe.wait_ge(S["h_ready"], h_need + k + 2)
                for x, (w, h) in enumerate(((WH, HH), (WH, HL), (WL, HH))):
                    for c in range(2):
                        mm = nc.tensor.matmul(PS[:, bank + c, 0:HALF], lhsT=w[:, t.p, k, :],
                                              rhs=h[:, k, c * HALF:(c + 1) * HALF],
                                              start=(k == 0 and x == 0), stop=(k == KT - 1 and x == 2))
            if part[1] == KT:
                mm.then_inc(S["proj_done"], 1)

        def halves(ap):
            return ap.rearrange("p (a b) -> p a b", b=HALF)

        def ps2(t, q=slice(0, P)):
            return PS[q, 2 * t.p:2 * t.p + 2, 0:HALF]

        def ps_pair(bank, q=slice(0, P)):
            return PS[q, bank:bank + 2, 0:HALF]

        def norm_act(act, own, r):
            if r == 0:
                for k in range(KT):
                    if k >= 2:
                        act.wait_ge(S["nrm_mm"], k - 1)
                    nc.scalar.activation(XR[:, k % 2], XY[:, k], ACT.Square).then_inc(S["nrm_sq"], 1); own.done("nrm_sq")
            act.wait_ge(S["nrm_var"], r + 1)
            nc.scalar.activation(RS[:], RS[:], ACT.Sqrt).then_inc(S["nrm_sqrt"], 1); own.done("nrm_sqrt")

        def norm_pe(pe, r):
            if r:
                pe.wait_ge(S["sq_sum"], KT * r + 2)
            for k in range(1 if r else KT):
                if r == 0:
                    pe.wait_ge(S["nrm_sq"], k + 1)
                for c in range(2):
                    src = RS[:] if r else XR[:, k % 2]
                    mm = nc.tensor.matmul(PS[:, 4 + c, 0:HALF], lhsT=ones, rhs=src[:, c * HALF:(c + 1) * HALF],
                                          start=(k == 0), stop=(r > 0 or k == KT - 1))
                mm.then_inc(S["nrm_mm"], 1)

        def norm_dve(dve, own, r):
            dve.wait_ge(S["nrm_mm"], KT + r)
            nc.vector.tensor_scalar(halves(RS[:]), ps_pair(4), 1.0 / D, EPS, ALU.mult, ALU.add
                                    ).then_inc(S["nrm_var"], 1); own.done("nrm_var")
            dve.wait_ge(S["nrm_sqrt"], r + 1)
            own.step(nc.vector.reciprocal(RS[:], RS[:]))

        def h_dve(dve, own, r, gcol):
            def low(k):
                dve.wait_ge(S["h_hi"], r * KT + k + 1)
                nc.vector.tensor_tensor(HL[:, k], XR[:, k % 2], HH[:, k].bitcast(F32), ALU.subtract
                                        ).then_inc(S["h_ready"], 1); own.done("h_ready")
            for k in range(KT):
                nc.vector.scalar_tensor_tensor(XR[:, k % 2], XY[:, k], PR[:, gcol + k:gcol + k + 1], RS[:],
                                               ALU.mult, ALU.mult).then_inc(S["h_tmp"], 1); own.done("h_tmp")
                if k:
                    low(k - 1)
            low(KT - 1)

        def h_act(act, own, r):
            for k in range(KT):
                act.wait_ge(S["h_tmp"], r * KT + k + 1)
                nc.scalar.activation(HH[:, k], XR[:, k % 2], ACT.Copy).then_inc(S["h_hi"], 1); own.done("h_hi")

        def y_split_act(act, own, r, done):
            act.wait_ge(S["proj_done"], done)
            for k in range(KT):
                nc.scalar.activation(HH[:, k], XY[:, k], ACT.Copy).then_inc(S["y_hi"], 1); own.done("y_hi")

        def y_split_dve(dve, own, r):
            for k in range(KT):
                dve.wait_ge(S["y_hi"], r * KT + k + 1)
                nc.vector.tensor_tensor(HL[:, k], XY[:, k], HH[:, k].bitcast(F32), ALU.subtract
                                        ).then_inc(S["h_ready"], 1); own.done("h_ready")

        def out_dve(dve, own, r, base):
            def body(i, last):
                for j in range(2):
                    t = Tile(base, j, i, 2)
                    dve.wait_ge(S["proj_done"], t.n + 1)
                    dve.wait_ge(S[f"x_res{j}"], (i + 8 * r + 1) * 16)
                    nc.vector.tensor_tensor(halves(XY[:, 2 * i + j, :]), ps2(t), halves(XR[:, j]), ALU.add
                                            ).then_inc(proj_read[t.p], 1)
                    dve.wait_ge(proj_read[t.p], t.m + 1)
                    if not last:
                        split_lo(dve, own, t.ahead(2))
                    dve.wait_ge(S["sq_made"], i * 2 + (16 * r + j + 1))
                    nc.vector.tensor_tensor(RS[:], RS[:], SQ[:, j], ALU.add).then_inc(S["sq_sum"], 1)
                    own.done("sq_sum")
            own.step(nc.vector.memset(RS[:], 0.0))
            with own.turns(8 - r, {"w_split": 2, "sq_sum": 2}) as i:
                body(i, False)
            if r:
                body(7, True)

        def out_act(act, own, r, base):
            def body(i, last):
                for j in range(2):
                    t = Tile(base, j, i, 2)
                    act.wait_ge(proj_read[t.p], t.m + 1)
                    act.wait_ge(S["sq_sum"], i * 2 + (16 * r + j + 1))
                    nc.scalar.activation(SQ[:, j], XY[:, 2 * i + j, :], ACT.Square).then_inc(S["sq_made"], 1)
                    own.done("sq_made")
                    if not last:
                        split_hi(act, own, t.ahead(2))
            with own.turns(8 - r, {"w_hi": 2, "sq_made": 2}) as i:
                body(i, False)
            if r:
                body(7, True)

        def out_pe(pe, r, base, h_need):
            with pe.Fori(0, 8) as i:
                for j in range(2):
                    project(pe, Tile(base, j, i, 2), h_need if j == 0 else None)

        def out_sp(sp, r, base, nxt):
            def body(i, last):
                for j in range(2):
                    t = Tile(base, j, i, 2)
                    if not (last and nxt is None):
                        load_ahead(sp, base, j, i, 2, lambda i, j: ("w_out1" if r else "w_out0", (2 * i + j) * P), last)
                    sp.wait_ge(proj_read[t.p], t.m)
                    sp.dma_start(XR[:, j], x_scr[:, bass.ds(2 * i + j, 1), :].rearrange("p a t -> p (a t)")
                                 ).then_inc(S[f"x_res{j}"], 16)
            sp_turns(sp, 8, body)

        def ring(u):
            if u % 8 < 4:
                return S1["kv"][:, u % 8]
            idle = S1["pr"] if u % 48 < 24 else S1["qr"]
            idle = idle.rearrange("p a b -> p (a b)")[:, (u % 8 - 4) * 512:(u % 8 - 3) * 512]
            return idle.rearrange("p (a d) -> p a d", d=DH)

        def landed_by(u):
            return sum(32 if v % 3 == 1 else 64 for v in range(u % 8, u + 1, 8))

        kvout = [("kvc", 0), ("kvc", 1), ("kvs", 0), ("kvs", 1), ("kvw", 0), ("kvw", 1)]

        @block.sync
        def _(sp):
            xp = I["x_prompt"].rearrange("a (i p) d -> (a i) p d", p=P)
            sp.dma_start(CC[:], I["c_common"]).then_inc(S["consts"], 16)
            for i in range(2):
                sp.dma_start(XROW[:, i], xp[i]).then_inc(S[f"xrow_in{i}"], 16)
            load_tile(sp, Tile(G0_BASE, 0), *where(0))
            load_tile(sp, Tile(P_BASE, 0), *where(1))
            for i in range(2, NT):
                sp.wait_ge(S["xt_made"], 4 * (i - 1))
                sp.dma_start(XROW[:, i % 2], xp[i]).then_inc(S[f"xrow_in{i % 2}"], 16)
            sp.dma_start(S0["c0"], I["c_layer0"]).then_inc(S["consts"], 16)
            sp.dma_start(XSROW[0:NS], I["x_sample"].rearrange("b o d -> (b o) d")).then_inc(S["small_in"], 16)
            for name, row, n in (("norm0_g", R_G0, 16), ("norm1_g", R_G1, 16), ("final_g", R_GF, 16),
                                 ("pool_scale", R_PS, 8), ("mh_norm_g", R_MH, 8)):
                sp.dma_start(PRROW[row:row + n], I[name].rearrange("(k p) -> k p", p=P)).then_inc(S["small_in"], 16)
            sp.dma_start(NROW[0:NS], I["state_mlstm_n"].rearrange("b h d -> b (h d)")).then_inc(S["small_in"], 16)
            sp.dma_start(S0["bg"][0:4, 0:2], I["b_gate0"].rearrange("(a h) -> h a", a=2),
                         allow_slow_non_contiguous=True).then_inc(S["small_in"], 16)
            sp.dma_start(GM0, I["state_mlstm_m"].rearrange("b h -> h b"),
                         allow_slow_non_contiguous=True).then_inc(S["small_in"], 16)
            load_ahead(sp, G0_BASE, 0, 0, 1, None, True)
            sp.wait_ge(S["xt_act"], 8)
            sp.wait_ge(S["xt_dve"], 9)
            sp.dma_start(x_scr, XY[:]).then_inc(S["x_saved"], 16)
            sp.wait_ge(S["npt_ready"], 1)
            sp.dma_start(S0b["sp"][0:120], I["state_pool"].rearrange("b r c -> (b r) c")).then_inc(S["sp_in"], 16)
            sp.dma_start(O["pool_s"][:, 0:14], I["state_pool"][:, 1:15]).then_inc(S["pool_out"], 16)

            def load_map(g):
                sp.dma_start(S0b["wp"], I["w_pool"][bass.ds(g, 1)].rearrange("o (c p) d -> p (o c) d", p=P)
                             ).then_inc(S["wp_in"], 16)

            def pool(g, last):
                for j in range(4):
                    load_ahead(sp, P_BASE, j, g, 4, at_pool, last)
                if not last:
                    sp.wait_ge(S["pl_mm"], g + 1)
                    load_map(g + 1)
            load_map(0)
            sp_turns(sp, 4, pool)

            sp.wait_ge(S["g_mr"], 1)
            sp.dma_start(g_scr, MR).then_inc(S["g_saved"], 16)
            sp.dma_start(O["m_p"].rearrange("o h -> h o"), GD[:, 32:33],
                         allow_slow_non_contiguous=True).then_inc(S["m_out"], 16)
            sp.dma_start(O["m_s"].rearrange("b h -> h b"), GD[:, 0:8],
                         allow_slow_non_contiguous=True).then_inc(S["m_out"], 16)
            sp.wait_ge(S["pl_ready"], 4)
            tail = S0b["tail"]
            sp.dma_start(O["pool_p"].rearrange("a r c -> (a r) c"), tail[0:15]).then_inc(S["tail_out"], 16)
            sp.dma_start(O["pool_s"][:, 14], tail[15:23]).then_inc(S["tail_out"], 16)
            sp.wait_ge(S["g_saved"], 16)
            sp.wait_ge(S["m_out"], 32)
            sp.wait_ge(S["pl_y"], 8 + 1)
            sp.wait_ge(S["tail_out"], 32)
            sp.wait_ge(S["g_acolT"], 1)
            for h in range(4):
                sp.dma_start(S0["gbc"][:, h], g_scr[h:h + 1, :].partition_broadcast(P)
                             ).then_inc(S["g_bc"], 16)

            def load_states(h):
                for b in range(NS):
                    sp.dma_start(S0["cb"][:, b].rearrange("p (c e) -> p c e", c=2),
                                 I["state_mlstm_c"][b, bass.ds(h, 1)].rearrange("o (c p) e -> p (o c) e", p=P)
                                 ).then_inc(S["c_in"], 16)

            def head(h, last):
                for j in range(10):
                    load_ahead(sp, M_BASE, j, h, 10, at_head, last)
                    if j < 8:
                        lo, n = j % 4 * P, P - (j % 4 == 3)
                        b = bass.ds(2 * h + j // 4, 1)
                        sp.dma_start(O["kvw_s"][b, lo:lo + n], I["cache_kv_win"][b, lo + 1:lo + 1 + n]
                                     ).then_inc(S["win_out"], 16)
                sp.wait_ge(S["m_st"], h + 1)
                sp.wait_ge(S["m_nst"], h + 1)
                sp.dma_start(O["c_p"][0, bass.ds(h, 1)].rearrange("o (c p) e -> p (o c) e", p=P),
                             S0["kr"][:, 0:512].rearrange("p (c e) -> p c e", c=2)).then_inc(S["st_out"], 16)
                sp.dma_start(O["n_p"][0, bass.ds(h, 1)], S0["nst"]).then_inc(S["st_out"], 16)
                sp.wait_ge(S["m_nev"], h + 1)
                sp.dma_start(O["n_s"][:, bass.ds(h, 1)].rearrange("b o d -> b (o d)"), S0["nor"]
                             ).then_inc(S["n_out"], 16)
                for b in range(NS):
                    sp.wait_ge(S["m_cn"], h * (2 * NS) + 2 * b + 2)
                    sp.dma_start(O["c_s"][b, bass.ds(h, 1)].rearrange("o (c p) e -> p (o c) e", p=P),
                                 S0["cb"][:, b].rearrange("p (c e) -> p c e", c=2)).then_inc(S["c_out"], 16)
                if not last:
                    sp.wait_ge(S["c_out"], (h + 1) * (16 * NS))
                    load_states(h + 1)
            load_states(0)
            sp_turns(sp, 4, head)

            out_sp(sp, 0, O0_BASE, G1_BASE)
            sp.wait_ge(S["c_out"], 64 * NS)
            sp.wait_ge(S["st_out"], 128)
            sp.wait_ge(S["n_out"], 64)
            sp.dma_start(S1["c1"], I["c_layer1"]).then_inc(S["consts"], 16)
            sp.dma_start(S1["ex"], I["c_expand"]).then_inc(S["consts"], 16)
            sp.dma_start(S1["bg"][0:48, 0:1], I["b_gate1"].rearrange("(a o) -> a o", o=1),
                         allow_slow_non_contiguous=True).then_inc(S["consts"], 16)
            sp.dma_start(S1["pg"][0:1].bitcast(I32), I["page_table"].rearrange("(o b) n -> o (b n)", o=1)
                         ).then_inc(S["consts"], 16)
            load_ahead(sp, G1_BASE, 0, 0, 1, None, True)
            sp.wait_ge(proj_read[0], (G1_BASE + 1) // 2)
            sp.wait_ge(proj_read[1], G1_BASE // 2)
            sp.dma_start(x_scr, XY[:]).then_inc(S["x_saved"], 16)
            sp.wait_ge(S["consts"], 16 * 6)

            win = I["cache_kv_win"]

            def load_unit(g, u):
                c, b, kind = (u // 24) % 2, (u % 24) // 3, u % 3
                cache = I["cache_kv_sel" if kind == 0 else "cache_kv_cmp"]
                pages = [sp.value_load(S1["pg"][0:1, b * NPG + pg:b * NPG + pg + 1].bitcast(I32),
                                       min_val=0, max_val=cache.shape[0] - 1) for pg in range(NPG) if kind != 1]
                if u == 52:
                    sp.wait_ge(S["at_T"], 16 * g + 16)
                elif 28 <= u < 32:
                    sp.wait_ge(S["a_cs"], g + 1)
                elif not (isinstance(g, int) and g == 0 and u < 8):
                    sp.wait_ge(S["d_used"], 48 * g + (u - 7))
                for pg in (2, 0) if kind == 1 else ():
                    sp.dma_start(ring(u)[:, pg:pg + 2], win[b, pg * P:(pg + 2) * P, c, bass.ds(g + u // 48, 1)
                                                                    ].rearrange("(a p) o d -> p a (o d)", p=P)
                                 ).then_inc(S[f"d_in{u % 8}"], 16)
                for pg in range(NPG) if kind != 1 else ():
                    src = cache[bass.ds(pages[pg], 1), :, c, bass.ds(g + u // 48, 1)].rearrange("q p o d -> p (q o d)")
                    sp.dma_start(ring(u)[:, pg], src).then_inc(S[f"d_in{u % 8}"], 16)

            UNITS = {4: (8, 14), 5: (14, 20), 6: (20, 26), 7: (26, 28), 10: (28, 35), 11: (35, 41), 12: (41, 47),
                     13: (47, 53)}

            def group(g, last):
                for j in range(14):
                    load_ahead(sp, A_BASE, j, g, 14, at_group, last)
                    if j in UNITS:
                        for u in range(*UNITS[j]):
                            if u < 48 or not last:
                                load_unit(g, u)
                    if j == 11:
                        sp.wait_ge(S["a_row"], 6 * g + 6)
                        for x in (1, 0, 2, 3, 4, 5):
                            name, c = kvout[x]
                            src = S1["rs"][:, (0, 1, 2, None, 3)[x]] if x in (0, 1, 2, 4) else S1["vr"][:, x // 4]
                            sp.dma_start(O[name + "_p"][0, :, c, bass.ds(g, 1)].rearrange("(i p) o d -> p i (o d)", p=P),
                                         src.rearrange("p (i d) -> p i d", d=DH)).then_inc(S["row_out"], 16)
                if not last:
                    for u in range(53, 56):
                        load_unit(g, u)
                sp.wait_ge(S["a_rd"], 2 * g + 2)
                for x in (1, 0, 2, 3, 4, 5):
                    name, c = kvout[x]
                    dst = O["kvw_s"][:, 511, c, bass.ds(g, 1)] if name == "kvw" else \
                        O[name + "_s"][:, 0, c, bass.ds(g, 1)]
                    sp.dma_start(dst.rearrange("b o d -> b (o d)"), S1["rd"][:, x]).then_inc(S["row_out"], 16)
            for u in range(8):
                load_unit(0, u)
            sp_turns(sp, 4, group)

            sp.wait_ge(S["a_yz"], 16)
            out_sp(sp, 1, O1_BASE, None)

            for i in range(NT):
                sp.wait_ge(S["fin_act"], 2 * i + 2)
                sp.wait_ge(S["fin_dve"], 2 * i + 2)
                sp.dma_start(O["y_prompt"][0, i * P:(i + 1) * P], YROW[:, i]).then_inc(S["y_out"], 16)
            sp.wait_ge(S["fin_act"], 2 * NT + 2)
            sp.wait_ge(S["fin_dve"], 2 * NT + 2)
            sp.dma_start(O["y_sample"][:, 0], YSROW[0:NS]).then_inc(S["y_out"], 16)
            for name, n in (("y_out", 16 * (NT + 1)), ("row_out", 16 * 48), ("win_out", 16 * 32), ("c_out", 64 * NS),
                            ("st_out", 128), ("n_out", 64), ("pool_out", 16), ("tail_out", 32), ("m_out", 32),
                            ("x_saved", 32), ("g_saved", 16)):
                sp.wait_ge(S[name], n)

        @block.tensor
        def _(pe):
            T = nc.tensor.transpose
            M = nc.tensor.matmul
            c0 = S0["c0"]
            pe.wait_ge(S["consts"], 16)
            for i in range(NT):
                pe.wait_ge(S[f"xrow_in{i % 2}"], (i // 2 + 1) * 16)
                for kk in range(4):
                    f = 4 * i + kk
                    if f >= 4:
                        pe.wait_ge(S["xt_dve" if f % 2 else "xt_act"], (f - 4) // 2 + 1)
                    for k in range(4):
                        mm = T(PS[:, f % 4, k * P:(k + 1) * P], XROW[:, i % 2, (4 * kk + k) * P:(4 * kk + k + 1) * P],
                               ident)
                    mm.then_inc(S["xt_made"], 1)
            pe.wait_ge(S["small_in"], 16 * 9)
            for k in range(KT):
                mm = T(PS[:, 4, k * NS:(k + 1) * NS], XSROW[0:NS, k * P:(k + 1) * P], ident[0:NS, 0:NS])
            mm.then_inc(S["xt_made"], 1)
            T(PS[:, 5, 0:64], PRROW[0:64, :], ident[0:64, 0:64]).then_inc(S["xt_made"], 1)
            for k in range(8):
                mm = T(PS[:, 6, k * NS:(k + 1) * NS], NROW[0:NS, k * P:(k + 1) * P], ident[0:NS, 0:NS])
            mm.then_inc(S["xt_made"], 1)
            pe.wait_ge(S["npt_ready"], 1)
            norm_pe(pe, 0)

            project(pe, Tile(G0_BASE, 0), 0)
            pe.wait_ge(S["consts"], 32)
            pe.wait_ge(proj_read[0], 1)
            for x, c in enumerate((C0_SELI, C0_SELF)):
                for a in range(2):
                    mm = M(PS[0:4, 4 + 2 * x + a, 0:HALF], lhsT=c0[:, c:c + 4],
                           rhs=S0b["zt"][:, 0, a * HALF:(a + 1) * HALF], start=True, stop=True)
            mm.then_inc(S["g_sel"], 1)

            pe.wait_ge(S["g_rows"], 1)
            pe.wait_ge(S["sp_in"], 16)
            for k in range(8):
                mm = M(PS[:, 5, k * NS:(k + 1) * NS], lhsT=S0b["sp"][0:120, k * P:(k + 1) * P],
                       rhs=c0[0:120, C0_PSEL + (k // 2) * NS:C0_PSEL + (k // 2 + 1) * NS], start=True, stop=True)
            mm.then_inc(S["pl_ss"], 1)
            with pe.Fori(0, 4) as g:
                for j in range(3):
                    project(pe, Tile(P_BASE, j, g, 4))
                pe.wait_ge(proj_read[Tile(P_BASE, 1).p], Tile(P_BASE, 1, g, 4).m + 1)
                pe.wait_ge(S["pl_y"], 2 * g + 1)
                for j in range(2):
                    mm = T(PS[0:23, 4, j * P:(j + 1) * P], S0b["ub"][:, j, 16 + 497:16 + 520], ident)
                mm.then_inc(S["pl_T"], 1)
                project(pe, Tile(P_BASE, 3, g, 4))
                pe.wait_ge(S["wp_in"], (g + 1) * 16)
                pe.wait_ge(S["pl_ready"], g + 1)
                for d in range(2):
                    for a in range(2):
                        for c in range(2):
                            mm = M(PS[:, 4 + 2 * d + a, 0:HALF], lhsT=S0b["wp"][:, c, d * P:(d + 1) * P],
                                   rhs=S0b["pl"][:, c, a * HALF:(a + 1) * HALF], start=(c == 0), stop=(c == 1))
                mm.then_inc(S["pl_mm"], 1)

            pe.wait_ge(S["pl_y"], 8 + 1)
            for i in range(NT):
                mm = T(PS[:, 4, i * 4:(i + 1) * 4], AR[:, i * P:(i + 1) * P], ident[0:4, 0:4])
            mm.then_inc(S["g_acolT"], 1)

            qT, kT, vT, vr, kr, pt, cb = (S0[n] for n in ("qT", "kT", "vT", "vr", "kr", "pt", "cb"))
            with pe.Fori(0, 4) as h:
                for j in range(6):
                    project(pe, Tile(M_BASE, j, h, 10))
                t5 = Tile(M_BASE, 5, h, 10)
                pe.wait_ge(proj_read[t5.p], t5.m + 1)
                pe.wait_ge(S["g_acol"], 1)
                for x, src in enumerate((kT, vT)):
                    for i in range(NT):
                        for c in range(2):
                            at = (i % 2) * HD + c * P
                            mm = T(PS[:, 4 + 2 * x + i // 2, at:at + P], src[:, c, i * P:(i + 1) * P], ident)
                    mm.then_inc(S["m_rowT"], 1)
                for c in range(2):
                    mm = T(PS[0:NS, 0, c * P:(c + 1) * P], vT[:, c, TP:TA], ident)
                mm.then_inc(S["m_rowT"], 1)
                pe.wait_ge(S["c_in"], (h + 1) * (16 * NS))
                for j in range(2):
                    for b in range(NS):
                        for c in range(2):
                            M(PS[:, 1, j * 8 + b:j * 8 + b + 1], lhsT=cb[:, b, c * HD + j * P:c * HD + (j + 1) * P],
                              rhs=qT[:, c, TP + b:TP + b + 1], start=(c == 0), stop=(c == 1))
                pe.wait_ge(S["m_prod"], h + 1)
                for c in range(2):
                    mm = M(PS[:, 1, 16:32], lhsT=ones, rhs=S0["pr"][:, c], start=(c == 0), stop=(c == 1))
                mm.then_inc(S["m_dec"], 1)

                def scores(i):
                    if i == 0:
                        pe.wait_ge(S["m_kr"], h + 1)
                    if i >= 2:
                        pe.wait_ge(S["m_P"], 4 * h + (i - 1))
                    for c in range(2):
                        mm = M(PS[:, 4 + i % 2, 0:TP - i * P], lhsT=kT[:, c, i * P:(i + 1) * P],
                               rhs=qT[:, c, i * P:TP], start=(c == 0), stop=(c == 1))
                    mm.then_inc(S["m_S"], 1)
                scores(0)
                for i in range(NT):
                    if i < NT - 1:
                        scores(i + 1)
                    if i == 0:
                        pe.wait_ge(S["m_vr"], h + 1)
                        pe.wait_ge(S["m_vd"], h + 1)
                    pe.wait_ge(S["m_P"], 4 * h + (i + 1))
                    L = TP - i * P
                    for j in range(2):
                        M(PS[:, 6 + j, i * P:TP], lhsT=vr[:, i * HD + j * P:i * HD + (j + 1) * P], rhs=pt[:, i % 2, 0:L],
                          start=(i == 0), stop=(i == NT - 1))
                    mm = M(PS[:, 0, i * P:TP], lhsT=ones, rhs=pt[:, i % 2, 0:L], start=(i == 0), stop=(i == NT - 1))
                    mm.then_inc(S["m_PV"], 1)
                pe.wait_ge(S["m_kw"], h + 1)
                for c in range(2):
                    for i in range(NT):
                        M(PS[:, 4, c * HD:(c + 1) * HD], lhsT=kr[:, i * HD + c * P:i * HD + (c + 1) * P],
                          rhs=vr[:, i * HD:(i + 1) * HD], start=(i == 0), stop=(i == NT - 1))
                for i in range(NT):
                    mm = M(PS[0:1, 5, 0:HD], lhsT=ones[:, 0:1], rhs=kr[:, i * HD:(i + 1) * HD],
                           start=(i == 0), stop=(i == NT - 1))
                mm.then_inc(S["m_stT"], 1)

                project(pe, Tile(M_BASE, 6, h, 10))
                pe.wait_ge(S["m_y"], h + 1)
                pe.wait_ge(S["m_decr"], h + 1)
                project(pe, Tile(M_BASE, 7, h, 10))
                pe.wait_ge(S["m_nst"], h + 1)
                pe.wait_ge(S["m_nT"], h + 1)
                for c in range(2):
                    mm = T(PS[0:NS, 5, c * P:(c + 1) * P], S0["nTh"][:, c], ident)
                mm.then_inc(S["m_nr"], 1)
                for q, bank in enumerate((4, 6, 7, 5)):
                    if q == 3:
                        pe.wait_ge(S["m_nev"], h + 1)
                    for y in range(2):
                        b = 2 * q + y
                        mm = M(PS[:, bank, y * HD:(y + 1) * HD], lhsT=c0[0:NS, C0_OH8 + b * P:C0_OH8 + (b + 1) * P],
                               rhs=S0["vdr"][0:NS], start=True, stop=True)
                    mm.then_inc(S["m_vb"], 1)
                project(pe, Tile(M_BASE, 8, h, 10))
                pe.wait_ge(S["m_cn"], (h + 1) * (2 * NS))
                pe.wait_ge(S["m_sq"], 2 * h + 2)
                for a in range(2):
                    for j in range(2):
                        mm = M(PS[:, 4 + a, 0:HALF], lhsT=ones, rhs=qT[:, j, a * HALF:(a + 1) * HALF],
                               start=(j == 0), stop=(j == 1))
                mm.then_inc(S["m_ssq"], 1)
                project(pe, Tile(M_BASE, 9, h, 10))
                pe.wait_ge(S["m_var"], h + 1)

            out_pe(pe, 0, O0_BASE, KT)
            norm_pe(pe, 1)
            project(pe, Tile(G1_BASE, 0), 2 * KT)
            pe.wait_ge(proj_read[1], (G1_BASE + 1) // 2)
            c1 = S1["c1"]
            for i in range(NT):
                mm = T(PS[:, 4, i * 48:(i + 1) * 48], XR[0:48, 0, i * P:(i + 1) * P], ident[0:48, 0:48])
            pe.wait_ge(S["g1_gd"], 1)
            mm = M(PS[0:96, 5, 0:4], lhsT=S1["gd"], rhs=c1[0:48, C1_GS:C1_GS + 4], start=True, stop=True)
            mm.then_inc(S["g1_T"], 1)
            pe.wait_ge(S["g1_gw"], 1)

            kT, vr, qr, qt, pr, pt, ptc, kv, zq, few = (
                S1[n] for n in ("kT", "vr", "qr", "qt", "pr", "pt", "ptc", "kv", "zq", "few"))
            with pe.Fori(0, 4) as g:
                def rows(x):
                    src = (XR[:, 0], XR[:, 1], kT[:, 0], XR[:, 0], kT[:, 1], XR[:, 1])[x]
                    pe.wait_ge(S["a_src"], 6 * g + (x + 1))
                    if x:
                        pe.wait_ge(S["a_row"], 6 * g + x)
                    if x < 3:
                        pe.wait_ge(S["d_km"], 8 * g + 2 * x + 4)
                    for i in range(NT):
                        mm = T(PS[:, 4, i * P:(i + 1) * P], src[:, i * P:(i + 1) * P], ident)
                    mm.then_inc(S["a_rowT"], 1)

                def landed(u):
                    pe.wait_ge(S[f"d_in{u % 8}"], 320 * g + landed_by(u))

                def turn_keys(b):
                    for kind, bank in ((0, 5), (1, 7)):
                        u = 3 * b + kind
                        landed(u)
                        for pg in range(NPG):
                            mm = T(PS[:, bank, pg * P:(pg + 1) * P], ring(u)[:, pg], ident)
                        mm.then_inc(S["d_used"], 1)
                    u = 3 * b + 2
                    landed(u)
                    if 2 <= b:
                        if b % 2 == 0 and b >= 4:
                            pe.wait_ge(S["a_row"], 6 * g + (b - 2) // 2)
                    if b:
                        pe.wait_ge(S["d_km"], 8 * g + b)
                    for pg in range(NPG):
                        mm = M(PS[:, 4, pg * 4:(pg + 1) * 4], lhsT=ring(u)[:, pg], rhs=c1[:, C1_AVG:C1_AVG + 4],
                               start=True, stop=True)
                    mm.then_inc(S["d_used"], 1)

                def score_keys(b):
                    pe.wait_ge(S["d_ka"], 8 * g + (b + 1))
                    M(PS[0:32, 6, :], lhsT=zq[:, 1, 32 * b:32 * b + 32], rhs=pt[:, 0], start=(b == 0),
                      stop=(b == NS - 1), skip_group_check=True)
                    pe.wait_ge(S["d_kb"], 8 * g + (b + 1))
                    M(PS[32:64, 6, :], lhsT=zq[:, 1, 32 * b:32 * b + 32], rhs=pt[:, 1], start=(b == 0),
                      stop=(b == NS - 1), skip_group_check=True)
                    pe.wait_ge(S["d_km"], 8 * g + (b + 1))
                    M(PS[64:96, 6, 0:NB], lhsT=zq[:, 0, 32 * b:32 * b + 32], rhs=S1["km"], start=(b == 0),
                      stop=(b == NS - 1), skip_group_check=True).then_inc(S["d_ks"], 1)

                def new_keys():
                    pe.wait_ge(S["d_prod"], g + 1)
                    M(PS[0:64, 5, 0:1], lhsT=S1["pn"].rearrange("p a b -> p (a b)"), rhs=ones[:, 0:1],
                      start=True, stop=True).then_inc(S["d_snew"], 1)

                for j in range(4):
                    project(pe, Tile(A_BASE, j, g, 14))
                for j in range(4, 8):
                    b = 2 * (j - 4)
                    if j == 4:
                        pe.wait_ge(S["d_z"], g + 1)
                    turn_keys(b)

                    def half_way(b=b):
                        score_keys(b)
                        turn_keys(b + 1)
                    project(pe, Tile(A_BASE, j, g, 14), between=half_way)
                    score_keys(b + 1)
                    if j > 4:
                        rows(j - 5)
                project(pe, Tile(A_BASE, 8, g, 14))
                rows(3)
                project(pe, Tile(A_BASE, 9, g, 14), between=new_keys)
                rows(4)
                pe.wait_ge(S["d_pd"], g + 1)
                T(PS[0:NB, 5, 384:512], S1["vcT"], ident)
                for pg in range(NPG):
                    T(PS[:, 5, pg * 64:(pg + 1) * 64], pr[0:64, 0, pg * P:(pg + 1) * P], ident[0:64, 0:64])
                T(PS[0:NB, 5, 256:288], pr[64:96, 0, 0:NB], ident[64:96, 64:96])
                M(PS[:, 5, 320:384], lhsT=S1["pnb"][0:64], rhs=ident[0:64, 0:64], start=True, stop=True
                  ).then_inc(S["d_pT"], 1)
                rows(5)
                pe.wait_ge(S["d_kb"], 8 * g + 8)
                for jj in range(QPK):
                    for i in range(NT):
                        at = (4 * jj + i) * NB
                        mm = M(PS[:, 7, at:at + NB], lhsT=qr[:, jj, i * P:(i + 1) * P], rhs=S1["kcb"],
                               start=True, stop=True)
                mm.then_inc(S["a_cs"], 1)

                def scores(n):
                    jj, i = n // 4, n % 4
                    for r in range(2):
                        mm = M(PS[:, r, 0:(i + 1) * P], lhsT=qt[:, jj, i * P:(i + 1) * P],
                               rhs=kT[:, r, 0:(i + 1) * P], start=True, stop=True)
                    mm.then_inc(S["at_s"], 1)

                def cmp_turn(jj):
                    pe.wait_ge(S["a_cp"], g + 1)
                    if jj:
                        pe.wait_ge(S["a_ptc"], 4 * g + jj)
                    for i in range(NT):
                        mm = T(PS[0:NB, 7, i * P:(i + 1) * P], S1["sc"][:, 4 * jj + i], ident)
                    mm.then_inc(S["a_ctT"], 1)

                def values(b):
                    for kind in range(3):
                        u = 24 + 3 * b + kind
                        landed(u)
                        for pg in range(NPG):
                            p = S1["ptc2"][:, pg, b:32:NS] if kind == 2 else \
                                S1["ptd"][:, pg, 32 * kind + b:32 * kind + 32:NS]
                            mm = M(PS[:, 6, P + b:P + 32:NS], lhsT=ring(u)[:, pg], rhs=p,
                                   start=(kind == 0 and pg == 0), stop=(kind == 2 and pg == NPG - 1))
                        mm.then_inc(S["d_used"], 1)

                scores(0)
                pe.wait_ge(S["d_pc"], g + 1)
                pe.wait_ge(S["a_row"], 6 * g + 6)
                for pg in range(NPG):
                    mm = M(PS[:, 4, pg * 32:(pg + 1) * 32], lhsT=S1["ex"][:, pg * P:(pg + 1) * P], rhs=S1["pc"],
                           start=True, stop=True)
                mm.then_inc(S["d_eT"], 1)
                cmp_turn(0)
                pe.wait_ge(S["d_ptd"], g + 1)
                for n in range(16):
                    jj, i = n // 4, n % 4
                    pe.wait_ge(S["at_sc"], 16 * g + (n + 1))
                    for r in range(2):
                        for s in range(i + 1):
                            mm = T(PS[:, 4 + r, s * P:(s + 1) * P], pr[:, 2 * (n % 2) + r, s * P:(s + 1) * P], ident)
                    mm.then_inc(S["at_T"], 1)
                    if n < 15:
                        scores(n + 1)
                    project(pe, Tile(A_BASE, 10 + jj, g, 14), part=(4 * i, 4 * i + 4), bank=2)
                    if i == 0:
                        pe.wait_ge(S["a_ptc"], 4 * g + (jj + 1))
                    if n:
                        pe.wait_ge(S["at_oe"], 16 * g + n)
                    if n >= 2 and n % 2 == 0:
                        values(n // 2 - 1)
                    M(PS[:, 6, 0:P], lhsT=S1["vcr"], rhs=ptc[:, jj % 2, i * P:(i + 1) * P], start=True, stop=False)
                    pe.wait_ge(S["at_pta"], 16 * g + (n + 1))
                    for s in range(i + 1):
                        M(PS[:, 6, 0:P], lhsT=vr[:, 0, s * P:(s + 1) * P], rhs=pt[:, 0, s * P:(s + 1) * P],
                          start=False, stop=False)
                    pe.wait_ge(S["at_ptb"], 16 * g + (n + 1))
                    for s in range(i + 1):
                        mm = M(PS[:, 6, 0:P], lhsT=vr[:, 1, s * P:(s + 1) * P], rhs=pt[:, 1, s * P:(s + 1) * P],
                               start=False, stop=(s == i))
                    mm.then_inc(S["at_o"], 1)
                    if i == 2 and jj < 3:
                        cmp_turn(jj + 1)
                    if n in (12, 14):
                        pe.wait_ge(S["a_ptc"], 4 * g + 4)
                        if n == 14:
                            pe.wait_ge(S["a_rd"], 2 * g + 1)
                        for x in (range(4) if n == 12 else range(4, 6)):
                            mm = T(PS[0:NS, 7, (x % 4) * P:(x % 4 + 1) * P], S1["kd"][:, x], ident)
                        mm.then_inc(S["a_rdT"], 1)
                pe.wait_ge(S["at_oe"], 16 * g + 16)
                values(7)
                pe.wait_ge(S["a_rd"], 2 * g + 2)
                pe.wait_ge(S["a_ys"], g + 1)
            out_pe(pe, 1, O1_BASE, 3 * KT)
            norm_pe(pe, 2)
            for f in range(20):
                i, kk = f // 4, f % 4
                if f == 0:
                    pe.wait_ge(S["fin_y"], KT)
                if f >= 4:
                    pe.wait_ge(S["fin_dve" if f % 2 else "fin_act"], (f - 4) // 2 + 1)
                for k in range(4):
                    if i < NT:
                        mm = T(PS[:, f % 4, k * P:(k + 1) * P], XY[:, 4 * kk + k, i * P:(i + 1) * P], ident)
                    else:
                        mm = T(PS[0:NS, f % 4, k * P:(k + 1) * P], XY[:, 4 * kk + k, TP:TA], ident)
                mm.then_inc(S["fin_T"], 1)

        @block.scalar
        def _(act):
            A = nc.scalar.activation
            own = Own(act, S, "act_step")
            for f in range(0, 16, 2):
                act.wait_ge(S["xt_made"], f + 1)
                A(XY[:, 4 * (f % 4):4 * (f % 4) + 4, (f // 4) * P:(f // 4 + 1) * P],
                  PS[:, f % 4, :].rearrange("p (k t) -> p k t", k=4), ACT.Copy).then_inc(S["xt_act"], 1); own.done("xt_act")
            split_hi(act, own, Tile(G0_BASE, 0))
            split_hi(act, own, Tile(P_BASE, 0))
            act.wait_ge(S["xt_act"], 8)
            act.wait_ge(S["xt_dve"], 9)
            norm_act(act, own, 0)
            h_act(act, own, 0)
            act.wait_ge(S["proj_done"], 1)
            act.wait_ge(S["npt_ready"], 1)
            A(halves(S0b["zt"][:, 0]), ps2(Tile(G0_BASE, 0)), ACT.Copy).then_inc(proj_read[0], 1); act.wait_ge(proj_read[0], 1)
            split_hi(act, own, Tile(P_BASE, 1))
            act.wait_ge(S["g_abs"], 1)
            A(T1R, T1R, ACT.Exp, scale=-1.0).then_inc(S["g_exp"], 1); own.done("g_exp")
            act.wait_ge(S["g_1p"], 1)
            A(T1R, T1R, ACT.Ln).then_inc(S["g_ln"], 1); own.done("g_ln")
            act.wait_ge(S["g_pre"], 1)
            A(MR[:, 512:1024], MR[:, 512:1024], ACT.Exp, scale=-1.0)
            A(MR[:, 1024:1048], MR[:, 1024:1048], ACT.Exp).then_inc(S["g_mr"], 1); own.done("g_mr")
            with own.turns(4, ACT_POOL) as g:
                for j in range(4):
                    t = Tile(P_BASE, j, g, 4)
                    act.wait_ge(S["proj_done"], t.n + 1)
                    if j == 0:
                        act.wait_ge(S["ub_zero"], 1)
                    if j == 2:
                        act.wait_ge(S["pl_y"], 2 * g + 1)
                        act.wait_ge(S["g_rows"], 1)
                    if j < 2:
                        A(halves(S0b["ub"][:, j, 16:536]), ps2(t), ACT.Copy).then_inc(proj_read[t.p], 1); act.wait_ge(proj_read[t.p], t.m + 1)
                    else:
                        A(halves(S0b["zt"][:, j - 2]), ps2(t), ACT.Silu).then_inc(proj_read[t.p], 1); act.wait_ge(proj_read[t.p], t.m + 1)
                    split_hi(act, own, t.ahead(2))
                act.wait_ge(S["pl_ready"], g + 1)
                act.wait_ge(S["pl_T"], g + 1)
            act.wait_ge(S["g_bc"], 64)
            act.wait_ge(S["pl_y"], 8 + 1)
            gbc = S0["gbc"]
            with own.turns(4, ACT_HEAD) as h:
                for j in range(6):
                    t = Tile(M_BASE, j, h, 10)
                    act.wait_ge(S["proj_done"], t.n + 1)
                    A(halves(S0[("qT", "kT", "vT")[j // 2]][:, j % 2]), ps2(t), ACT.Copy,
                      scale=(HD ** -0.5 if j // 2 == 1 else 1.0)).then_inc(proj_read[t.p], 1); act.wait_ge(proj_read[t.p], t.m + 1)
                    split_hi(act, own, t.ahead(2))
                act.wait_ge(S["m_wsin"], h + 1)
                A(S0["ws"], S0["ws"], ACT.Exp).then_inc(S["m_ws"], 1); own.done("m_ws")
                act.wait_ge(S["m_rowT"], 3 * h + 2)
                A(S0["vr"].rearrange("p (a b) -> p a b", a=2), PS[:, 6:8, :], ACT.Copy).then_inc(S["m_vr"], 1); own.done("m_vr")
                for i in range(NT):
                    act.wait_ge(S["m_dt"], 4 * h + (i + 1))
                    A(S0["dt"][:, i % 2, 0:TP - i * P], S0["dt"][:, i % 2, 0:TP - i * P], ACT.Exp, scale=-1.0
                      ).then_inc(S["m_D"], 1); own.done("m_D")
                act.wait_ge(S["m_PV"], 4 * h + 4)
                A(S0["ad"], PS[:, 0, :], ACT.Abs).then_inc(S["m_abs"], 1); own.done("m_abs")
                act.wait_ge(S["m_stT"], h + 1)
                A(S0["kr"][:, 0:512], PS[:, 4, :], ACT.Copy).then_inc(S["m_st"], 1); own.done("m_st")
                A(S0["nst"], PS[0:1, 5, 0:HD], ACT.Copy).then_inc(S["m_nst"], 1); own.done("m_nst")
                act.wait_ge(S["m_dec"], h + 1)
                for b in range(NS):
                    A(S0["cb"][:, b], S0["cb"][:, b], ACT.Copy, scale=gbc[:, h, 1024 + b:1025 + b]).then_inc(S["c_sc"], 1); own.done("c_sc")
                act.wait_ge(S["m_decr"], h + 1)
                for j in range(2):
                    t = Tile(M_BASE, 6 + j, h, 10)
                    act.wait_ge(S["proj_done"], t.n + 1)
                    A(halves(S0["vT"][:, j]), ps2(t), ACT.Sigmoid).then_inc(proj_read[t.p], 1); act.wait_ge(proj_read[t.p], t.m + 1)
                    split_hi(act, own, t.ahead(2))
                for j in range(2):
                    act.wait_ge(S["m_oy"], 2 * h + j + 1)
                    A(S0["qT"][:, j], XY[:, 8 + 2 * h + j, :], ACT.Square).then_inc(S["m_sq"], 1); own.done("m_sq")
                t = Tile(M_BASE, 8, h, 10)
                act.wait_ge(S["proj_done"], t.n + 1)
                A(halves(S0["kT"][:, 0]), ps2(t), ACT.Silu).then_inc(proj_read[t.p], 1); act.wait_ge(proj_read[t.p], t.m + 1)
                split_hi(act, own, t.ahead(2))
                act.wait_ge(S["m_var"], h + 1)
                A(RS[:], RS[:], ACT.Sqrt).then_inc(S["m_sqrt"], 1); own.done("m_sqrt")
                t = Tile(M_BASE, 9, h, 10)
                act.wait_ge(S["proj_done"], t.n + 1)
                A(halves(S0["kT"][:, 1]), ps2(t), ACT.Silu).then_inc(proj_read[t.p], 1); act.wait_ge(proj_read[t.p], t.m + 1)
                split_hi(act, own, t.ahead(2))
                act.wait_ge(S["m_yz"], 2 * h + 2)
            act.wait_ge(S["m_yz"], 8)
            y_split_act(act, own, 0, O0_BASE)
            out_act(act, own, 0, O0_BASE)
            act.wait_ge(proj_read[0], (G1_BASE + 1) // 2)
            act.wait_ge(proj_read[1], G1_BASE // 2)
            norm_act(act, own, 1)
            h_act(act, own, 1)
            t = Tile(G1_BASE, 0)
            act.wait_ge(S["proj_done"], t.n + 1)
            act.wait_ge(S["consts"], 16 * 6)
            act.wait_ge(S["h_ready"], 3 * KT)
            A(halves(XR[0:48, 0]), ps2(t, slice(0, 48)), ACT.Sigmoid, bias=S1["bg"][0:48, 0:1]
              ).then_inc(proj_read[t.p], 1)
            act.wait_ge(proj_read[t.p], t.m + 1)
            split_hi(act, own, t.ahead(2))
            act.wait_ge(S["g1_T"], 1)
            act.wait_ge(S["g1_gw"], 1)

            kT, qr, qt, pr, pt, vr, rs = (S1[n] for n in ("kT", "qr", "qt", "pr", "pt", "vr", "rs"))
            with own.turns(4, ACT_GROUP) as g:
                def rows(x):
                    dst = vr[:, x // 4] if x in (3, 5) else rs[:, (0, 1, 2, None, 3)[x]]
                    act.wait_ge(S["a_rowT"], 6 * g + (x + 1))
                    A(dst, PS[:, 4, :], ACT.Copy).then_inc(S["a_row"], 1); own.done("a_row")

                def keys(b):
                    act.wait_ge(S["d_used"], 48 * g + (3 * b + 1))
                    A(pt[:, 0], PS[:, 5, :], ACT.Copy).then_inc(S["d_ka"], 1); own.done("d_ka")

                for j in range(10):
                    t = Tile(A_BASE, j, g, 14)
                    if 4 <= j < 8:
                        keys(2 * (j - 4))
                        keys(2 * (j - 4) + 1)
                    if j == 9:
                        dst = S1["dst"]
                        act.wait_ge(S["d_nm"], g + 1)
                        A(pr[0:64, 0], PS[0:64, 6, :], ACT.Exp, bias=dst[0:64, 1:2], scale=SCALE,
                          accum_out=dst[0:64, 2:3])
                        A(pr[64:96, 0, 0:NB], PS[64:96, 6, 0:NB], ACT.Exp, bias=dst[64:96, 1:2], scale=SCALE,
                          accum_out=dst[64:96, 2:3])
                        A(dst[0:64, 3:4], PS[0:64, 5, 0:1], ACT.Exp, bias=dst[0:64, 1:2], scale=SCALE
                          ).then_inc(S["d_exp"], 1); own.done("d_exp")
                    act.wait_ge(S["proj_done"], t.n + 1)
                    if j in (4, 5, 7, 9):
                        x = j - 4
                        if x >= 3:
                            act.wait_ge(S["a_src"], 6 * g + (x // 2))
                            act.wait_ge(S["a_rowT"], 6 * g + (x // 2))
                        A(halves(XR[:, (0, 1, None, 0, None, 1)[x]]), ps2(t), ACT.Copy).then_inc(proj_read[t.p], 1)
                        act.wait_ge(proj_read[t.p], t.m + 1)
                    else:
                        r = {0: 0, 1: 1, 2: 2, 3: 3, 6: 4, 8: 5}[j]
                        if r:
                            act.wait_ge(S["a_rot"], 6 * g + r)
                        if r < 4:
                            A(halves(qr[:, r]), ps2(t), ACT.Copy)
                        A(halves(RS[0:64]), ps2(t, slice(64, 128)), ACT.Copy)
                        A(halves(RS[64:128]), ps2(t, slice(0, 64)), ACT.Copy).then_inc(S["a_sw"], 1); own.done("a_sw")
                    split_hi(act, own, t.ahead(2))
                    if j >= 5:
                        rows(j - 5)
                rows(5)
                act.wait_ge(S["a_cin"], g + 1)
                A(S1["sc"], S1["sc"], ACT.Exp).then_inc(S["a_cexp"], 1); own.done("a_cexp")

                def expo(n):
                    act.wait_ge(S["at_nm"], 16 * g + (n + 1))
                    L = (n % 4 + 1) * P
                    for r in range(2):
                        ins = A(pr[:, 2 * (n % 2) + r, 0:L], PS[:, r, 0:L], ACT.Exp,
                                bias=S1["st"][:, 4 + n % 2, r:r + 1], scale=SCALE,
                                accum_out=S1["st"][:, n % 2, r:r + 1])
                    ins.then_inc(S["at_exp"], 1); own.done("at_exp")
                    act.wait_ge(S["at_w"], 16 * g + (n + 1))
                    for r in range(2):
                        ins = A(pr[:, 2 * (n % 2) + r, 0:L], pr[:, 2 * (n % 2) + r, 0:L], ACT.Copy,
                                scale=S1["st"][:, 6 + n % 2, r:r + 1])
                    ins.then_inc(S["at_sc"], 1); own.done("at_sc")
                act.wait_ge(S["d_pT"], g + 1)
                expo(0)
                for n in range(16):
                    L = (n % 4 + 1) * P
                    act.wait_ge(S["at_T"], 16 * g + (n + 1))
                    A(pt[:, 0, 0:L], PS[:, 4, 0:L], ACT.Copy).then_inc(S["at_pta"], 1); own.done("at_pta")
                    if n < 15:
                        expo(n + 1)
                    if n % 4 == 3:
                        t = Tile(A_BASE, 10 + n // 4, g, 14)
                        act.wait_ge(S["proj_done"], t.n + 1)
                        act.wait_ge(S["a_src"], 6 * g + 6)
                        if n >= 11:
                            act.wait_ge(S["a_yz"], 4 * g + (n // 4 - 1))
                        A(halves(XR[:, (n // 4) % 2]), PS[:, 2:4, 0:HALF], ACT.Silu).then_inc(proj_read[t.p], 1)
                        act.wait_ge(proj_read[t.p], t.m + 1)
                        split_hi(act, own, t.ahead(2))
                act.wait_ge(S["a_yz"], 4 * g + 4)
                act.wait_ge(S["a_ys"], g + 1)
                act.wait_ge(S["row_out"], 192 * g + 192)
                act.wait_ge(S["at_o"], 16 * g + 16)
            act.wait_ge(S["a_ys"], 4)
            act.wait_ge(S["a_yz"], 16)
            y_split_act(act, own, 1, O1_BASE)
            out_act(act, own, 1, O1_BASE)
            act.wait_ge(proj_read[0], N_TILES // 2)
            act.wait_ge(proj_read[1], N_TILES // 2)
            norm_act(act, own, 2)
            for f in range(0, 20, 2):
                i, kk = f // 4, f % 4
                act.wait_ge(S["fin_T"], f + 1)
                if f == 0:
                    act.wait_ge(S["proj_done"], N_TILES)
                q = slice(0, P if i < NT else NS)
                dst = YROW[:, i] if i < NT else YSROW
                A(dst[q, kk * 512:(kk + 1) * 512], PS[q, f % 4, :], ACT.Copy).then_inc(S["fin_act"], 1); own.done("fin_act")

        @block.vector
        def _(dve):
            V = nc.vector
            own = Own(dve, S, "dve_step")
            step = own.step
            dve.sem_inc(S["pl_y"], 1)
            own.done("pl_y")
            dve.sem_inc(S["sq_sum"], 2)
            own.done("sq_sum")
            own.done("sq_sum")
            TT, TS, STT, CP = V.tensor_tensor, V.tensor_scalar, V.scalar_tensor_tensor, V.tensor_copy

            def CPR(out, in_):
                return TS(out, in_, 1.0, None, ALU.mult)
            for f in range(1, 16, 2):
                dve.wait_ge(S["xt_made"], f + 1)
                CP(XY[:, 4 * (f % 4):4 * (f % 4) + 4, (f // 4) * P:(f // 4 + 1) * P],
                   PS[:, f % 4, :].rearrange("p (k t) -> p k t", k=4)).then_inc(S["xt_dve"], 1); own.done("xt_dve")
            dve.wait_ge(S["xt_made"], 17)
            CP(XY[:, :, TP:TA], PS[:, 4, 0:KT * NS].rearrange("p (k b) -> p k b", b=NS)).then_inc(S["xt_dve"], 1); own.done("xt_dve")
            dve.wait_ge(S["xt_made"], 19)
            step(CP(PR[:], PS[:, 5, 0:64]))
            CP(S0["nT"], PS[:, 6, 0:64].rearrange("p (k b) -> p k b", b=NS)).then_inc(S["npt_ready"], 1); own.done("npt_ready")
            dve.wait_ge(S["npt_ready"], 1)
            dve.wait_ge(S["xt_act"], 8)
            dve.wait_ge(S["xt_dve"], 9)
            split_lo(dve, own, Tile(G0_BASE, 0))
            split_lo(dve, own, Tile(P_BASE, 0))
            step(V.memset(S0b["ub"][:, :, 0:16], 0.0))
            V.memset(GONE, 1.0).then_inc(S["ub_zero"], 1); own.done("ub_zero")
            norm_dve(dve, own, 0)
            h_dve(dve, own, 0, R_G0)
            dve.wait_ge(S["g_sel"], 1)
            dve.wait_ge(S["ub_zero"], 1)
            bg = S0["bg"]
            TS(halves(IGR), ps_pair(4, slice(0, 4)), bg[0:4, 0:1], None, ALU.add)
            TS(halves(FGR), ps_pair(6, slice(0, 4)), bg[0:4, 1:2], None, ALU.add).then_inc(S["g_rows"], 1); own.done("g_rows")
            dve.wait_ge(S["g_rows"], 1)
            split_lo(dve, own, Tile(P_BASE, 1))
            step(TS(LFR, FGR, -1.0, None, ALU.mult))
            TT(T1R, FGR, LFR, ALU.max).then_inc(S["g_abs"], 1); own.done("g_abs")
            dve.wait_ge(S["g_exp"], 1)
            TS(T1R, T1R, 1.0, None, ALU.add).then_inc(S["g_1p"], 1); own.done("g_1p")
            dve.wait_ge(S["g_ln"], 1)
            step(STT(LFR, FGR, 0.0, T1R, ALU.min, ALU.subtract))
            step(V.tensor_tensor_scan(BR, GONE, LFR[:, 0:TP], 0.0, ALU.mult, ALU.add))
            step(TT(AR, IGR[:, 0:TP], BR, ALU.subtract))
            step(V.tensor_tensor_scan(MR[:, 0:TP], AR, AR, 0.0, ALU.max, ALU.max))
            step(TT(MR[:, TP:2 * TP], BR, MR[:, 0:TP], ALU.add))
            step(CP(GD[:, 32:33], MR[:, 2 * TP - 1:2 * TP]))
            step(TT(GD[:, 8:16], LFR[:, TP:TA], GM0, ALU.add))
            step(TT(GD[:, 0:8], GD[:, 8:16], IGR[:, TP:TA], ALU.max))
            TT(MR[:, 1024:1032], GD[:, 8:16], GD[:, 0:8], ALU.subtract)
            TT(MR[:, 1032:1040], IGR[:, TP:TA], GD[:, 0:8], ALU.subtract)
            TS(MR[:, 1040:1048], GD[:, 0:8], -1.0, None, ALU.mult).then_inc(S["g_pre"], 1); own.done("g_pre")
            dve.wait_ge(S["pl_ss"], 1)
            step(CP(S0b["ss"], PS[:, 5, 0:64].rearrange("p (k b) -> p k b", b=NS)))
            dve.wait_ge(S["x_saved"], 16)
            ub, sa, sb_, pl, zt, us = (S0b[n] for n in ("ub", "sa", "sb", "pl", "zt", "us"))
            for g in range(4):
                t0 = Tile(P_BASE, 4 * g)
                w = 2 ** (g + 1)
                split_lo(dve, own, Tile(P_BASE, 4 * g).ahead(2))
                split_lo(dve, own, Tile(P_BASE, 4 * g + 1).ahead(2))
                t1 = Tile(P_BASE, 4 * g + 1)
                dve.wait_ge(proj_read[t1.p], t1.m + 1)
                if g:
                    dve.wait_ge(S["pl_mm"], g)
                src, dst = ub, sa
                for lvl in range(g + 1):
                    lo, sh = 2 ** (lvl + 1) - 1, 2 ** lvl
                    step(TT(dst[:, :, lo:528], src[:, :, lo:528], src[:, :, lo - sh:528 - sh], ALU.add))
                    src, dst = dst, (sb_ if dst is sa else sa)
                step(STT(pl[:, :, 0:TP], src[:, :, 16:528], 1.0 / w, ub[:, :, 16:528], ALU.mult, ALU.subtract))
                ic = S0["c0"][:, C0_ICNT + g * 16:C0_ICNT + g * 16 + w]
                for j in range(2):
                    step(TT(dst[:, j, 0:w], src[:, j, 16:16 + w], ic, ALU.mult))
                step(TT(pl[:, :, 0:w], dst[:, :, 0:w], ub[:, :, 16:16 + w], ALU.subtract))
                split_lo(dve, own, Tile(P_BASE, 4 * g + 2).ahead(2))
                dve.wait_ge(S["pl_T"], g + 1)
                step(TT(us, S0b["ss"][:, 2 * g:2 * g + 2], ub[:, :, 528:536], ALU.add))
                step(CP(S0b["tail"][0:23, g * 256:(g + 1) * 256], PS[0:23, 4, 0:256]))
                STT(pl[:, :, TP:TA], us, 1.0 / w, ub[:, :, 528:536], ALU.mult, ALU.subtract
                    ).then_inc(S["pl_ready"], 1); own.done("pl_ready")
                split_lo(dve, own, Tile(P_BASE, 4 * g + 3).ahead(2))
                dve.wait_ge(S["pl_mm"], g + 1)
                t3 = Tile(P_BASE, 4 * g + 3)
                dve.wait_ge(proj_read[t3.p], t3.m + 1)
                for d in range(2):
                    STT(halves(XY[:, 2 * g + d]), ps_pair(4 + 2 * d), PR[:, R_PS + 2 * g + d:R_PS + 2 * g + d + 1],
                        halves(zt[:, d]), ALU.mult, ALU.mult).then_inc(S["pl_y"], 1); own.done("pl_y")
            dve.wait_ge(S["g_acolT"], 1)
            CP(S0["acol"].rearrange("p (h i) -> p i h", i=NT), PS[:, 4, 0:16].rearrange("p (i h) -> p i h", h=4)
               ).then_inc(S["g_acol"], 1); own.done("g_acol")
            dve.wait_ge(S["g_acol"], 1)
            dve.wait_ge(S["g_bc"], 64)

            qT, kT, vT, kr, pt, dt, gbc, acol = (S0[n] for n in ("qT", "kT", "vT", "kr", "pt", "dt", "gbc", "acol"))
            PD, DT, KDW, cb = S0["pr"], S0["dtmp"], S0["kdw"], S0["cb"]
            with own.turns(4, DVE_HEAD) as h:
                for j in range(6):
                    split_lo(dve, own, Tile(M_BASE, j, h, 10).ahead(2))
                t5 = Tile(M_BASE, 5, h, 10)
                dve.wait_ge(proj_read[t5.p], t5.m + 1)
                TS(S0["ws"], acol[:, bass.ds(4 * h, 4)], gbc[:, h, 511:512], None, ALU.subtract).then_inc(S["m_wsin"], 1); own.done("m_wsin")
                nTh = S0["nT"][:, bass.ds(2 * h, 2), :]
                TT(PD[:, :, 0:8], qT[:, :, TP:TA], kT[:, :, TP:TA], ALU.mult)
                TT(PD[:, :, 8:16], qT[:, :, TP:TA], nTh, ALU.mult).then_inc(S["m_prod"], 1); own.done("m_prod")

                def decay(i):
                    L = TP - i * P
                    TS(dt[:, i % 2, 0:L], gbc[:, h, i * P:TP], acol[:, bass.ds(4 * h + i, 1)], 0.0,
                       ALU.subtract, ALU.max).then_inc(S["m_dt"], 1); own.done("m_dt")
                decay(0)
                decay(1)
                dve.wait_ge(S["m_rowT"], 3 * h + 1)
                CP(kr.rearrange("p (a b) -> p a b", a=2), PS[:, 4:6, :]).then_inc(S["m_kr"], 1); own.done("m_kr")
                dve.wait_ge(S["m_rowT"], 3 * h + 3)
                CP(S0["vdr"][0:NS], PS[0:NS, 0, 0:HD]).then_inc(S["m_vd"], 1); own.done("m_vd")
                for i in range(NT):
                    L = TP - i * P
                    dve.wait_ge(S["m_D"], 4 * h + (i + 1))
                    dve.wait_ge(S["m_S"], 4 * h + (i + 1))
                    if i >= 2:
                        dve.wait_ge(S["m_PV"], 4 * h + (i - 1))
                    step(TT(pt[:, i % 2, 0:L], PS[:, 4 + i % 2, 0:L], dt[:, i % 2, 0:L], ALU.mult))
                    TT(pt[:, i % 2, 0:P], pt[:, i % 2, 0:P], S0["c0"][:, C0_MASKT:C0_MASKT + P], ALU.mult
                       ).then_inc(S["m_P"], 1); own.done("m_P")
                    if i < 2:
                        decay(i + 2)
                dve.wait_ge(S["m_ws"], h + 1)
                dve.wait_ge(S["m_kr"], h + 1)
                for i in range(NT):
                    ins = TS(kr[:, i * HD:(i + 1) * HD], kr[:, i * HD:(i + 1) * HD], S0["ws"][:, i:i + 1], None, ALU.mult)
                ins.then_inc(S["m_kw"], 1); own.done("m_kw")
                dve.wait_ge(S["m_dec"], h + 1)
                iw, dw, fl = (gbc[:, h, 1024 + 8 * x:1032 + 8 * x] for x in range(3))
                TT(DT[:, 0], PS[:, 1, 16:24], dw, ALU.mult)
                TT(DT[:, 1], PS[:, 1, 24:32], iw, ALU.mult)
                TT(DT[:, 4], PS[:, 1, 0:8], iw, ALU.mult)
                TT(DT[:, 5], PS[:, 1, 8:16], iw, ALU.mult)
                TT(KDW[:, 0], kT[:, 0, TP:TA], dw, ALU.mult)
                TT(KDW[:, 1], kT[:, 1, TP:TA], dw, ALU.mult)
                TT(nTh[:, 0], nTh[:, 0], iw, ALU.mult)
                step(TT(nTh[:, 1], nTh[:, 1], iw, ALU.mult))
                TT(DT[:, 1], DT[:, 1], DT[:, 0], ALU.add)
                TT(DT[:, 6], vT[:, 0, TP:TA], DT[:, 0], ALU.mult)
                TT(DT[:, 7], vT[:, 1, TP:TA], DT[:, 0], ALU.mult)
                step(TT(nTh, nTh, KDW, ALU.add))
                CPR(S0["nTh"], nTh).then_inc(S["m_nT"], 1); own.done("m_nT")
                TT(DT[:, 4:6], DT[:, 4:6], DT[:, 6:8], ALU.add)
                step(TS(DT[:, 2], DT[:, 1], -1.0, None, ALU.mult))
                step(TT(DT[:, 1], DT[:, 1], DT[:, 2], ALU.max))
                step(TT(DT[:, 1], DT[:, 1], fl, ALU.max))
                step(V.reciprocal(DT[:, 1], DT[:, 1]))
                TT(XY[:, bass.ds(8 + 2 * h, 1), TP:TA], DT[:, 4:5], DT[:, 1:2], ALU.mult)
                TT(XY[:, bass.ds(9 + 2 * h, 1), TP:TA], DT[:, 5:6], DT[:, 1:2], ALU.mult).then_inc(S["m_decr"], 1); own.done("m_decr")
                dve.wait_ge(S["m_abs"], h + 1)
                step(TT(S0["ad"], S0["ad"], gbc[:, h, TP:2 * TP], ALU.max))
                step(V.reciprocal(S0["ad"], S0["ad"]))
                for j in range(2):
                    ins = TT(XY[:, bass.ds(8 + 2 * h + j, 1), 0:TP], PS[:, 6 + j:7 + j, :],
                             S0["ad"].rearrange("p (o t) -> p o t", o=1), ALU.mult)
                ins.then_inc(S["m_y"], 1); own.done("m_y")
                dve.wait_ge(S["m_y"], h + 1)
                dve.wait_ge(S["m_decr"], h + 1)
                for j in range(2):
                    t = Tile(M_BASE, 6 + j, h, 10)
                    dve.wait_ge(proj_read[t.p], t.m + 1)
                    y = XY[:, bass.ds(8 + 2 * h + j, 1), :]
                    TT(y, y, vT[:, j:j + 1], ALU.mult).then_inc(S["m_oy"], 1); own.done("m_oy")
                    split_lo(dve, own, t.ahead(2))
                dve.wait_ge(S["m_nr"], h + 1)
                CP(S0["nor"], PS[0:NS, 5, 0:HD]).then_inc(S["m_nev"], 1); own.done("m_nev")
                dve.wait_ge(S["c_sc"], 8 * h + 8)
                for q, bank in enumerate((4, 6, 7, 5)):
                    dve.wait_ge(S["m_vb"], 4 * h + (q + 1))
                    for y in range(2):
                        b = 2 * q + y
                        for c in range(2):
                            STT(cb[:, b, c * HD:(c + 1) * HD], PS[:, bank, y * HD:(y + 1) * HD], KDW[:, c, b:b + 1],
                                cb[:, b, c * HD:(c + 1) * HD], ALU.mult, ALU.add).then_inc(S["m_cn"], 1); own.done("m_cn")
                split_lo(dve, own, Tile(M_BASE, 8, h, 10).ahead(2))
                dve.wait_ge(S["m_ssq"], h + 1)
                TS(halves(RS[:]), ps_pair(4), 1.0 / HD, EPS, ALU.mult, ALU.add).then_inc(S["m_var"], 1); own.done("m_var")
                dve.wait_ge(S["m_sqrt"], h + 1)
                step(V.reciprocal(RS[:], RS[:]))
                for j in range(2):
                    y = XY[:, bass.ds(8 + 2 * h + j, 1), :]
                    ins = STT(y, y, PR[:, bass.ds(R_MH + 2 * h + j, 1)], RS[:].rearrange("p (o t) -> p o t", o=1),
                              ALU.mult, ALU.mult)
                step(ins)
                split_lo(dve, own, Tile(M_BASE, 9, h, 10).ahead(2))
                t9 = Tile(M_BASE, 9, h, 10)
                dve.wait_ge(proj_read[t9.p], t9.m + 1)
                for j in range(2):
                    y = XY[:, bass.ds(8 + 2 * h + j, 1), :]
                    TT(y, y, kT[:, j:j + 1], ALU.mult).then_inc(S["m_yz"], 1); own.done("m_yz")
                dve.wait_ge(S["st_out"], 32 * h + 32)
                dve.wait_ge(S["n_out"], 16 * h + 16)

            dve.wait_ge(S["m_yz"], 8)
            y_split_dve(dve, own, 0)
            out_dve(dve, own, 0, O0_BASE)
            dve.wait_ge(proj_read[0], (G1_BASE + 1) // 2)
            dve.wait_ge(proj_read[1], G1_BASE // 2)
            norm_dve(dve, own, 1)
            h_dve(dve, own, 1, R_G1)
            dve.wait_ge(S["consts"], 16 * 6)
            dve.wait_ge(S["x_saved"], 32)
            dve.wait_ge(proj_read[1], (G1_BASE + 1) // 2)
            c1 = S1["c1"]
            TT(S1["gd"].rearrange("p (x b) -> p x b", b=NS),
               XR[0:48, 0, TP:TA].rearrange("p (o b) -> p o b", o=1).broadcast_to([48, 12, NS]),
               c1[0:48, C1_GM:C1_GM + 96].rearrange("p (x b) -> p x b", b=NS), ALU.mult).then_inc(S["g1_gd"], 1)
            own.done("g1_gd")
            split_lo(dve, own, Tile(G1_BASE, 0).ahead(2))
            dve.wait_ge(S["g1_T"], 1)
            CP(S1["gw"].rearrange("p c i -> p i c"), PS[:, 4, 0:192].rearrange("p (i c) -> p i c", i=NT))
            CP(S1["gdr"][0:96], PS[0:96, 5, 0:4]).then_inc(S["g1_gw"], 1); own.done("g1_gw")
            step(V.memset(S1["zq"], 0.0))

            kT, qr, qt, pr, pt, st, sc, cst, kd, zq, dst, pn, on = (
                S1[n] for n in ("kT", "qr", "qt", "pr", "pt", "st", "sc", "cst", "kd", "zq", "dst", "pn", "on"))
            with own.turns(4, DVE_GROUP) as g:
                def keys(b):
                    dve.wait_ge(S["d_used"], 48 * g + (3 * b + 2))
                    CP(pt[:, 1], PS[:, 7, :]).then_inc(S["d_kb"], 1); own.done("d_kb")
                    dve.wait_ge(S["d_used"], 48 * g + (3 * b + 3))
                    CP(S1["km"], PS[:, 4, 0:NB]).then_inc(S["d_km"], 1); own.done("d_km")

                def spread(ap):
                    return ap.rearrange("p (o b) -> p o b", o=1).broadcast_to([P, QPK, NS])

                for j in range(10):
                    t = Tile(A_BASE, j, g, 14)
                    x = j - 4
                    if 4 <= j < 8:
                        keys(2 * (j - 4))
                        keys(2 * (j - 4) + 1)
                    if j == 9:
                        dve.wait_ge(S["d_snew"], g + 1)
                        V.tensor_reduce(dst[64:96, 0:1], PS[64:96, 6, 0:NB], AX, ALU.max)
                        step(V.tensor_reduce(dst[0:64, 0:1], PS[0:64, 6, :], AX, ALU.max))
                        step(TT(dst[0:64, 0:1], dst[0:64, 0:1], PS[0:64, 5, 0:1], ALU.max))
                        TS(dst[0:96, 1:2], dst[0:96, 0:1], -SCALE, None, ALU.mult).then_inc(S["d_nm"], 1)
                        own.done("d_nm")
                        dve.wait_ge(S["d_exp"], g + 1)
                        step(TT(dst[0:64, 2:3], dst[0:64, 2:3], dst[0:64, 3:4], ALU.add))
                        step(V.reciprocal(dst[0:96, 4:5], dst[0:96, 2:3]))
                        step(TT(dst[0:96, 4:5], dst[0:96, 4:5], S1["gdr"][0:96, bass.ds(g, 1)], ALU.mult))
                        TS(pr[64:96, 0, 0:NB], pr[64:96, 0, 0:NB], dst[64:96, 4:5], None, ALU.mult)
                        step(TT(dst[0:64, 3:4], dst[0:64, 3:4], dst[0:64, 4:5], ALU.mult))
                        TS(S1["pnb"][0:64], ones[0:64], dst[0:64, 3:4], None, ALU.mult)
                        TS(pr[0:64, 0], pr[0:64, 0], dst[0:64, 4:5], None, ALU.mult).then_inc(S["d_pd"], 1)
                        own.done("d_pd")
                    if x in (0, 1, 3, 5):
                        dve.wait_ge(proj_read[t.p], t.m + 1)
                        if x < 2:
                            m = S1["kcb"] if x == 0 else S1["vcT"]
                            step(V.tensor_reduce(m, XR[:, x, 0:TP].rearrange("p (n t) -> p n t", t=32), AX, ALU.add))
                            step(TS(m, m, 1.0 / 32, None, ALU.mult))
                        CP(kd[:, x:x + 1], XR[:, (0, 1, None, 0, None, 1)[x]:(1, 2, None, 1, None, 2)[x], TP:TA]
                           ).then_inc(S["a_src"], 1); own.done("a_src")
                    else:
                        r = {0: 0, 1: 1, 2: 2, 3: 3, 6: 4, 8: 5}[j]
                        to = kT[:, r - 4] if r >= 4 else qt[:, r]
                        dve.wait_ge(S["a_sw"], 6 * g + (r + 1))
                        TT(halves(to), ps2(t), halves(cosT), ALU.mult).then_inc(proj_read[t.p], 1)
                        step(TT(RS[:], RS[:], sinT, ALU.mult))
                        dve.wait_ge(proj_read[t.p], t.m + 1)
                        TT(to, to, RS[:], ALU.add).then_inc(S["a_rot"], 1); own.done("a_rot")
                        if r >= 4:
                            CP(kd[:, x:x + 1], kT[:, r - 4:r - 3, TP:TA]).then_inc(S["a_src"], 1); own.done("a_src")
                        if r == 3:
                            for y, q in enumerate((qr, qt)):
                                ins = CP(zq[:, y].rearrange("p (b x) -> p b x", x=33)[:, :, 0:32:NS],
                                         q[:, :, TP:TA].rearrange("p j b -> p b j"))
                            ins.then_inc(S["d_z"], 1); own.done("d_z")
                        if r == 5:
                            for y in range(2):
                                ins = TT(pn[:, y].rearrange("p (j b) -> p j b", b=NS), qt[:, :, TP:TA],
                                         spread(kd[:, 2 + 2 * y]), ALU.mult)
                            ins.then_inc(S["d_prod"], 1); own.done("d_prod")
                    split_lo(dve, own, t.ahead(2))

                dve.wait_ge(S["d_pT"], g + 1)
                CP(S1["ptd"].rearrange("p a b -> p (a b)"), PS[:, 5, 0:256])
                CP(S1["vcr"], PS[0:NB, 5, 384:512])
                CP(S1["pc"], PS[0:NB, 5, 256:288]).then_inc(S["d_pc"], 1); own.done("d_pc")
                for y in range(2):
                    ins = TT(on[:, y].rearrange("p (j b) -> p j b", b=NS),
                             PS[:, 5, 320 + 32 * y:352 + 32 * y].rearrange("p (j b) -> p j b", b=NS),
                             spread(kd[:, 3 + 2 * y]), ALU.mult)
                step(ins)
                step(TT(on[:, 2], on[:, 0], on[:, 1], ALU.add))

                dve.wait_ge(S["a_cs"], g + 1)
                for jj in range(QPK):
                    ins = TT(sc[:, 4 * jj:4 * jj + 4], PS[:, 7, jj * 64:(jj + 1) * 64].rearrange("p (i n) -> p i n", n=NB),
                             c1[:, C1_CMP:C1_CMP + 64].rearrange("p (i n) -> p i n", n=NB), ALU.add)
                step(ins)
                step(V.tensor_reduce(cst[:, 0], sc, AX, ALU.max))
                step(TS(cst[:, 1], cst[:, 0], -SCALE, 1.0e20, ALU.mult, ALU.min))
                STT(sc, sc, SCALE, cst[:, 1].rearrange("p (n o) -> p n o", o=1).broadcast_to([P, 16, NB]),
                    ALU.mult, ALU.add).then_inc(S["a_cin"], 1); own.done("a_cin")

                def maxima(n):
                    i = n % 4
                    dve.wait_ge(S["at_s"], 16 * g + (n + 1))
                    for r in range(2):
                        blk = PS[:, r, i * P:(i + 1) * P]
                        ins = TT(blk, blk, c1[:, C1_NEG:C1_NEG + P], ALU.add)
                    step(ins)
                    step(V.tensor_reduce(st[:, 2 + n % 2], PS[:, 0:2, 0:(i + 1) * P], AX, ALU.max))
                    TS(st[:, 4 + n % 2], st[:, 2 + n % 2], -SCALE, None, ALU.mult).then_inc(S["at_nm"], 1)
                    own.done("at_nm")

                def weight(n):
                    jj, i = n // 4, n % 4
                    dve.wait_ge(S["at_exp"], 16 * g + (n + 1))
                    step(V.reciprocal(st[:, n % 2], st[:, n % 2]))
                    TT(st[:, 6 + n % 2:7 + n % 2].rearrange("p o r -> p r o"),
                       st[:, n % 2:n % 2 + 1].rearrange("p o r -> p r o"),
                       S1["gw"][:, bass.ds(12 * g + (3 * jj + 1), 2), i:i + 1], ALU.mult).then_inc(S["at_w"], 1)
                    own.done("at_w")

                maxima(0)
                dve.wait_ge(S["a_cexp"], g + 1)
                step(V.tensor_reduce(cst[:, 2], sc, AX, ALU.add))
                step(TS(cst[:, 2], cst[:, 2], 1e-30, None, ALU.max))
                step(V.reciprocal(cst[:, 2], cst[:, 2]))
                for jj in range(QPK):
                    ins = TT(cst[:, 3:4, 4 * jj:4 * jj + 4], cst[:, 2:3, 4 * jj:4 * jj + 4],
                             S1["gw"][:, bass.ds(12 * g + 3 * jj, 1), :], ALU.mult)
                step(ins)
                TT(sc, sc, cst[:, 3].rearrange("p (n o) -> p n o", o=1).broadcast_to([P, 16, NB]), ALU.mult
                   ).then_inc(S["a_cp"], 1); own.done("a_cp")
                weight(0)
                dve.wait_ge(S["d_eT"], g + 1)
                CP(S1["ptc2"].rearrange("p a b -> p (a b)"), PS[:, 4, 0:128]).then_inc(S["d_ptd"], 1)
                own.done("d_ptd")

                def cmp_rows(jj):
                    dve.wait_ge(S["a_ctT"], 4 * g + (jj + 1))
                    CP(S1["ptc"][:, jj % 2], PS[0:NB, 7, :]).then_inc(S["a_ptc"], 1); own.done("a_ptc")
                cmp_rows(0)
                for n in range(16):
                    jj, i = n // 4, n % 4
                    L = (i + 1) * P
                    dve.wait_ge(S["at_T"], 16 * g + (n + 1))
                    CP(pt[:, 1, 0:L], PS[:, 5, 0:L]).then_inc(S["at_ptb"], 1); own.done("at_ptb")
                    if n < 15:
                        maxima(n + 1)
                        weight(n + 1)
                    dve.wait_ge(S["at_o"], 16 * g + (n + 1))
                    CPR(XY[:, bass.ds(4 * g + jj, 1), i * P:(i + 1) * P], PS[:, 6:7, 0:P]).then_inc(S["at_oe"], 1)
                    own.done("at_oe")
                    if i == 2 and jj < 3:
                        cmp_rows(jj + 1)
                    if n in (12, 14):
                        a, b = (0, 4) if n == 12 else (4, 6)
                        dve.wait_ge(S["a_rdT"], 2 * g + (n - 10) // 2)
                        CP(S1["rd"][:, a:b], PS[0:NS, 7, 0:(b - a) * P].rearrange("p (a b) -> p a b", b=P)
                           ).then_inc(S["a_rd"], 1); own.done("a_rd")
                    if i == 3:
                        t = Tile(A_BASE, 10 + jj, g, 14)
                        dve.wait_ge(proj_read[t.p], t.m + 1)
                        y = XY[:, bass.ds(4 * g + jj, 1), 0:TP]
                        TT(y, y, XR[:, jj % 2:jj % 2 + 1, 0:TP], ALU.mult)
                        CP(S1["zs"][:, jj:jj + 1], XR[:, jj % 2:jj % 2 + 1, TP:TA]).then_inc(S["a_yz"], 1)
                        own.done("a_yz")
                        split_lo(dve, own, t.ahead(2))
                dve.wait_ge(S["d_used"], 48 * g + 48)
                step(TT(on[:, 2], on[:, 2], PS[:, 6, P:P + 32], ALU.add))
                TT(XY[:, bass.ds(4 * g, 4), TP:TA], on[:, 2].rearrange("p (j b) -> p j b", b=NS), S1["zs"], ALU.mult
                   ).then_inc(S["a_ys"], 1); own.done("a_ys")
                dve.wait_ge(S["row_out"], 192 * g + 192)
            y_split_dve(dve, own, 1)
            out_dve(dve, own, 1, O1_BASE)
            dve.wait_ge(proj_read[0], N_TILES // 2)
            dve.wait_ge(proj_read[1], N_TILES // 2)
            norm_dve(dve, own, 2)
            for k in range(KT):
                STT(XY[:, k], XY[:, k], PR[:, R_GF + k:R_GF + k + 1], RS[:], ALU.mult, ALU.mult).then_inc(S["fin_y"], 1); own.done("fin_y")
            for f in range(1, 20, 2):
                i, kk = f // 4, f % 4
                dve.wait_ge(S["fin_T"], f + 1)
                q = slice(0, P if i < NT else NS)
                d = YROW[:, i] if i < NT else YSROW
                CP(d[q, kk * 512:(kk + 1) * 512], PS[q, f % 4, :]).then_inc(S["fin_dve"], 1); own.done("fin_dve")


_INS = ["x_prompt", "x_sample", "state_pool", "state_mlstm_c", "state_mlstm_n", "state_mlstm_m", "cache_kv_cmp",
        "cache_kv_sel", "cache_kv_win", "page_table", "norm0_g", "w_in0", "b_gate0", "w_pool", "pool_scale",
        "mh_norm_g", "w_out0", "norm1_g", "w_in1", "b_gate1", "w_out1", "final_g"]
_OUTS = [("y_prompt", (1, TP, D)), ("y_sample", (NS, 1, D)), ("pool_p", (1, 15, 1024)), ("pool_s", (NS, 15, 1024)),
         ("c_p", (1, GH, HD, HD)), ("c_s", (NS, GH, HD, HD)), ("n_p", (1, GH, HD)), ("n_s", (NS, GH, HD)),
         ("m_p", (1, GH)), ("m_s", (NS, GH)),
         ("kvc_p", (1, TP, 2, NKV, DH)), ("kvc_s", (NS, 1, 2, NKV, DH)),
         ("kvs_p", (1, TP, 2, NKV, DH)), ("kvs_s", (NS, 1, 2, NKV, DH)),
         ("kvw_p", (1, 512, 2, NKV, DH)), ("kvw_s", (NS, 512, 2, NKV, DH))]


def kernel(**inputs):
    import numpy as _np
    import concourse.bacc as _bacc
    from concourse import mybir as _mybir
    from concourse.bass_utils import run_bass_kernel_spmd as _run

    nc = _bacc.Bacc("TRN2", target_bir_lowering=False, num_devices=1,
                     dynamic_dma_scratch_size=256)
    arrays, ins, outs = {}, {}, {}
    for name in _INS:
        arrays[f"in_{name}"] = _np.ascontiguousarray(inputs[name])
    for name, c in zip(("c_common", "c_layer0", "c_layer1", "c_expand"), constants()):
        arrays[f"in_{name}"] = c
    for name, a in arrays.items():
        ins[name[3:]] = nc.dram_tensor(name, a.shape, _mybir.dt.from_np(a.dtype), kind="ExternalInput").ap()
    for name, shape in _OUTS:
        outs[name] = nc.dram_tensor(f"out_{name}", shape, _mybir.dt.float32, kind="ExternalOutput").ap()
    trunk(nc, ins, outs)
    r = _run(nc, [arrays], core_ids=[0])
    return tuple(r.results[0][f"out_{name}"] for name, _ in _OUTS)
```
